# Optimizing a Trainium2 kernel written in Bass

```python
import jax, jax.numpy as jnp
from jax import lax
import numpy as np
import math

D_MODEL = 1024
BATCH = 1
SEQ = 256
DEPTH = 1

GRID_W = 64
CTX_LEN = 256
EPS = 1e-6

MLSTM_HEADS = 4
MLSTM_DH = 128
MLSTM_W = MLSTM_HEADS * MLSTM_DH
MLSTM_GATES = 2 * 2 * MLSTM_HEADS
MLSTM_CHUNK = 128

ATTN_Q_HEADS = 8
ATTN_KV_HEADS = 2
ATTN_GROUP = ATTN_Q_HEADS // ATTN_KV_HEADS
ATTN_DH = 64
ATTN_Q_W = ATTN_Q_HEADS * ATTN_DH
ATTN_KV_W = ATTN_KV_HEADS * ATTN_DH
WINDOW = 128
ATTN_BLOCK = 128
ROPE_BASE = 10000.0
ROPE_AXIS_FREQS = ATTN_DH // 4

N_BRANCH = 2
IN_SIZES = (MLSTM_W, MLSTM_W, MLSTM_W, MLSTM_W, MLSTM_GATES,
            ATTN_Q_W, ATTN_KV_W, ATTN_KV_W, N_BRANCH * D_MODEL)
D_IN = 4 * MLSTM_W + MLSTM_GATES + ATTN_Q_W + 2 * ATTN_KV_W + N_BRANCH * D_MODEL

PEER_HEADS = 8
PEER_N_KEYS = 128
PEER_N_EXPERTS = PEER_N_KEYS * PEER_N_KEYS
PEER_KEY_DIM = 256
PEER_HALF = PEER_KEY_DIM // 2
PEER_TOPK = 16
PEER_BLOCK = 128


def _rms(x, g):
    xf = x.astype(jnp.float32)
    y = xf * lax.rsqrt(jnp.mean(xf * xf, axis=-1, keepdims=True) + EPS)
    return y.astype(x.dtype) * g

def _modulate(x, g, shift, scale):
    return _rms(x, g) * (1 + scale) + shift

def _adaln(cond, w, b):
    mod = jax.nn.silu(cond) @ w + b
    return tuple(m[:, None, :] for m in jnp.split(mod, 6, axis=-1))

def _split_in(p):
    idx = []
    acc = 0
    for s in IN_SIZES[:-1]:
        acc += s
        idx.append(acc)
    return jnp.split(p, idx, axis=-1)

def _axial_rope(T):
    rows = T // GRID_W
    row = jnp.broadcast_to(jnp.arange(rows)[:, None], (rows, GRID_W)).reshape(T)
    col = jnp.broadcast_to(jnp.arange(GRID_W)[None, :], (rows, GRID_W)).reshape(T)
    inv = ROPE_BASE ** (-jnp.arange(ROPE_AXIS_FREQS, dtype=jnp.float32) / ROPE_AXIS_FREQS)
    ang = jnp.concatenate([row[:, None].astype(jnp.float32) * inv,
                           col[:, None].astype(jnp.float32) * inv], axis=-1)
    return jnp.cos(ang), jnp.sin(ang)

def _rope(t, cos, sin):
    t1, t2 = jnp.split(t, 2, axis=-1)
    c = cos[None, :, None, :]
    s = sin[None, :, None, :]
    return jnp.concatenate([t1 * c - t2 * s, t2 * c + t1 * s], axis=-1).astype(t.dtype)

def _chunk_seq(t, reverse):
    if reverse:
        t = jnp.flip(t, axis=1)
    B, T = t.shape[:2]
    t = jnp.moveaxis(t, 2, 1)
    return t.reshape((B, t.shape[1], T // MLSTM_CHUNK, MLSTM_CHUNK) + t.shape[3:])

def _unchunk(h, reverse):
    B, H = h.shape[:2]
    h = jnp.moveaxis(h.reshape(B, H, -1, h.shape[-1]), 1, 2)
    return jnp.flip(h, axis=1) if reverse else h

def _mlstm_summaries(k, v, li, lf):
    b = jnp.cumsum(lf, axis=-1)
    a = b[..., -1]
    w_log = a[..., None] - b + li
    m_loc = jnp.max(w_log, axis=-1)
    w = jnp.exp(w_log - m_loc[..., None])
    C_loc = jnp.einsum('bhcs,bhcsk,bhcsv->bhckv', w, k, v)
    n_loc = jnp.einsum('bhcs,bhcsk->bhck', w, k)
    return b, a, m_loc, C_loc, n_loc

def _mlstm_scan(a, m_loc, C_loc, n_loc, state0):
    def step(carry, inp):
        C, n, m = carry
        a_c, m_c, C_c, n_c = inp
        m_new = jnp.maximum(a_c + m, m_c)
        d_old = jnp.exp(a_c + m - m_new)
        d_new = jnp.exp(m_c - m_new)
        C_new = d_old[..., None, None] * C + d_new[..., None, None] * C_c
        n_new = d_old[..., None] * n + d_new[..., None] * n_c
        return (C_new, n_new, m_new), (C, n, m)
    xs = tuple(jnp.moveaxis(t, 2, 0) for t in (a, m_loc, C_loc, n_loc))
    final, starts = lax.scan(step, state0, xs)
    starts = tuple(jnp.moveaxis(t, 0, 2) for t in starts)
    return starts, final

def _mlstm_outputs(q, k, v, li, b, starts):
    C_s, n_s, m_s = starts
    L = q.shape[-2]
    log_inter = b + m_s[..., None]
    log_d = b[..., :, None] - b[..., None, :] + li[..., None, :]
    seen = jnp.tril(jnp.ones((L, L), dtype=bool))
    log_d = jnp.where(seen, log_d, -jnp.inf)
    m_t = jnp.maximum(log_inter, jnp.max(log_d, axis=-1))
    s = jnp.einsum('bhctk,bhcsk->bhcts', q, k) * jnp.exp(log_d - m_t[..., None])
    inter = jnp.exp(log_inter - m_t)
    num = (jnp.einsum('bhcts,bhcsv->bhctv', s, v)
           + inter[..., None] * jnp.einsum('bhctk,bhckv->bhctv', q, C_s))
    den = jnp.sum(s, axis=-1) + inter * jnp.einsum('bhctk,bhck->bhct', q, n_s)
    return num / jnp.maximum(jnp.abs(den), jnp.exp(-m_t))[..., None]

def _mlstm_direction(ctx_in, lat_in, reverse, with_ctx_out):
    qc, kc, vc, ic, fc = (_chunk_seq(t, reverse) for t in ctx_in)
    ql, kl, vl, il, fl = (_chunk_seq(t, reverse) for t in lat_in)
    B, H = qc.shape[:2]
    state0 = (jnp.zeros((B, H, MLSTM_DH, MLSTM_DH), jnp.float32),
              jnp.zeros((B, H, MLSTM_DH), jnp.float32),
              jnp.zeros((B, H), jnp.float32))
    bc, ac, mc, Cc, nc = _mlstm_summaries(kc, vc, ic, fc)
    starts_c, final_c = _mlstm_scan(ac, mc, Cc, nc, state0)
    bl, al, ml, Cl, nl = _mlstm_summaries(kl, vl, il, fl)
    starts_l, _ = _mlstm_scan(al, ml, Cl, nl, final_c)
    h_lat = _unchunk(_mlstm_outputs(ql, kl, vl, il, bl, starts_l), reverse)
    h_ctx = _unchunk(_mlstm_outputs(qc, kc, vc, ic, bc, starts_c), reverse) if with_ctx_out else None
    return h_lat, h_ctx

def _mlstm_branch(parts_lat, parts_ctx, b_mgates, norm_g, with_ctx_out):
    def prep(parts):
        q, k, v, o, gates = parts
        B, T = q.shape[:2]
        hd = lambda t: t.astype(jnp.float32).reshape(B, T, MLSTM_HEADS, MLSTM_DH)
        g = (gates.astype(jnp.float32) + b_mgates.astype(jnp.float32)).reshape(B, T, 2, 2, MLSTM_HEADS)
        return hd(q), hd(k) * (MLSTM_DH ** -0.5), hd(v), o, g

    ql, kl, vl, ol, gl = prep(parts_lat)
    qc, kc, vc, oc, gc = prep(parts_ctx)
    hs_lat, hs_ctx = [], []
    for d, reverse in enumerate((False, True)):
        lat_in = (ql, kl, vl, gl[:, :, d, 0], jax.nn.log_sigmoid(gl[:, :, d, 1]))
        ctx_in = (qc, kc, vc, gc[:, :, d, 0], jax.nn.log_sigmoid(gc[:, :, d, 1]))
        hl, hc = _mlstm_direction(ctx_in, lat_in, reverse, with_ctx_out)
        hs_lat.append(hl)
        hs_ctx.append(hc)

    def finish(h, o):
        B, T = h.shape[:2]
        hn = h * lax.rsqrt(jnp.mean(h * h, axis=-1, keepdims=True) + EPS)
        return hn.reshape(B, T, MLSTM_W).astype(o.dtype) * norm_g * jax.nn.sigmoid(o)

    m_lat = finish(hs_lat[0] + hs_lat[1], ol)
    m_ctx = finish(hs_ctx[0] + hs_ctx[1], oc) if with_ctx_out else None
    return m_lat, m_ctx

def _softmax_with_sink(logits, sink_b):
    sink_col = jnp.broadcast_to(sink_b, logits.shape[:-1] + (1,))
    return jax.nn.softmax(jnp.concatenate([logits, sink_col], axis=-1), axis=-1)[..., :-1]

def _window_attention(q, k, v, kc, vc, sink):
    B, T = q.shape[:2]
    nb = T // ATTN_BLOCK
    scale = ATTN_DH ** -0.5
    qb = q.reshape(B, nb, ATTN_BLOCK, ATTN_KV_HEADS, ATTN_GROUP, ATTN_DH)

    def band(t):
        tp = jnp.pad(t, ((0, 0), (ATTN_BLOCK, ATTN_BLOCK), (0, 0), (0, 0)))
        tp = tp.reshape(B, nb + 2, ATTN_BLOCK, ATTN_KV_HEADS, ATTN_DH)
        return jnp.concatenate([tp[:, :-2], tp[:, 1:-1], tp[:, 2:]], axis=2)

    kw, vw = band(k), band(v)
    qi = jnp.arange(ATTN_BLOCK)[:, None]
    kj = jnp.arange(3 * ATTN_BLOCK)[None, :]
    key_pos = jnp.arange(nb)[:, None, None] * ATTN_BLOCK - ATTN_BLOCK + kj[None]
    mask = (jnp.abs(kj - ATTN_BLOCK - qi) <= WINDOW)[None] & (key_pos >= 0) & (key_pos < T)
    s_loc = jnp.einsum('bnqhgd,bnkhd->bnhgqk', qb, kw).astype(jnp.float32) * scale
    s_loc = jnp.where(mask[None, :, None, None], s_loc, -jnp.inf)
    s_ctx = jnp.einsum('bnqhgd,bchd->bnhgqc', qb, kc).astype(jnp.float32) * scale
    sink_b = sink.astype(jnp.float32).reshape(ATTN_KV_HEADS, ATTN_GROUP, 1, 1)
    p = _softmax_with_sink(jnp.concatenate([s_loc, s_ctx], axis=-1), sink_b)
    p_loc = p[..., :3 * ATTN_BLOCK].astype(v.dtype)
    p_ctx = p[..., 3 * ATTN_BLOCK:].astype(v.dtype)
    out = (jnp.einsum('bnhgqk,bnkhd->bnqhgd', p_loc, vw)
           + jnp.einsum('bnhgqc,bchd->bnqhgd', p_ctx, vc))
    return out.reshape(B, T, ATTN_Q_W)

def _context_attention(qc, kc, vc, sink):
    B, Lc = qc.shape[:2]
    qg = qc.reshape(B, Lc, ATTN_KV_HEADS, ATTN_GROUP, ATTN_DH)
    s = jnp.einsum('bqhgd,bkhd->bhgqk', qg, kc).astype(jnp.float32) * (ATTN_DH ** -0.5)
    sink_b = sink.astype(jnp.float32).reshape(ATTN_KV_HEADS, ATTN_GROUP, 1, 1)
    p = _softmax_with_sink(s, sink_b).astype(vc.dtype)
    return jnp.einsum('bhgqk,bkhd->bqhgd', p, vc).reshape(B, Lc, ATTN_Q_W)

def _attn_branch(parts_lat, parts_ctx, q_g, k_g, sink, cos, sin, with_ctx_out):
    def heads(t, h):
        return t.reshape(t.shape[0], t.shape[1], h, ATTN_DH)
    ql, kl, vl = parts_lat
    qc, kc, vc = parts_ctx
    ql = _rope(_rms(heads(ql, ATTN_Q_HEADS), q_g), cos, sin)
    kl = _rope(_rms(heads(kl, ATTN_KV_HEADS), k_g), cos, sin)
    vl = heads(vl, ATTN_KV_HEADS)
    kc = _rms(heads(kc, ATTN_KV_HEADS), k_g)
    vc = heads(vc, ATTN_KV_HEADS)
    a_lat = _window_attention(ql, kl, vl, kc, vc, sink)
    a_ctx = None
    if with_ctx_out:
        a_ctx = _context_attention(_rms(heads(qc, ATTN_Q_HEADS), q_g), kc, vc, sink)
    return a_lat, a_ctx

def _token_mixer(h_lat, h_ctx, w_in, b_mgates, mlstm_norm_g, q_g, k_g, sink,
                 w_bm, w_ba, w_out, cos, sin, with_ctx_out):
    pl = _split_in(h_lat @ w_in)
    pc = _split_in(h_ctx @ w_in)
    m_lat, m_ctx = _mlstm_branch(pl[:5], pc[:5], b_mgates, mlstm_norm_g, with_ctx_out)
    a_lat, a_ctx = _attn_branch(pl[5:8], pc[5:8], q_g, k_g, sink, cos, sin, with_ctx_out)

    def merge(m, a, gates):
        g_m, g_a = jnp.split(gates, 2, axis=-1)
        return (jax.nn.sigmoid(g_m) * (m @ w_bm) + jax.nn.sigmoid(g_a) * (a @ w_ba)) @ w_out

    y_lat = merge(m_lat, a_lat, pl[8])
    y_ctx = merge(m_ctx, a_ctx, pc[8]) if with_ctx_out else None
    return y_lat, y_ctx

def _peer(h, w_query, sub_keys, expert_u, expert_v):
    B, T, D = h.shape
    tok = h.reshape(-1, PEER_BLOCK, D)

    def block(xb):
        q = (xb @ w_query).reshape(PEER_BLOCK, PEER_HEADS, 2, PEER_HALF)
        s = jnp.einsum('mhpd,hpnd->mhpn', q, sub_keys).astype(jnp.float32)
        s1, i1 = lax.top_k(s[:, :, 0], PEER_TOPK)
        s2, i2 = lax.top_k(s[:, :, 1], PEER_TOPK)
        cand = (s1[..., :, None] + s2[..., None, :]).reshape(PEER_BLOCK, PEER_HEADS, PEER_TOPK * PEER_TOPK)
        cidx = (i1[..., :, None] * PEER_N_KEYS + i2[..., None, :]).reshape(PEER_BLOCK, PEER_HEADS, PEER_TOPK * PEER_TOPK)
        top, pos = lax.top_k(cand, PEER_TOPK)
        idx = jnp.take_along_axis(cidx, pos, axis=-1)
        g = jax.nn.softmax(top, axis=-1)
        act = jax.nn.gelu(jnp.einsum('mhkd,md->mhk', expert_u[idx], xb).astype(jnp.float32))
        w = (g * act).astype(xb.dtype)
        return jnp.einsum('mhk,mhkd->md', w, expert_v[idx])

    return lax.map(block, tok).reshape(B, T, D)

def first_inputs(seed: int = 0) -> dict:
    key = jax.random.key(seed)
    ks = jax.random.split(key, 24)
    f32 = jnp.float32

    def nrm(k, shape, s):
        return jax.random.normal(k, shape, f32) * s

    gate_base = jnp.tile(jnp.concatenate([jnp.zeros((MLSTM_HEADS,), f32),
                                          jnp.linspace(3.0, 6.0, MLSTM_HEADS, dtype=f32)]), 2)
    return {
        'x': nrm(ks[0], (BATCH, SEQ, D_MODEL), 1.0),
        'c': nrm(ks[1], (BATCH, D_MODEL), 1.0),
        'ctx': nrm(ks[2], (BATCH, CTX_LEN, D_MODEL), 1.0),
        'c_ctx': nrm(ks[3], (D_MODEL,), 1.0),
        'w_ada': nrm(ks[4], (DEPTH, D_MODEL, 6 * D_MODEL), D_MODEL ** -0.5),
        'b_ada': nrm(ks[5], (DEPTH, 6 * D_MODEL), 0.02),
        'norm_mix_g': 1.0 + nrm(ks[6], (DEPTH, D_MODEL), 0.02),
        'norm_ffn_g': 1.0 + nrm(ks[7], (DEPTH, D_MODEL), 0.02),
        'w_in': nrm(ks[8], (DEPTH, D_MODEL, D_IN), D_MODEL ** -0.5),
        'b_mgates': gate_base + nrm(ks[9], (DEPTH, MLSTM_GATES), 0.1),
        'mlstm_norm_g': 1.0 + nrm(ks[10], (DEPTH, MLSTM_W), 0.02),
        'attn_q_norm_g': 1.0 + nrm(ks[11], (DEPTH, ATTN_DH), 0.02),
        'attn_k_norm_g': 1.0 + nrm(ks[12], (DEPTH, ATTN_DH), 0.02),
        'attn_sink': nrm(ks[13], (DEPTH, ATTN_Q_HEADS), 0.5),
        'w_branch_m': nrm(ks[14], (DEPTH, MLSTM_W, D_MODEL), MLSTM_W ** -0.5),
        'w_branch_a': nrm(ks[15], (DEPTH, ATTN_Q_W, D_MODEL), ATTN_Q_W ** -0.5),
        'w_out': nrm(ks[16], (DEPTH, D_MODEL, D_MODEL), D_MODEL ** -0.5),
        'peer_w_query': nrm(ks[17], (DEPTH, D_MODEL, PEER_HEADS * PEER_KEY_DIM), D_MODEL ** -0.5),
        'peer_sub_keys': nrm(ks[18], (DEPTH, PEER_HEADS, 2, PEER_N_KEYS, PEER_HALF), PEER_HALF ** -0.5),
        'peer_u': nrm(ks[19], (DEPTH, PEER_N_EXPERTS, D_MODEL), D_MODEL ** -0.5),
        'peer_v': nrm(ks[20], (DEPTH, PEER_N_EXPERTS, D_MODEL), 0.5),
    }

def first_block(x, c, ctx, c_ctx, w_ada, b_ada, norm_mix_g, norm_ffn_g, w_in, b_mgates,
              mlstm_norm_g, attn_q_norm_g, attn_k_norm_g, attn_sink, w_branch_m, w_branch_a,
              w_out, peer_w_query, peer_sub_keys, peer_u, peer_v):
    T = x.shape[1]
    cos, sin = _axial_rope(T)
    for layer in range(DEPTH):
        update_ctx = layer + 1 < DEPTH
        sh1, sc1, g1, sh2, sc2, g2 = _adaln(c, w_ada[layer], b_ada[layer])
        csh1, csc1, cg1, csh2, csc2, cg2 = _adaln(c_ctx[None], w_ada[layer], b_ada[layer])
        h_lat = _modulate(x, norm_mix_g[layer], sh1, sc1)
        h_ctx = _modulate(ctx, norm_mix_g[layer], csh1, csc1)
        y_lat, y_ctx = _token_mixer(h_lat, h_ctx, w_in[layer], b_mgates[layer], mlstm_norm_g[layer],
                                    attn_q_norm_g[layer], attn_k_norm_g[layer], attn_sink[layer],
                                    w_branch_m[layer], w_branch_a[layer], w_out[layer],
                                    cos, sin, update_ctx)
        x = x + g1 * y_lat
        x = x + g2 * _peer(_modulate(x, norm_ffn_g[layer], sh2, sc2), peer_w_query[layer],
                           peer_sub_keys[layer], peer_u[layer], peer_v[layer])
        if update_ctx:
            ctx = ctx + cg1 * y_ctx
            ctx = ctx + cg2 * _peer(_modulate(ctx, norm_ffn_g[layer], csh2, csc2), peer_w_query[layer],
                                    peer_sub_keys[layer], peer_u[layer], peer_v[layer])
    return x


D_MIX = D_MODEL
D_FOURIER = D_MIX // 4
FOURIER_GROUPS = 4
D_FG = D_FOURIER // FOURIER_GROUPS
HEAD_DIM = 64
NA_HEADS = (D_MIX // 2) // HEAD_DIM
D_NA = NA_HEADS * HEAD_DIM
D_CONV = D_MIX - D_FOURIER - D_NA
CONV_WIDTH = 3
D_IN_PROJ = D_FOURIER + 3 * D_NA + 3 * D_CONV

NA_KH = 8
NA_KW = 16
NA_QB = 16
NA_KB = 32

N_GROUPS = 4
EXPERTS_PER_GROUP = 8
N_EXPERTS = N_GROUPS * EXPERTS_PER_GROUP
TOP_K = 2
D_EXPERT = 512

NEG_INF = -1e30


def rms_norm(x, gain):
    xf = x.astype(jnp.float32)
    y = xf * lax.rsqrt(jnp.mean(xf * xf, axis=-1, keepdims=True) + EPS)
    return (y * gain.astype(jnp.float32)).astype(x.dtype)

def split_in(u):
    o = [D_FOURIER, D_FOURIER + D_NA, D_FOURIER + 2 * D_NA, D_FOURIER + 3 * D_NA,
         D_FOURIER + 3 * D_NA + D_CONV, D_FOURIER + 3 * D_NA + 2 * D_CONV]
    f, q, k, v, gb, gc, h = jnp.split(u, o, axis=-1)
    heads = lambda t: t.reshape(*t.shape[:-1], NA_HEADS, HEAD_DIM)
    return f, heads(q), heads(k), heads(v), gb, gc, h

def fourier_mix(f):
    b, n, _ = f.shape
    fg = f.reshape(b, n, FOURIER_GROUPS, D_FG).astype(jnp.float32)
    out = jnp.fft.fft2(fg, axes=(1, 3), norm="ortho").real
    return out.reshape(b, n, D_FOURIER).astype(f.dtype)

def short_conv(h, w):
    return lax.conv_general_dilated(
        h, w[:, None, :].astype(h.dtype), window_strides=(1,), padding=((1, 1),),
        dimension_numbers=("NWC", "WIO", "NWC"), feature_group_count=h.shape[-1])

def na_latent(q, k, v, kc, vc, rpb):
    b, n, h, dh = q.shape
    rows = n // GRID_W
    kh = min(NA_KH, rows)
    ncb = GRID_W // NA_QB
    r = jnp.arange(rows)
    row_start = jnp.clip(r - kh // 2, 0, rows - kh)
    row_idx = row_start[:, None] + jnp.arange(kh)[None, :]
    cols = jnp.arange(GRID_W)
    col_start = jnp.clip(cols - NA_KW // 2, 0, GRID_W - NA_KW)
    band_start = jnp.clip(col_start[::NA_QB], 0, GRID_W - NA_KB)
    band_idx = band_start[:, None] + jnp.arange(NA_KB)[None, :]
    qcol = cols.reshape(ncb, NA_QB)
    qcs = col_start.reshape(ncb, NA_QB)
    kcol = band_idx[:, None, :]
    valid = (kcol >= qcs[..., None]) & (kcol < qcs[..., None] + NA_KW)
    roff = row_idx - r[:, None] + (NA_KH - 1)
    coff = jnp.clip(kcol - qcol[..., None] + (NA_KW - 1), 0, 2 * NA_KW - 2)
    bias = rpb[:, roff[:, None, None, :, None], coff[None, :, :, None, :]]

    qg = q.reshape(b, rows, ncb, NA_QB, h, dh)
    kg = k.reshape(b, rows, GRID_W, h, dh)
    vg = v.reshape(b, rows, GRID_W, h, dh)
    ri = row_idx[:, :, None, None]
    ci = band_idx[None, None]
    kb = kg[:, ri, ci]
    vb = vg[:, ri, ci]

    s_loc = jnp.einsum("brcqhd,brkcjhd->bhrcqkj", qg, kb).astype(jnp.float32)
    s_loc = jnp.where(valid[:, :, None, :], s_loc + bias.astype(jnp.float32), NEG_INF)
    s_ctx = jnp.einsum("brcqhd,blhd->bhrcql", qg, kc).astype(jnp.float32)
    kj = kh * NA_KB
    s = jnp.concatenate([s_loc.reshape(*s_loc.shape[:5], kj), s_ctx], axis=-1)
    p = jax.nn.softmax(s, axis=-1).astype(v.dtype)
    p_loc = p[..., :kj].reshape(s_loc.shape)
    p_ctx = p[..., kj:]
    o = (jnp.einsum("bhrcqkj,brkcjhd->brcqhd", p_loc, vb)
         + jnp.einsum("bhrcql,blhd->brcqhd", p_ctx, vc))
    return o.reshape(b, n, h * dh)

def na_context(qc, kc, vc):
    s = jnp.einsum("blhd,bmhd->bhlm", qc, kc).astype(jnp.float32)
    p = jax.nn.softmax(s, axis=-1).astype(vc.dtype)
    o = jnp.einsum("bhlm,bmhd->blhd", p, vc)
    return o.reshape(*o.shape[:2], D_NA)

def mix_out(f, attn, conv, w_fourier, w_out):
    return jnp.concatenate([fourier_mix(f) @ w_fourier, attn, conv], axis=-1) @ w_out

def hier_moe(t, w_rg, b_rg, w_re, b_re, w_gate, w_up, w_down):
    n_tok = t.shape[0]
    g_logits = (t @ w_rg + b_rg).astype(jnp.float32)
    g_prob = jax.nn.softmax(g_logits, axis=-1)
    g_idx = jnp.argmax(g_logits, axis=-1)
    g_w = jnp.take_along_axis(g_prob, g_idx[:, None], axis=-1)
    e_logits = (t @ w_re + b_re).astype(jnp.float32).reshape(n_tok, N_GROUPS, EXPERTS_PER_GROUP)
    e_sel = jnp.take_along_axis(e_logits, g_idx[:, None, None], axis=1)[:, 0]
    top_v, top_i = lax.top_k(e_sel, TOP_K)
    pair_w = g_w * jax.nn.softmax(top_v, axis=-1)
    expert_id = g_idx[:, None] * EXPERTS_PER_GROUP + top_i
    combine = jnp.sum(jax.nn.one_hot(expert_id, N_EXPERTS, dtype=jnp.float32)
                      * pair_w[..., None], axis=1).astype(t.dtype)
    y = jnp.zeros_like(t)
    for e in range(N_EXPERTS):
        he = jax.nn.silu(t @ w_gate[e]) * (t @ w_up[e])
        y = y + combine[:, e:e + 1] * (he @ w_down[e])
    return y

def trunk_layer(x, xc, mod_x, mod_c, norm1, norm2, w_in, w_fourier, w_conv, rpb, w_out,
                w_rg, b_rg, w_re, b_re, w_gate, w_up, w_down, last):
    b, n, d = x.shape
    l = xc.shape[1]
    sh1, sc1, g1, sh2, sc2, g2 = jnp.split(mod_x[:, None, :], 6, axis=-1)
    csh1, csc1, cg1, csh2, csc2, cg2 = jnp.split(mod_c, 6, axis=-1)
    scale = 1.0 / math.sqrt(HEAD_DIM)

    ux = (rms_norm(x, norm1) * (1 + sc1) + sh1) @ w_in
    uc = (rms_norm(xc, norm1) * (1 + csc1) + csh1) @ w_in
    fx, qx, kx, vx, bx, cx, hx = split_in(ux)
    fc, qc, kc, vc, bc, cc, hc = split_in(uc)
    attn_x = na_latent(qx * scale, kx, vx, kc, vc, rpb)
    conv_x = bx * short_conv(cx * hx, w_conv)
    x = x + g1 * mix_out(fx, attn_x, conv_x, w_fourier, w_out)
    if not last:
        attn_c = na_context(qc * scale, kc, vc)
        conv_c = bc * short_conv(cc * hc, w_conv)
        xc = xc + cg1 * mix_out(fc, attn_c, conv_c, w_fourier, w_out)

    hx2 = rms_norm(x, norm2) * (1 + sc2) + sh2
    if last:
        y = hier_moe(hx2.reshape(-1, d), w_rg, b_rg, w_re, b_re, w_gate, w_up, w_down)
        x = x + g2 * y.reshape(b, n, d)
    else:
        hc2 = rms_norm(xc, norm2) * (1 + csc2) + csh2
        tok = jnp.concatenate([hx2.reshape(-1, d), hc2.reshape(-1, d)], axis=0)
        y = hier_moe(tok, w_rg, b_rg, w_re, b_re, w_gate, w_up, w_down)
        x = x + g2 * y[:b * n].reshape(b, n, d)
        xc = xc + cg2 * y[b * n:].reshape(b, l, d)
    return x, xc

def second_inputs(seed: int = 0) -> dict:
    key = jax.random.key(seed)
    ks = jax.random.split(key, 24)
    d = D_MODEL
    nrm = lambda k, shape, s: jax.random.normal(k, shape, jnp.float32) * s
    return {
        "x": nrm(ks[0], (BATCH, SEQ, d), 1.0),
        "c": nrm(ks[1], (BATCH, d), 1.0),
        "ctx": nrm(ks[2], (BATCH, CTX_LEN, d), 1.0),
        "c_ctx": nrm(ks[3], (d,), 1.0),
        "w_ada": nrm(ks[4], (DEPTH, d, 6 * d), 0.5 * d ** -0.5),
        "b_ada": nrm(ks[5], (DEPTH, 6 * d), 0.02),
        "norm1": 1.0 + nrm(ks[6], (DEPTH, d), 0.05),
        "norm2": 1.0 + nrm(ks[7], (DEPTH, d), 0.05),
        "w_in": nrm(ks[8], (DEPTH, d, D_IN_PROJ), d ** -0.5),
        "w_fourier": nrm(ks[9], (DEPTH, D_FOURIER, D_FOURIER), D_FOURIER ** -0.5),
        "w_conv": nrm(ks[10], (DEPTH, CONV_WIDTH, D_CONV), CONV_WIDTH ** -0.5),
        "rpb": nrm(ks[11], (DEPTH, NA_HEADS, 2 * NA_KH - 1, 2 * NA_KW - 1), 0.1),
        "w_out": nrm(ks[12], (DEPTH, D_MIX, d), D_MIX ** -0.5),
        "w_rg": nrm(ks[13], (DEPTH, d, N_GROUPS), d ** -0.5),
        "b_rg": nrm(ks[14], (DEPTH, N_GROUPS), 0.01),
        "w_re": nrm(ks[15], (DEPTH, d, N_EXPERTS), d ** -0.5),
        "b_re": nrm(ks[16], (DEPTH, N_EXPERTS), 0.01),
        "w_gate": nrm(ks[17], (DEPTH, N_EXPERTS, d, D_EXPERT), d ** -0.5),
        "w_up": nrm(ks[18], (DEPTH, N_EXPERTS, d, D_EXPERT), d ** -0.5),
        "w_down": nrm(ks[19], (DEPTH, N_EXPERTS, D_EXPERT, d), D_EXPERT ** -0.5),
        "norm_final": 1.0 + nrm(ks[20], (d,), 0.05),
    }

def second_block(x, c, ctx, c_ctx, w_ada, b_ada, norm1, norm2, w_in, w_fourier, w_conv, rpb,
              w_out, w_rg, b_rg, w_re, b_re, w_gate, w_up, w_down, norm_final):
    xc = ctx
    sc = jax.nn.silu(c)
    scc = jax.nn.silu(c_ctx)
    for li in range(DEPTH):
        mod_x = sc @ w_ada[li] + b_ada[li]
        mod_c = scc @ w_ada[li] + b_ada[li]
        x, xc = trunk_layer(x, xc, mod_x, mod_c, norm1[li], norm2[li], w_in[li], w_fourier[li],
                            w_conv[li], rpb[li], w_out[li], w_rg[li], b_rg[li], w_re[li],
                            b_re[li], w_gate[li], w_up[li], w_down[li], li == DEPTH - 1)
    return rms_norm(x, norm_final)


def setup_inputs(seed=0):
    out = dict(first_inputs(seed))
    for name, value in second_inputs(seed + 1).items():
        if name != "x":
            out[name + "_2"] = value
    return out


def reference(
    x, c, ctx, c_ctx, w_ada, b_ada, norm_mix_g, norm_ffn_g, w_in, b_mgates, mlstm_norm_g,
    attn_q_norm_g, attn_k_norm_g, attn_sink, w_branch_m, w_branch_a, w_out, peer_w_query,
    peer_sub_keys, peer_u, peer_v, c_2, ctx_2, c_ctx_2, w_ada_2, b_ada_2, norm1_2, norm2_2,
    w_in_2, w_fourier_2, w_conv_2, rpb_2, w_out_2, w_rg_2, b_rg_2, w_re_2, b_re_2, w_gate_2,
    w_up_2, w_down_2, norm_final_2,
):
    x = first_block(
        x, c, ctx, c_ctx, w_ada, b_ada, norm_mix_g, norm_ffn_g, w_in, b_mgates, mlstm_norm_g,
        attn_q_norm_g, attn_k_norm_g, attn_sink, w_branch_m, w_branch_a, w_out, peer_w_query,
        peer_sub_keys, peer_u, peer_v,
    )
    return second_block(
        x, c_2, ctx_2, c_ctx_2, w_ada_2, b_ada_2, norm1_2, norm2_2, w_in_2, w_fourier_2,
        w_conv_2, rpb_2, w_out_2, w_rg_2, b_rg_2, w_re_2, b_re_2, w_gate_2, w_up_2, w_down_2,
        norm_final_2,
    )


_drawn_inputs = setup_inputs


def setup_inputs(seed=0):
    import zlib

    import numpy as np

    out = dict(_drawn_inputs(seed))
    spreads = {}
    factors = {'mlstm_norm_g': 3.467,
     'attn_q_norm_g': 8.0,
     'attn_k_norm_g': 8.0,
     'attn_sink': 8.0,
     'norm1_2': 3.029,
     'norm2_2': 3.413,
     'rpb_2': 8.0,
     'b_rg_2': 64.0,
     'b_re_2': 8.0}
    for name, (base, spread) in spreads.items():
        noise = np.random.default_rng([zlib.crc32(name.encode()), seed]).standard_normal(out[name].shape)
        drawn = base * np.exp(spread * noise) if base else spread * noise
        out[name] = __import__('jax').numpy.asarray(drawn.astype(out[name].dtype))
    for name, factor in factors.items():
        out[name] = (out[name] * factor).astype(out[name].dtype)
    return out
```

```python
from contextlib import ExitStack

import numpy as np

import concourse.bass as bass
from concourse import mybir

F32 = mybir.dt.float32
U32 = mybir.dt.uint32
ALU = mybir.AluOpType
ACT = mybir.ActivationFunctionType
X = mybir.AxisListType.X

P = 128
D = 1024
KD = D // P
T = 256
NT = T // P
EPS = 1e-6
NEG = -1e30
BIG_NEG = -3.0e38
SLAB = 4096
SLOTS = 4

HEADS = 4
KEY_SCALE = float(P) ** -0.5
AH = 8
DH = 64
ATT_SCALE = float(DH) ** -0.5
UNITS = NT * AH

RH = 8
TOPK = 16
NKEY = 128
HALF_E1 = NKEY // 2
GROUP = 8

NG = 4
EPG = 8
NE = NG * EPG
DE = 512

ADA_SLABS = 6 * D // 512
S_ADA = 0
S_K, S_V, S_GKV, S_Q, S_AQ, S_O, S_MG = (2 * ADA_SLABS + i for i in range(7))
S_BM = S_MG + 4
S_BA = S_BM + 1
S_OUT = S_BA + 1
S_QUERY = S_OUT + 2
S_PEER = S_QUERY + 4
HALF_SLABS = HALF_E1 // 4
S_K2 = S_PEER + 4 * HALF_SLABS
S_V2, S_Q2, S_FH2, S_G2 = (S_K2 + i for i in range(1, 5))
S_OUT2 = S_G2 + 1
S_MOE = S_OUT2 + 2
N_SLABS = S_MOE + 3 * NE

CONSTS = {}
_n = 0
for _name, _w in (("ident", P), ("ones", P), ("tri0", P), ("tri1", P), ("seen0", P), ("seen1", P),
                  ("window", NT * T), ("near", DH), ("cos", NT * 32), ("sin", NT * 32), ("iota", P),
                  ("dft_c", NT * T), ("dft_s", NT * T), ("dch_c", P), ("dch_s", P)):
    CONSTS[_name] = (_n, _w)
    _n += _w
N_CONST = _n

COLS = {}
_n = 0
for _name, _w in (("b_ada", 2 * 6 * KD), ("g_mix", KD), ("g_ffn", KD), ("g1", KD), ("g2", KD),
                  ("g_final", KD), ("w_conv", 6)):
    COLS[_name] = (_n, _w)
    _n += _w
N_COL = _n
ROWS = {}
_n = 0
for _name, _w in (("b_gates", 16), ("g_mlstm", 512), ("g_q", DH), ("g_k", DH), ("sink", AH),
                  ("b_router", NG + NE)):
    ROWS[_name] = (_n, _w)
    _n += _w
N_ROW = _n


def two_block_kernel(nc, w_stream, cond, x_t, ctx_t, ctx2_t, consts, cols, rows, sub_keys, rpb,
                     w_four, w_router, out):
    with ExitStack() as ctx:
        def sb(name, n, dt=F32):
            return ctx.enter_context(nc.sbuf_tensor(name, [P, n], dt))

        def sem(name):
            return ctx.enter_context(nc.semaphore(name))

        slab = [sb(f"slab{i}", SLAB) for i in range(SLOTS)]
        big = sb("big", 20080)
        scratch = sb("scratch", 4096)
        xT = sb("xT", KD * T)
        hT = sb("hT", KD * T)
        hcT = sb("hcT", KD * T)
        cst = sb("cst", N_CONST)
        col = sb("col", N_COL)
        row = sb("row", N_ROW)
        condr = sb("condr", KD * 4)
        conds = sb("conds", KD * 4)
        mod = sb("mod", 2 * 6 * KD * 2)
        gain = sb("gain", KD)
        rstd = sb("rstd", T)
        stat = sb("stat", 4 * 2 * UNITS)
        small = sb("small", 640)
        pick = sb("pick", 3 * T)
        ps = ctx.enter_context(nc.psum_tensor("ps", [P, 8 * 512], F32))

        def bank(b, n=512, at=0):
            return ps[:, b * 512 + at:b * 512 + at + n]

        def const(name):
            o, w = CONSTS[name]
            return cst[:, o:o + w]

        def colv(name):
            o, w = COLS[name]
            return col[:, o:o + w]

        def rowv(name):
            o, w = ROWS[name]
            return row[:, o:o + w]

        def at(t, o, n):
            return t[:, o:o + n]

        ident, ones, iota = const("ident"), const("ones"), const("iota")

        def modc(block, part, j, who=0):
            c = ((block * 6 + part) * KD + j) * 2 + who
            return mod[:, c:c + 1]

        def modp(block, part, who=0):
            c = (block * 6 + part) * KD * 2 + who
            return mod[:, c:c + 2 * KD - 1:2]

        qT = at(big, 0, 1024)
        kN = at(big, 1024, 2048)
        kTl = at(big, 3072, 1024)
        vA = at(big, 4096, 4 * HEADS * 129).rearrange("p (c h v) -> p c h v", c=4, h=HEADS)
        sigO = at(big, 6160, 1024)
        gat = at(big, 7184, 64)
        aqN = at(big, 7248, 1024)
        akN = at(big, 8272, 512)
        avN = at(big, 8784, 512)
        qR = at(big, 9296, 1024)
        kR = at(big, 10320, 512)
        kSw = at(big, 10832, 512)
        qTa = at(big, 11344, 1024)
        kTa = at(big, 12368, 1024)
        hN = at(big, 13392, 1024)
        pair = [at(big, 14416, 512), at(big, 14928, 512)]
        state = [[at(big, 15440 + (2 * v + d) * 516, 516).rearrange("p (h v) -> p h v", h=HEADS)
                  for d in range(2)] for v in range(2)]
        t1 = at(big, 17504, 516).rearrange("p (h v) -> p h v", h=HEADS)
        t2 = at(big, 18020, 516).rearrange("p (h v) -> p h v", h=HEADS)
        probsT = [at(big, 19052, 512), at(big, 19564, 512)]
        decay = hcT
        logit = [at(hT, 0, 512), at(hT, 512, 512)]
        probs = [at(hT, 1024, 512), at(hT, 1536, 512)]
        aN = at(big, 0, 1024)
        mT = at(big, 1024, 1024)
        aT = at(big, 2048, 1024)
        merged = at(big, 3072, 2048)
        tmpm = [at(big, 5120, 512), at(big, 5632, 512)]
        sigG = scratch
        qTr = at(big, 0, 4096)
        subk = at(big, 4096, 2048)
        sc = [at(big, 6144, 2048), at(big, 16384, 2048)]
        cand = at(big, 8192, 2048)
        tmpr = at(big, 10240, 2048)
        R0 = 14336
        top1 = at(big, R0, 256)
        idx1 = at(big, R0 + 256, 256).bitcast(U32)
        idx1f = at(big, R0 + 512, 256)
        top2 = at(big, R0 + 768, 128)
        pos = at(big, R0 + 896, 128).bitcast(U32)
        posa = at(big, R0 + 1024, 128).bitcast(U32)
        posb = at(big, R0 + 1152, 128).bitcast(U32)
        posaf = at(big, R0 + 1280, 128)
        posbf = at(big, R0 + 1408, 128)
        choice = [at(big, R0 + 1536 + 128 * i, 128) for i in range(3)]
        zsum = at(big, R0 + 1920, 16)
        gate = at(big, 0, HALF_E1 * T)
        oh2 = [at(scratch, 0, 1024), at(scratch, 1024, 1024)]
        oh1 = [at(scratch, 2048, 512), at(scratch, 2560, 512)]
        gel = [at(scratch, 3072, 512), at(scratch, 3584, 512)]
        kT2 = at(big, 0, 2048)
        vN2 = at(big, 2048, 2048)
        qT2 = at(big, 4096, 1024)
        fN = at(big, 5120, 512)
        hcv = at(big, 5632, 512)
        gbc = at(big, 6144, 1024)
        tCS = at(big, 7168, 1024)
        foT = at(big, 8192, 512)
        catT = at(big, 8704, 2048)
        aN2 = at(big, 10752, 1024)
        ucv = at(big, 11776, 512)
        vcv = at(big, 12288, 512)
        bias2 = at(big, 12800, 3072)
        wf = at(big, 15872, 512)
        wr = at(big, 16384, KD * (NG + NE))
        comb = at(big, 0, NE * T)
        silg = at(big, 8192, 1024)
        he = [at(big, 10240, 1024), at(big, 11264, 1024)]
        diag = [at(big, 12288, 512), at(big, 12800, 512)]
        yfin = at(big, 0, 2048)
        M0 = 13312
        lg = at(big, M0, 40)
        lgp = at(big, M0 + 40, 8)
        m8 = at(big, M0 + 48, 8)
        i8 = at(big, M0 + 56, 8).bitcast(U32)
        gidx = at(big, M0 + 64, 1)
        goh = at(big, M0 + 68, 4)
        nmx = at(big, M0 + 72, 1)
        gex = at(big, M0 + 76, 4)
        gz = at(big, M0 + 80, 1)
        esel = at(big, M0 + 88, 8)
        esel4 = at(big, M0 + 96, 32)
        e8 = at(big, M0 + 128, 8)
        j8 = at(big, M0 + 136, 8).bitcast(U32)
        j8f = at(big, M0 + 144, 8)
        pw = at(big, M0 + 152, 4)
        c8 = at(big, M0 + 160, 16)
        comb32 = at(big, M0 + 176, 64)

        slab_loaded = [sem(f"slab_loaded{i}") for i in range(SLOTS)]
        slab_used = sem("slab_used")
        cond_loaded = sem("cond_loaded")
        inputs_loaded = sem("inputs_loaded")
        subk_loaded = sem("subk_loaded")
        ctx2_loaded = sem("ctx2_loaded")
        small2_loaded = sem("small2_loaded")
        out_stored = sem("out_stored")
        cond_ready = sem("cond_ready")
        mod_filled = sem("mod_filled")
        mod_stored = sem("mod_stored")
        norm_sq = sem("norm_sq")
        norm_sum = sem("norm_sum")
        norm_inv = sem("norm_inv")
        norm_rstd = sem("norm_rstd")
        norm_scaled = sem("norm_scaled")
        norm_done = sem("norm_done")
        bank_filled = sem("bank_filled")
        bank_emptied = sem("bank_emptied")
        gates_biased = sem("gates_biased")
        soft_ready = sem("soft_ready")
        lf_ready = sem("lf_ready")
        cums_filled = sem("cums_filled")
        diag_ready = sem("diag_ready")
        rrow_filled = sem("rrow_filled")
        rrow_used = sem("rrow_used")
        exps_in = sem("exps_in")
        exps_out = sem("exps_out")
        kw_ready = sem("kw_ready")
        cloc_filled = sem("cloc_filled")
        cloc_used = sem("cloc_used")
        kT_filled = sem("kT_filled")
        kT_stored = sem("kT_stored")
        qk_filled = sem("qk_filled")
        decay_in = sem("decay_in")
        decay_out = sem("decay_out")
        smat_ready = sem("smat_ready")
        smatT_filled = sem("smatT_filled")
        smatT_stored = sem("smatT_stored")
        num_filled = sem("num_filled")
        num_used = sem("num_used")
        hms_ready = sem("hms_ready")
        hrstd_ready = sem("hrstd_ready")
        m_ready = sem("m_ready")
        turn_filled = sem("turn_filled")
        turn_stored = sem("turn_stored")
        qkms_ready = sem("qkms_ready")
        qkrstd_ready = sem("qkrstd_ready")
        roped = sem("roped")
        scores_filled = sem("scores_filled")
        scaled = sem("scaled")
        logits_ready = sem("logits_ready")
        probs_ready = sem("probs_ready")
        sink_ready = sem("sink_ready")
        probsT_filled = sem("probsT_filled")
        probsT_stored = sem("probsT_stored")
        head_filled = sem("head_filled")
        head_stored = sem("head_stored")
        branch_filled = sem("branch_filled")
        merged_ready = sem("merged_ready")
        y_filled = sem("y_filled")
        x_updated = sem("x_updated")
        rscores_filled = sem("rscores_filled")
        rscores_stored = sem("rscores_stored")
        top_ready = sem("top_ready")
        texp_ready = sem("texp_ready")
        choice_ready = sem("choice_ready")
        choiceT_filled = sem("choiceT_filled")
        pick_ready = sem("pick_ready")
        oh1_ready = sem("oh1_ready")
        oh2_ready = sem("oh2_ready")
        ohw_ready = sem("ohw_ready")
        gate_filled = sem("gate_filled")
        gate_stored = sem("gate_stored")
        act_filled = sem("act_filled")
        gelu_ready = sem("gelu_ready")
        weight_ready = sem("weight_ready")
        peer_half = sem("peer_half")
        conv_ready = sem("conv_ready")
        four_filled = sem("four_filled")
        four_stored = sem("four_stored")
        router_filled = sem("router_filled")
        rexp_in = sem("rexp_in")
        rexp_out = sem("rexp_out")
        cdiag_ready = sem("cdiag_ready")
        comb_filled = sem("comb_filled")
        comb_stored = sem("comb_stored")
        up_filled = sem("up_filled")
        silu_ready = sem("silu_ready")
        he_ready = sem("he_ready")
        down_done = sem("down_done")
        hid_mul = sem("hid_mul")
        zeros_ready = sem("zeros_ready")
        dve_step = sem("dve_step")
        act_step = sem("act_step")
        pool_step = sem("pool_step")

        block = ctx.enter_context(nc.Block())

        UNITS_B1 = 4 + 4 + 4 + 2 + 2 + 2 + 8
        UNITS_Q = 8
        UNITS_B2 = 14

        @block.sync
        def _(sp):
            def load(n, slot, value):
                if value is not None:
                    sp.wait_ge(slab_used, value)
                sp.dma_start(slab[slot][:, :], w_stream[n]).then_inc(slab_loaded[slot], 16)

            for s in range(SLOTS):
                load(s, s, None)
            whole = N_SLABS // SLOTS
            with sp.Fori(1, whole) as i:
                for s in range(SLOTS):
                    load(i * SLOTS + s, s, i * SLOTS + (s - SLOTS + 1))
            for s in range(N_SLABS % SLOTS):
                n = whole * SLOTS + s
                load(n, s, n - SLOTS + 1)

        @block.gpsimd
        def _(pool):
            pool.wait_ge(pick_ready, 6)
            groups = T // GROUP
            for half in range(2):
                with pool.Fori(0, groups // 2) as g:
                    for s in range(2):
                        pool.wait_ge(oh1_ready, g * 2 + (half * groups + s + 1))
                        o1 = oh1[s].rearrange("p (m e) -> p m e", m=GROUP)
                        nc.gpsimd.tensor_tensor(
                            o1, o1, pick[:, bass.ds(g * (2 * GROUP) + (s * GROUP + 2 * T), GROUP)].unsqueeze(2)
                            .broadcast_to([P, GROUP, HALF_E1]), ALU.mult).then_inc(ohw_ready, 1)

        @block.scalar
        def _(act):
            steps = [0]

            def step(ins):
                steps[0] += 1
                ins.then_inc(act_step, 1)
                act.wait_ge(act_step, steps[0])

            act.dma_start(condr[:, :], cond).then_inc(cond_loaded, 16)
            for dst, src in ((cst, consts), (col, cols), (row, rows), (xT, x_t), (hcT, ctx_t)):
                act.dma_start(dst[:, :], src).then_inc(inputs_loaded, 16)
            act.wait_ge(cond_loaded, 16)
            nc.scalar.activation(conds[:, :], condr[:, :], ACT.Silu).then_inc(cond_ready, 1)

            def norm(i, dst, shift):
                act.wait_ge(norm_inv, i + 1)
                nc.scalar.activation(rstd[:, :], rstd[:, :], ACT.Sqrt).then_inc(norm_rstd, 1)
                if shift is not None:
                    for k in range(KD):
                        act.wait_ge(norm_scaled, NORM_SCALED[i] + k + 1)
                        nc.scalar.activation(dst[:, k * T:(k + 1) * T], dst[:, k * T:(k + 1) * T],
                                             ACT.Identity, bias=shift(k)).then_inc(norm_done, 1)

            unit = [0]

            def empty(dst, func=ACT.Copy, scale=1.0, src=None):
                u = unit[0]
                unit[0] += 1
                act.wait_ge(bank_filled, u + 1)
                nc.scalar.activation(dst, bank(u % 8) if src is None else src(u % 8), func,
                                     scale=scale).then_inc(bank_emptied, 1)

            norm(0, hT, lambda k: modc(0, 0, k, 0))
            norm(1, hcT, lambda k: modc(0, 0, k, 1))
            for c in range(4):
                empty(kN[:, c * 512:(c + 1) * 512], scale=KEY_SCALE)
            for c in range(4):
                empty(vA[:, c, :, 0:P], src=lambda b: bank(b).rearrange("p (h v) -> p h v", h=HEADS))
            for c in range(4):
                u = unit[0]
                unit[0] += 1
                act.wait_ge(bank_filled, u + 1)
                nc.scalar.activation(gat[:, c * 16:(c + 1) * 16], bank(u % 8, 16), ACT.Copy)
                nc.scalar.activation(akN[:, c * P:(c + 1) * P], bank(u % 8, P, 16), ACT.Copy)
                nc.scalar.activation(avN[:, c * P:(c + 1) * P], bank(u % 8, P, 16 + P),
                                     ACT.Copy).then_inc(bank_emptied, 1)
            for c in range(2):
                empty(qT[:, c * 512:(c + 1) * 512])
            for c in range(2):
                empty(aqN[:, c * 512:(c + 1) * 512])
            for c in range(2):
                empty(sigO[:, c * 512:(c + 1) * 512], ACT.Sigmoid)
            for c in range(8):
                empty(sigG[:, c * 512:(c + 1) * 512], ACT.Sigmoid)

            soft = small[:, 64:96]
            act.wait_ge(gates_biased, 1)
            step(nc.scalar.activation(soft, small[:, 32:64], ACT.Abs))
            step(nc.scalar.activation(soft, soft, ACT.Exp, scale=-1.0))
            nc.scalar.activation(soft, soft, ACT.Ln, bias=1.0).then_inc(soft_ready, 1)
            for c in range(2):
                act.wait_ge(kT_filled, c + 1)
                nc.scalar.activation(
                    kTl.rearrange("p (h t) -> p h t", h=HEADS)[:, :, c * P:(c + 1) * P],
                    bank(6 + c).rearrange("p (h t) -> p h t", h=HEADS), ACT.Copy).then_inc(kT_stored, 1)
            act.wait_ge(exps_in, 1)
            nc.scalar.activation(small[:, 400:504], small[:, 296:400], ACT.Exp).then_inc(exps_out, 1)
            act.wait_ge(decay_in, 4)
            nc.scalar.activation(decay[:, :], decay[:, :], ACT.Exp).then_inc(decay_out, 1)
            for n in range(4):
                act.wait_ge(smatT_filled, n + 1)
                if n >= 2:
                    act.wait_ge(num_filled, n - 1)
                else:
                    act.wait_ge(cloc_filled, 6)
                nc.scalar.activation(pair[n % 2], bank(1 + n % 2), ACT.Copy).then_inc(smatT_stored, 1)
            act.wait_ge(hms_ready, 1)
            nc.scalar.activation(small[:, 512:520], small[:, 512:520], ACT.Sqrt).then_inc(hrstd_ready, 1)
            act.wait_ge(qkms_ready, 1)
            nc.scalar.activation(small[:, 520:544], small[:, 520:544], ACT.Sqrt).then_inc(qkrstd_ready, 1)

            def turned(n, dst):
                act.wait_ge(turn_filled, n + 1)
                nc.scalar.activation(dst, bank(n % 8), ACT.Copy).then_inc(turn_stored, 1)

            for n in range(2):
                turned(n, qTa[:, n * 512:(n + 1) * 512])
            for n in range(2):
                turned(2 + n, kTa[:, n * 512:(n + 1) * 512])

            def attention(blk):
                def scale(u):
                    act.wait_ge(scores_filled, u + 1)
                    if u >= 2:
                        act.wait_ge(probs_ready, u - 1)
                    nc.scalar.activation(logit[u % 2], bank(u % 2), ACT.Copy,
                                         scale=ATT_SCALE).then_inc(scaled, 1)

                def softmax(u):
                    st = stat[:, 4 * u:4 * u + 4]
                    act.wait_ge(logits_ready, u + 1)
                    if u >= 2:
                        act.wait_ge(probsT_filled, u - 1)
                    nc.scalar.activation(probs[u % 2], logit[u % 2], ACT.Exp, bias=st[:, 0:1],
                                         accum_out=st[:, 1:2]).then_inc(probs_ready, 1)
                    if blk == 0:
                        h = u % AH
                        nc.scalar.activation(st[:, 2:3], rowv("sink")[:, h:h + 1], ACT.Exp,
                                             bias=st[:, 0:1]).then_inc(sink_ready, 1)

                first = blk * UNITS
                scale(first)
                for u in range(first, first + UNITS):
                    if u + 1 < first + UNITS:
                        scale(u + 1)
                    softmax(u)

            attention(0)
            for n in range(2):
                turned(4 + n, mT[:, n * 512:(n + 1) * 512])
            for n in range(2):
                turned(6 + n, aT[:, n * 512:(n + 1) * 512])
            act.wait_ge(y_filled, 2)
            act.dma_start(subk, sub_keys).then_inc(subk_loaded, 16)
            norm(2, hT, lambda k: modc(0, 3, k, 0))
            act.dma_start(hcT[:, :], ctx2_t).then_inc(ctx2_loaded, 16)
            for c in range(8):
                empty(qTr[:, c * 512:(c + 1) * 512])
            for t in range(NT):
                for b in range(4):
                    act.wait_ge(rscores_filled, t * 4 + b + 1)
                    nc.scalar.activation(sc[t][:, b * 512:(b + 1) * 512], bank(4 * t + b),
                                         ACT.Copy).then_inc(rscores_stored, 1)
            for t in range(NT):
                act.wait_ge(top_ready, t + 1)
                nc.scalar.activation(choice[2], choice[2], ACT.Exp).then_inc(texp_ready, 1)
                for i in range(3):
                    act.wait_ge(choiceT_filled, 3 * t + i + 1)
                    nc.scalar.activation(pick[:, i * T + t * P:i * T + (t + 1) * P],
                                         bank(i, P), ACT.Copy).then_inc(pick_ready, 1)

            gview = gate.rearrange("p (e m) -> p m e", m=T)
            groups = T // GROUP
            for half in range(2):
                if half:
                    act.wait_ge(peer_half, half)
                with act.Fori(0, groups // 2) as g:
                    for s in range(2):
                        act.wait_ge(gate_filled, g * 2 + (half * groups + s + 1))
                        nc.scalar.activation(gview[:, bass.ds(g * (2 * GROUP) + s * GROUP, GROUP), :],
                                             bank(s).rearrange("p (m e) -> p m e", m=GROUP),
                                             ACT.Copy).then_inc(gate_stored, 1)
                base = half * 2 * HALF_SLABS
                with act.Fori(0, HALF_SLABS // 4) as i:
                    for s in range(8):
                        act.wait_ge(act_filled, i * 8 + (base + s + 1))
                        if half or s >= 2:
                            act.wait_ge(weight_ready, i * 8 + (base + s - 1))
                        else:
                            act.wait_ge(weight_ready, i * 8 + (base + s))
                        nc.scalar.activation(gel[s % 2], bank(s % 4),
                                             ACT.Gelu_apprx_tanh).then_inc(gelu_ready, 1)

            act.wait_ge(peer_half, 2)
            for dst, src in ((bias2, rpb), (wf, w_four), (wr, w_router)):
                act.dma_start(dst, src).then_inc(small2_loaded, 16)
            norm(3, hcT, lambda k: modc(1, 0, k, 1))
            norm(4, hT, lambda k: modc(1, 0, k, 0))
            for c in range(4):
                empty(kT2[:, c * 512:(c + 1) * 512])
            for c in range(4):
                empty(vN2[:, c * 512:(c + 1) * 512])
            for c in range(2):
                empty(qT2[:, c * 512:(c + 1) * 512])
            empty(fN)
            empty(hcv)
            for c in range(2):
                empty(gbc[:, c * 512:(c + 1) * 512])
            for n, dst in enumerate((tCS[:, 0:512], tCS[:, 512:1024], foT, catT[:, 0:512])):
                act.wait_ge(four_filled, n + 1)
                nc.scalar.activation(dst, bank(n % 2), ACT.Copy).then_inc(four_stored, 1)
            attention(1)
            for n in range(2):
                turned(8 + n, catT[:, (1 + n) * 512:(2 + n) * 512])
            norm(5, hT, lambda k: modc(1, 3, k, 0))
            for t in range(NT):
                act.wait_ge(rexp_in, 2 * t + 1)
                nc.scalar.activation(gex, gex, ACT.Exp, accum_out=gz).then_inc(rexp_out, 1)
                act.wait_ge(rexp_in, 2 * t + 2)
                nc.scalar.activation(pw[:, 0:2], pw[:, 0:2], ACT.Exp,
                                     accum_out=pw[:, 2:3]).then_inc(rexp_out, 1)
            cview = comb.rearrange("p (e m) -> p e m", m=T)
            for n in range(2 * NE // 4):
                t, q = n // (NE // 4), n % (NE // 4)
                act.wait_ge(comb_filled, n + 1)
                nc.scalar.activation(cview[:, 4 * q:4 * q + 4, t * P:(t + 1) * P],
                                     bank(n % 2).rearrange("p (e m) -> p e m", e=4),
                                     ACT.Copy).then_inc(comb_stored, 1)

            def silu(e, first=False):
                for b in range(2):
                    act.wait_ge(up_filled, e * 4 + b + 1)
                    if not first:
                        act.wait_ge(he_ready, e)
                    nc.scalar.activation(silg[:, b * 512:(b + 1) * 512], bank(b),
                                         ACT.Silu).then_inc(silu_ready, 1)

            silu(0, True)
            with act.Fori(1, NE) as e:
                silu(e)
            norm(6, None, None)
            act.wait_ge(norm_done, NORM_DONE[6] + KD)
            act.dma_start(out, yfin).then_inc(out_stored, 16)
            act.wait_ge(out_stored, 16)

        @block.tensor
        def _(pe):
            def weights(n, i=None):
                v = 16 * (n // SLOTS + 1)
                pe.wait_ge(slab_loaded[n % SLOTS], v if i is None else i * 16 + v)
                return slab[n % SLOTS]

            def used(ins):
                ins.then_inc(slab_used, 1)

            def release():
                pe.sem_inc(slab_used, 1)

            def chain(dst, pairs):
                for k, (a, b) in enumerate(pairs):
                    ins = nc.tensor.matmul(dst, a, b, start=k == 0, stop=k == len(pairs) - 1)
                return ins

            pe.wait_ge(cond_ready, 1)
            cnd = conds.rearrange("p (k c) -> p k c", k=KD)

            def ada(m, i, s):
                n = m * ADA_SLABS + s
                w = weights(n, i).rearrange("p (k n) -> p k n", k=KD)
                if not (isinstance(i, int) and m == 0):
                    pe.wait_ge(mod_stored, i * 4 + (n - 3))
                for j in range(4):
                    ins = chain(bank(s, 2, 2 * j), [(w[:, k, j * P:(j + 1) * P], cnd[:, k, 2 * m:2 * m + 2])
                                                    for k in range(KD)])
                ins.then_inc(mod_filled, 1)
                pe.wait_ge(mod_filled, i * 4 + (n + 1))
                release()

            for m in range(2):
                for s in range(4):
                    ada(m, 0, s)
                with pe.Fori(1, ADA_SLABS // 4) as i:
                    for s in range(4):
                        ada(m, i, s)

            def norm(i):
                b = 6 + i % 2
                sq = scratch[:, (i % 2) * 2048:(i % 2) * 2048 + 2048]
                pe.wait_ge(norm_sq, i + 1)
                chain(bank(b, T), [(ones, sq[:, k * T:(k + 1) * T]) for k in range(KD)]).then_inc(norm_sum, 1)

            norm(0)
            norm(1)
            unit = [0]

            def fill(parts, after=None):
                u = unit[0]
                unit[0] += 1
                if u >= 8:
                    pe.wait_ge(bank_emptied, u - 7)
                for o, n, pairs in parts:
                    ins = chain(bank(u % 8, n, o), pairs)
                ins.then_inc(bank_filled, 1)
                return u

            def slab_done():
                pe.wait_ge(bank_filled, unit[0])
                release()

            def by_token(h, t, w, n):
                return [(0, n, [(h[:, k * T + t * P:k * T + (t + 1) * P], w[:, k, 0:n]) for k in range(KD)])]

            def by_feature(h, w, j):
                return [(w[:, k, j * P:(j + 1) * P], h[:, k * T:(k + 1) * T]) for k in range(KD)]

            def k_view(n, width=512):
                return weights(n)[:, 0:KD * width].rearrange("p (k n) -> p k n", k=KD)

            pe.wait_ge(norm_done, 2 * KD)
            tiles = ((hcT, 0), (hcT, 1), (hT, 0), (hT, 1))
            for s, width in ((S_K, 512), (S_V, 512), (S_GKV, 272)):
                w = k_view(s, width)
                for h, t in tiles:
                    fill(by_token(h, t, w, width))
                slab_done()
            w = k_view(S_Q)
            for j in range(0, 4, 2):
                fill([(0, T, by_feature(hT, w, j)), (T, T, by_feature(hT, w, j + 1))])
            slab_done()
            for s in (S_AQ, S_O):
                w = k_view(s)
                for t in range(NT):
                    fill(by_token(hT, t, w, 512))
                slab_done()
            for s in range(S_MG, S_MG + 4):
                w = k_view(s)
                for j in range(0, 4, 2):
                    fill([(0, T, by_feature(hT, w, j)), (T, T, by_feature(hT, w, j + 1))])
                slab_done()
            pe.wait_ge(bank_emptied, unit[0])

            pe.wait_ge(lf_ready, 1)
            lf = small[:, 96:128]
            for d in range(2):
                nc.tensor.matmul(bank(0, 16, 16 * d), const(f"tri{d}"), lf[:, 16 * d:16 * d + 16],
                                 start=True, stop=True)
            nc.tensor.matmul(bank(0, 32, 32), ones, lf, start=True, stop=True).then_inc(cums_filled, 1)
            for c in range(2):
                for h in range(HEADS):
                    ins = nc.tensor.transpose(bank(6 + c, P, h * P), kN[:, (2 + c) * 512 + h * P:(2 + c) * 512 + (h + 1) * P],
                                              ident)
                ins.then_inc(kT_filled, 1)
            for n in range(8):
                pe.wait_ge(diag_ready, n + 1)
                if n >= 2:
                    pe.wait_ge(rrow_used, n - 1)
                nc.tensor.matmul(bank(1 + n % 2), ones, pair[n % 2], start=True, stop=True).then_inc(rrow_filled, 1)
            for c in range(2):
                pe.wait_ge(kT_stored, c + 1)
                for h in range(HEADS):
                    o = h * T + c * P
                    ins = nc.tensor.matmul(bank(3 * c, P, h * P), qT[:, o:o + P], kTl[:, o:o + P],
                                           start=True, stop=True)
                ins.then_inc(qk_filled, 1)
            for n in range(6):
                p, d = n // 2, n % 2
                c = (p, p ^ 1)[d]
                pe.wait_ge(kw_ready, n + 1)
                if n >= 1:
                    pe.wait_ge(cloc_used, n)
                for h in range(HEADS):
                    ins = nc.tensor.matmul(ps[:, 4 * 512 + h * 256:4 * 512 + h * 256 + 129],
                                           pair[n % 2][:, h * P:(h + 1) * P], vA[:, c, h, :], start=True, stop=True)
                ins.then_inc(cloc_filled, 1)
            for n in range(4):
                p, d = n // 2, n % 2
                lc = (p, p ^ 1)[d]
                pe.wait_ge(smat_ready, n + 1)
                for h in range(HEADS):
                    o = (2 * d + p) * 512 + h * P
                    ins = nc.tensor.transpose(bank(1 + n % 2, P, h * P), decay[:, o:o + P], ident)
                ins.then_inc(smatT_filled, 1)
                if n == 0:
                    pe.wait_ge(cloc_used, 6)
                else:
                    pe.wait_ge(num_used, n)
                for h in range(HEADS):
                    nc.tensor.matmul(ps[:, 4 * 512 + h * 256:4 * 512 + h * 256 + 129],
                                     qT[:, h * T + lc * P:h * T + (lc + 1) * P], state[p][d][:, h, :],
                                     start=True, stop=True)
                pe.wait_ge(smatT_stored, n + 1)
                for h in range(HEADS):
                    ins = nc.tensor.matmul(ps[:, 6 * 512 + h * 256:6 * 512 + h * 256 + 129],
                                           pair[n % 2][:, h * P:(h + 1) * P], vA[:, 2 + lc, h, :],
                                           start=True, stop=True)
                ins.then_inc(num_filled, 1)

            def turn(n, srcs):
                for j, s in enumerate(srcs):
                    ins = nc.tensor.transpose(bank(n % 8, P, j * P), s, ident)
                ins.then_inc(turn_filled, 1)

            pe.wait_ge(num_used, 4)
            pe.wait_ge(roped, 1)
            for n in range(2):
                turn(n, [qR[:, t * 512 + pr * P:t * 512 + (pr + 1) * P]
                         for pr in (2 * n, 2 * n + 1) for t in range(NT)])
            for n, k in enumerate((kR, kSw)):
                turn(2 + n, [k[:, c * P:(c + 1) * P] for c in (2, 3, 0, 1)])

            def attention(blk):
                first = blk * UNITS

                def keys(h):
                    if blk == 0:
                        kv, base = h // 4, h % 2
                        return kTa[DH * base:DH * base + DH, (0 if kv == base else 512):(512 if kv == base else 1024)]
                    return kT2[DH * (h % 2):DH * (h % 2) + DH, (h // 2) * 512:(h // 2 + 1) * 512]

                def queries(b, h):
                    q = qTa if blk == 0 else qT2
                    o = (h // 2) * T + b * P
                    return q[DH * (h % 2):DH * (h % 2) + DH, o:o + P]

                def values(c, h):
                    if blk == 0:
                        o = (2, 3, 0, 1)[c] * P + (h // 4) * DH
                        return avN[:, o:o + DH]
                    return vN2[:, c * 512 + h * DH:c * 512 + (h + 1) * DH]

                def scores(u):
                    b, h = (u - first) // AH, u % AH
                    if u >= 2:
                        pe.wait_ge(scaled, u - 1)
                    nc.tensor.matmul(bank(u % 2), queries(b, h), keys(h), start=True,
                                     stop=True).then_inc(scores_filled, 1)

                def apply(u):
                    b, h = (u - first) // AH, u % AH
                    pe.wait_ge(probs_ready, u + 1)
                    if u >= 2:
                        pe.wait_ge(probsT_stored, u - 1)
                    for c in range(4):
                        ins = nc.tensor.transpose(bank(2 + u % 2, P, c * P), probs[u % 2][:, c * P:(c + 1) * P], ident)
                    ins.then_inc(probsT_filled, 1)
                    pe.wait_ge(probsT_stored, u + 1)
                    if u >= 2:
                        pe.wait_ge(head_stored, u - 1)
                    chain(bank(4 + u % 2, DH), [(probsT[u % 2][:, c * P:(c + 1) * P], values(c, h))
                                                for c in range(4)]).then_inc(head_filled, 1)

                scores(first)
                for u in range(first, first + UNITS):
                    if u + 1 < first + UNITS:
                        scores(u + 1)
                    apply(u)

            pe.wait_ge(turn_stored, 4)
            attention(0)
            pe.wait_ge(m_ready, 1)
            pe.wait_ge(head_stored, UNITS)
            for i, src in enumerate((hN, aN)):
                for n in range(2):
                    turn(4 + 2 * i + n, [src[:, t * 512 + j * P:t * 512 + (j + 1) * P]
                                         for j in (2 * n, 2 * n + 1) for t in range(NT)])
            pe.wait_ge(turn_stored, 8)
            for i, src in enumerate((mT, aT)):
                w = weights(S_BM + i).rearrange("p (k n) -> p k n", k=4)
                for b in range(4):
                    for j in range(2):
                        o = (2 * b + j) * P
                        ins = chain(bank(4 * i + b, T, j * T),
                                    [(w[:, k, o:o + P], src[:, k * T:(k + 1) * T]) for k in range(4)])
                ins.then_inc(branch_filled, 1)
                pe.wait_ge(branch_filled, i + 1)
                release()

            def project_out(s0, src, base):
                for half in range(2):
                    w = weights(s0 + half).rearrange("p (k n) -> p k n", k=KD)
                    for b in range(2):
                        for j in range(2):
                            ins = chain(bank(2 * half + b, T, j * T), by_feature(src, w, 2 * b + j))
                    ins.then_inc(y_filled, 1)
                    pe.wait_ge(y_filled, base + half + 1)
                    release()

            pe.wait_ge(merged_ready, 4)
            project_out(S_OUT, merged, 0)

            norm(2)
            pe.wait_ge(norm_done, 3 * KD)
            for s in range(4):
                w = k_view(S_QUERY + s)
                for j in range(0, 4, 2):
                    fill([(0, T, by_feature(hT, w, j)), (T, T, by_feature(hT, w, j + 1))])
                slab_done()
            pe.wait_ge(bank_emptied, unit[0])
            pe.wait_ge(subk_loaded, 16)
            for t in range(NT):
                for b in range(4):
                    for j in range(4):
                        hp = 4 * b + j
                        ins = nc.tensor.matmul(bank(4 * t + b, P, j * P), qTr[:, hp * T + t * P:hp * T + (t + 1) * P],
                                               subk[:, hp * P:(hp + 1) * P], start=True, stop=True)
                    ins.then_inc(rscores_filled, 1)
            pe.wait_ge(rscores_stored, 8)
            for t in range(NT):
                pe.wait_ge(choice_ready, t + 1)
                if t:
                    pe.wait_ge(pick_ready, 3 * t)
                for i in range(3):
                    nc.tensor.transpose(bank(i, P), choice[i], ident).then_inc(choiceT_filled, 1)

            pe.wait_ge(pick_ready, 6)
            def open_sums():
                for b in range(4):
                    nc.tensor.matmul(bank(4 + b), const("ones"), zeros512, start=True, stop=True)

            zeros512 = cst[:, CONSTS["window"][0]:CONSTS["window"][0] + 512]
            pe.wait_ge(zeros_ready, 1)
            open_sums()
            groups = T // GROUP
            for half in range(2):
                def gates(g, s, half=half):
                    n = g * 2 + (half * groups + s)
                    pe.wait_ge(ohw_ready, n + 1)
                    pe.wait_ge(oh2_ready, n + 1)
                    if not (isinstance(g, int) and half == 0):
                        pe.wait_ge(gate_stored, n - 1)
                    for m in range(GROUP):
                        ins = nc.tensor.matmul(bank(s, HALF_E1, m * HALF_E1), oh2[s][:, m * P:(m + 1) * P],
                                               oh1[s][:, m * HALF_E1:(m + 1) * HALF_E1], start=True, stop=True)
                    ins.then_inc(gate_filled, 1)

                for s in range(2):
                    gates(0, s)
                with pe.Fori(1, groups // 2) as g:
                    for s in range(2):
                        gates(g, s)
                pe.wait_ge(gate_stored, (half + 1) * groups)
                base = S_PEER + half * 2 * HALF_SLABS
                ubase = half * 2 * HALF_SLABS

                def activations(i, s, half=half, base=base, ubase=ubase):
                    w = weights(base + s, i).rearrange("p (k n) -> p k n", k=KD)
                    for b in range(2):
                        u = i * 8 + (ubase + 2 * s + b)
                        if not (isinstance(i, int) and half == 0 and 2 * s + b < 4):
                            pe.wait_ge(gelu_ready, u - 3)
                        for j in range(2):
                            ins = chain(bank((2 * s + b) % 4, T, j * T), by_feature(hT, w, 2 * b + j))
                        ins.then_inc(act_filled, 1)
                    pe.wait_ge(act_filled, u + 1)
                    release()

                for s in range(4):
                    activations(0, s)
                with pe.Fori(1, HALF_SLABS // 4) as i:
                    for s in range(4):
                        activations(i, s)
                pe.wait_ge(weight_ready, (half + 1) * 2 * HALF_SLABS)
                base = S_PEER + (2 * half + 1) * HALF_SLABS
                with pe.Fori(0, HALF_SLABS // 4) as i:
                    for s in range(4):
                        w = weights(base + s, i).rearrange("p (e n) -> p e n", e=4)
                        for e in range(4):
                            for c in range(KD):
                                ins = nc.tensor.matmul(bank(4 + c // 2, T, (c % 2) * T), w[:, e, c * P:(c + 1) * P],
                                                       gate[:, bass.ds(i * (16 * T) + (4 * s + e) * T, T)],
                                                       start=False, stop=True, skip_group_check=True)
                        used(ins)
                nc.tensor.matmul(bank(0, 1), ones, ones[:, 0:1], start=True, stop=True).then_inc(peer_half, 1)

            norm(3)
            norm(4)
            pe.wait_ge(norm_done, 5 * KD)
            w = k_view(S_K2)
            for j in range(4):
                fill([(0, T, by_feature(hT, w, j)), (T, T, by_feature(hcT, w, j))])
            slab_done()
            w = k_view(S_V2)
            for h, t in ((hT, 0), (hT, 1), (hcT, 0), (hcT, 1)):
                fill(by_token(h, t, w, 512))
            slab_done()
            w = k_view(S_Q2)
            for j in range(0, 4, 2):
                fill([(0, T, by_feature(hT, w, j)), (T, T, by_feature(hT, w, j + 1))])
            slab_done()
            w = k_view(S_FH2)
            fill([(t * T, T, [(hT[:, k * T + t * P:k * T + (t + 1) * P], w[:, k, 0:T]) for k in range(KD)])
                  for t in range(NT)])
            fill([(0, T, by_feature(hT, w, 2)), (T, T, by_feature(hT, w, 3))])
            slab_done()
            w = k_view(S_G2)
            for j in range(0, 4, 2):
                fill([(0, T, by_feature(hT, w, j)), (T, T, by_feature(hT, w, j + 1))])
            slab_done()
            pe.wait_ge(bank_emptied, unit[0])
            pe.wait_ge(small2_loaded, 48)
            for n, name in enumerate(("dft_c", "dft_s")):
                tab = const(name)
                for j in range(2):
                    ins = chain(bank(n, T, j * T), [(fN[:, t * T + j * P:t * T + (j + 1) * P], tab[:, t * T:(t + 1) * T])
                                                    for t in range(NT)])
                ins.then_inc(four_filled, 1)
            pe.wait_ge(four_stored, 2)
            for j in range(2):
                ins = chain(bank(0, T, j * T), [(const("dch_c"), tCS[:, j * T:(j + 1) * T]),
                                                (const("dch_s"), tCS[:, 512 + j * T:512 + (j + 1) * T])])
            ins.then_inc(four_filled, 1)
            pe.wait_ge(four_stored, 3)
            for j in range(2):
                ins = chain(bank(1, T, j * T), [(wf[:, k * T + j * P:k * T + (j + 1) * P], foT[:, k * T:(k + 1) * T])
                                                for k in range(2)])
            ins.then_inc(four_filled, 1)
            pe.wait_ge(four_stored, 4)
            attention(1)
            pe.wait_ge(head_stored, 2 * UNITS)
            for n in range(2):
                turn(8 + n, [aN2[:, t * 512 + j * P:t * 512 + (j + 1) * P] for j in (2 * n, 2 * n + 1) for t in range(NT)])
            pe.wait_ge(turn_stored, 10)
            pe.wait_ge(conv_ready, 1)
            project_out(S_OUT2, catT, 2)
            norm(5)
            pe.wait_ge(norm_done, 6 * KD)
            nr = NG + NE
            for t in range(NT):
                chain(bank(t, nr), [(hT[:, k * T + t * P:k * T + (t + 1) * P], wr[:, k * nr:(k + 1) * nr])
                                    for k in range(KD)]).then_inc(router_filled, 1)
            for n in range(2 * NE // 4):
                pe.wait_ge(cdiag_ready, n + 1)
                if n >= 2:
                    pe.wait_ge(comb_stored, n - 1)
                nc.tensor.matmul(bank(n % 2), ones, diag[n % 2], start=True, stop=True).then_inc(comb_filled, 1)
            pe.wait_ge(comb_stored, 2 * NE // 4)
            for b in range(4):
                nc.tensor.matmul(bank(4 + b), ones, zeros512, start=True, stop=True)

            def up(e, n, i=None, first=False):
                for g in range(2):
                    w = weights(n + g, i).rearrange("p (k n) -> p k n", k=KD)
                    for b in range(2):
                        if not first:
                            if g == 0:
                                pe.wait_ge(silu_ready, e * 2 + (b - 1))
                            else:
                                pe.wait_ge(he_ready, e)
                        for j in range(2):
                            ins = chain(bank(2 * g + b, T, j * T), by_feature(hT, w, 2 * b + j))
                        ins.then_inc(up_filled, 1)
                    pe.wait_ge(up_filled, e * 4 + (2 * g + 2))
                    release()

            def down(e, par, n, i=None):
                w = weights(n, i).rearrange("p (f n) -> p f n", f=4)
                pe.wait_ge(he_ready, e + 1)
                for f in range(4):
                    for c in range(KD):
                        ins = nc.tensor.matmul(bank(4 + c // 2, T, (c % 2) * T), w[:, f, c * P:(c + 1) * P],
                                               he[par][:, f * T:(f + 1) * T], start=False, stop=True,
                                               skip_group_check=True)
                ins.then_inc(down_done, 1)
                pe.wait_ge(down_done, e + 1)
                release()

            up(0, S_MOE, first=True)
            with pe.Fori(0, (NE - 1) // 4) as i:
                for r in range(4):
                    n = S_MOE + 2 + 3 * r
                    up(i * 4 + (1 + r), n, i * 3)
                    down(i * 4 + r, r % 2, n + 2, i * 3)
            for e in range((NE - 1) // 4 * 4 + 1, NE):
                n = S_MOE + 2 + 3 * (e - 1)
                up(e, n)
                down(e - 1, (e - 1) % 2, n + 2)
            down(NE - 1, (NE - 1) % 2, N_SLABS - 1)
            norm(6)

        @block.vector
        def _(dve):
            V = nc.vector
            steps = [0]

            def step(ins):
                steps[0] += 1
                ins.then_inc(dve_step, 1)
                dve.wait_ge(dve_step, steps[0])

            dve.wait_ge(inputs_loaded, 16 * 5)

            def squares(i, src):
                sq = scratch[:, (i % 2) * 2048:(i % 2) * 2048 + 2048]
                V.tensor_tensor(sq, src[:, :], src[:, :], ALU.mult).then_inc(norm_sq, 1)

            def norm(i, src, dst, g, scale):
                b = 6 + i % 2
                dve.wait_ge(norm_sum, i + 1)
                step(V.tensor_scalar(rstd[:, :], bank(b, T), 1.0 / D, EPS, ALU.mult, ALU.add))
                V.reciprocal(rstd[:, :], rstd[:, :]).then_inc(norm_inv, 1)
                if scale is None:
                    step(V.tensor_copy(gain[:, :], g))
                else:
                    step(V.tensor_scalar(gain[:, :], scale, 1.0, None, ALU.add))
                    step(V.tensor_tensor(gain[:, :], gain[:, :], g, ALU.mult))
                dve.wait_ge(norm_rstd, i + 1)
                for k in range(KD):
                    V.scalar_tensor_tensor(out=dst[:, k * T:(k + 1) * T], in0=src[:, k * T:(k + 1) * T],
                                           scalar=gain[:, k:k + 1], in1=rstd[:, :], op0=ALU.mult,
                                           op1=ALU.mult).then_inc(norm_scaled if scale is not None else norm_done, 1)

            squares(0, xT)
            squares(1, hcT)
            md = mod.rearrange("p (n c) -> p n c", c=2)
            with dve.Fori(0, 2 * ADA_SLABS // 4) as i:
                for s in range(4):
                    dve.wait_ge(mod_filled, i * 4 + (s + 1))
                    V.tensor_tensor(md[:, bass.ds(i * 16 + s * 4, 4), :],
                                    bank(s, 8).rearrange("p (j c) -> p j c", c=2),
                                    colv("b_ada")[:, bass.ds(i * 16 + s * 4, 4)].unsqueeze(2).broadcast_to([P, 4, 2]),
                                    ALU.add).then_inc(mod_stored, 1)
            dve.wait_ge(mod_stored, 2 * ADA_SLABS)
            norm(0, xT, hT, colv("g_mix"), modp(0, 1, 0))
            dve.wait_ge(norm_scaled, KD)
            norm(1, hcT, hcT, colv("g_mix"), modp(0, 1, 1))

            L2 = small
            li, fg, soft, lf = L2[:, 0:32], L2[:, 32:64], L2[:, 64:96], L2[:, 96:128]
            cum, tot, rr = L2[:, 128:160], L2[:, 160:192], L2[:, 192:224]
            rmax = L2[:, 224:256]
            lmax = L2[:, 256:272]
            mst = L2[:, 272:296]
            exin, exout = L2[:, 296:400], L2[:, 400:504]
            v3 = lambda t: t.rearrange("p (d c h) -> p d c h", d=2, c=4)
            g4 = gat.rearrange("p (c d g h) -> p c d g h", c=4, d=2, g=2)
            bg = rowv("b_gates").rearrange("p (d g h) -> p d g h", d=2, g=2)
            dve.wait_ge(bank_emptied, 12)
            dve.wait_ge(norm_done, 2 * KD)
            for gi, dst in ((0, li), (1, fg)):
                for d in range(2):
                    for p in range(4):
                        c = (p, p ^ 1)[d]
                        ins = V.tensor_tensor(v3(dst)[:, d, p, :], g4[:, c, d, gi, :], bg[:, d, gi, :], ALU.add)
            ins.then_inc(gates_biased, 1)
            dve.wait_ge(gates_biased, 1)
            V.memset(vA[:, :, :, P:P + 1], 1.0)
            step(V.tensor_scalar(lf, fg, 0.0, None, ALU.min))
            dve.wait_ge(soft_ready, 1)
            V.tensor_tensor(lf, lf, soft, ALU.subtract).then_inc(lf_ready, 1)
            dve.wait_ge(cums_filled, 1)
            V.tensor_copy(cum, bank(0, 32))
            step(V.tensor_copy(tot, bank(0, 32, 32)))
            step(V.tensor_tensor(rr, li, cum, ALU.subtract))
            idb = ident.unsqueeze(1).broadcast_to([P, HEADS, P])
            h3 = lambda t: t.rearrange("p (h s) -> p h s", h=HEADS)

            def place_diag(n):
                if n >= 2:
                    dve.wait_ge(rrow_filled, n - 1)
                V.tensor_tensor(h3(pair[n % 2]), idb, rr[:, 4 * n:4 * n + 4].unsqueeze(2).broadcast_to([P, HEADS, P]),
                                ALU.mult).then_inc(diag_ready, 1)

            place_diag(0)
            dve.wait_ge(bank_filled, UNITS_B1)
            for n in range(8):
                d, p = n // 4, n % 4
                if n + 1 < 8:
                    place_diag(n + 1)
                dve.wait_ge(rrow_filled, n + 1)
                rowb = bank(1 + n % 2).rearrange("p (h s) -> p h s", h=HEADS)
                ins = V.tensor_reduce(rmax[:, 4 * n:4 * n + 4], rowb, X, ALU.max)
                if p >= 2:
                    dst = h3(decay[:, (2 * d + p - 2) * 512:(2 * d + p - 1) * 512])
                    ins = V.tensor_tensor(dst, rowb, const(f"seen{d}").unsqueeze(1).broadcast_to([P, HEADS, P]), ALU.add)
                ins.then_inc(rrow_used, 1)
            dve.wait_ge(rrow_used, 8)
            for n in range(4):
                ins = V.tensor_reduce(lmax[:, 4 * n:4 * n + 4], h3(decay[:, n * 512:(n + 1) * 512]), X, ALU.max)
            ex = lambda q: exin[:, 8 * q:8 * q + 8].rearrange("p (d h) -> p d h", d=2)
            eo = lambda q: exout[:, 8 * q:8 * q + 8].rearrange("p (d h) -> p d h", d=2)
            ms = lambda q: mst[:, 8 * q:8 * q + 8].rearrange("p (d h) -> p d h", d=2)
            lm = lmax.rearrange("p (d c h) -> p d c h", d=2, c=2)
            step(ins)
            for p in range(3):
                if p == 0:
                    step(V.tensor_copy(ex(0), v3(tot)[:, :, 0, :]))
                else:
                    step(V.tensor_tensor(ex(3 * p), v3(tot)[:, :, p, :], ms(p - 1), ALU.add))
                step(V.tensor_tensor(ex(3 * p + 1), v3(tot)[:, :, p, :], v3(rmax)[:, :, p, :], ALU.add))
                step(V.tensor_tensor(ms(p), ex(3 * p), ex(3 * p + 1), ALU.max))
                step(V.tensor_tensor(ex(3 * p), ex(3 * p), ms(p), ALU.subtract))
                step(V.tensor_tensor(ex(3 * p + 1), ex(3 * p + 1), ms(p), ALU.subtract))
                step(V.tensor_tensor(ex(3 * p + 2), v3(rr)[:, :, p, :], v3(rmax)[:, :, p, :], ALU.subtract))
            for q in range(2):
                step(V.tensor_tensor(lm[:, :, q, :], lm[:, :, q, :], ms(q + 1), ALU.max))
                step(V.tensor_tensor(ex(9 + q), ms(q + 1), lm[:, :, q, :], ALU.subtract))
                step(V.tensor_tensor(ex(11 + q), v3(cum)[:, :, 2 + q, :], lm[:, :, q, :], ALU.add))
                step(V.tensor_scalar(ex(11 + q), ex(11 + q), -1.0, None, ALU.mult))
            V.engine_nop().then_inc(exps_in, 1)
            for n in range(4):
                dd = h3(decay[:, n * 512:(n + 1) * 512])
                V.tensor_tensor(dd, dd, lmax[:, 4 * n:4 * n + 4].unsqueeze(2).broadcast_to([P, HEADS, P]),
                                ALU.subtract).then_inc(decay_in, 1)
            dve.wait_ge(exps_out, 1)
            bc = lambda a: a.unsqueeze(2).broadcast_to([P, HEADS, 129])
            ps4 = lambda b: ps[:, b * 512:(b + 2) * 512].rearrange("p (h v) -> p h v", h=HEADS)[:, :, 0:129]

            def weight_keys(n):
                p, d = n // 2, n % 2
                c = (p, p ^ 1)[d]
                if n >= 2:
                    dve.wait_ge(cloc_filled, n - 1)
                else:
                    dve.wait_ge(rrow_filled, 8)
                V.tensor_tensor(h3(pair[n % 2]), h3(kN[:, c * 512:(c + 1) * 512]),
                                eo(3 * p + 2)[:, d, :].unsqueeze(2).broadcast_to([P, HEADS, P]),
                                ALU.mult).then_inc(kw_ready, 1)

            weight_keys(0)
            for n in range(6):
                p, d = n // 2, n % 2
                if n + 1 < 6:
                    weight_keys(n + 1)
                dve.wait_ge(cloc_filled, n + 1)
                old, new = eo(3 * p)[:, d, :], eo(3 * p + 1)[:, d, :]
                src, dst = (state[0][d], state[0][d]) if p < 2 else (state[0][d], state[1][d])
                if p == 0:
                    V.tensor_tensor(dst, ps4(4), bc(new), ALU.mult).then_inc(cloc_used, 1)
                    dve.wait_ge(cloc_used, n + 1)
                else:
                    V.tensor_tensor(t1, ps4(4), bc(new), ALU.mult).then_inc(cloc_used, 1)
                    step(V.tensor_tensor(dst, src, bc(old), ALU.mult))
                    dve.wait_ge(cloc_used, n + 1)
                    step(V.tensor_tensor(dst, dst, t1, ALU.add))
            dve.wait_ge(decay_out, 1)
            dve.wait_ge(qk_filled, 2)
            for n in range(4):
                p, d = n // 2, n % 2
                lc = (p, p ^ 1)[d]
                o = (2 * d + p) * 512
                V.tensor_tensor(decay[:, o:o + 512], bank(3 * lc), decay[:, o:o + 512], ALU.mult).then_inc(smat_ready, 1)
            for n in range(4):
                p, d = n // 2, n % 2
                lc = (p, p ^ 1)[d]
                dve.wait_ge(num_filled, n + 1)
                step(V.tensor_tensor(t1, ps4(4), bc(eo(9 + p)[:, d, :]), ALU.mult))
                V.tensor_tensor(t1, t1, ps4(6), ALU.add).then_inc(num_used, 1)
                dve.wait_ge(num_used, n + 1)
                den, den2 = small[:, 608:612], small[:, 612:616]
                step(V.tensor_scalar(den2, t1[:, :, P], -1.0, None, ALU.mult))
                step(V.tensor_tensor(den, t1[:, :, P], den2, ALU.max))
                step(V.tensor_tensor(den, den, eo(11 + p)[:, d, :], ALU.max))
                step(V.reciprocal(den, den))
                hb = den.unsqueeze(2).broadcast_to([P, HEADS, P])
                dst = h3(hN[:, lc * 512:(lc + 1) * 512])
                if p == 0:
                    step(V.tensor_tensor(dst, t1[:, :, 0:P], hb, ALU.mult))
                else:
                    step(V.tensor_tensor(t1[:, :, 0:P], t1[:, :, 0:P], hb, ALU.mult))
                    step(V.tensor_tensor(dst, dst, t1[:, :, 0:P], ALU.add))
            sqh = at(big, 14416, 1024)
            h8 = lambda t: t.rearrange("p (h s) -> p h s", s=P)
            rs8 = small[:, 512:520]
            step(V.tensor_tensor(sqh, hN, hN, ALU.mult))
            step(V.tensor_reduce(rs8, h8(sqh), X, ALU.add))
            step(V.tensor_scalar(rs8, rs8, 1.0 / P, EPS, ALU.mult, ALU.add))
            V.reciprocal(rs8, rs8).then_inc(hms_ready, 1)
            sqk = at(big, 16464, 1536)
            rq = small[:, 520:544]
            step(V.tensor_tensor(sqk[:, 0:1024], aqN, aqN, ALU.mult))
            step(V.tensor_tensor(sqk[:, 1024:1536], akN, akN, ALU.mult))
            step(V.tensor_reduce(rq, sqk.rearrange("p (h s) -> p h s", s=DH), X, ALU.add))
            step(V.tensor_scalar(rq, rq, 1.0 / DH, EPS, ALU.mult, ALU.add))
            V.reciprocal(rq, rq).then_inc(qkms_ready, 1)
            dve.wait_ge(hrstd_ready, 1)
            step(V.tensor_tensor(h8(hN), h8(hN), rs8.unsqueeze(2).broadcast_to([P, 8, P]), ALU.mult))
            h2 = lambda t: t.rearrange("p (t f) -> p t f", t=NT)
            step(V.tensor_tensor(h2(hN), h2(hN), rowv("g_mlstm").unsqueeze(1).broadcast_to([P, NT, 512]), ALU.mult))
            dve.wait_ge(bank_emptied, 18)
            V.tensor_tensor(hN, hN, sigO, ALU.mult).then_inc(m_ready, 1)
            dve.wait_ge(qkrstd_ready, 1)
            d64 = lambda t: t.rearrange("p (h s) -> p h s", s=DH)
            for t, nh, r, g in ((aqN, 16, rq[:, 0:16], "g_q"), (akN, 8, rq[:, 16:24], "g_k")):
                step(V.tensor_tensor(d64(t), d64(t), r.unsqueeze(2).broadcast_to([P, nh, DH]), ALU.mult))
                step(V.tensor_tensor(d64(t), d64(t), rowv(g).unsqueeze(1).broadcast_to([P, nh, DH]), ALU.mult))
            step(V.tensor_copy(kR[:, 0:256], akN[:, 0:256]))
            for src, dst, nh in ((aqN, qR, AH), (akN[:, 256:512], kR[:, 256:512], 2)):
                s4 = src.rearrange("p (t h s) -> p t h s", t=NT, s=DH)
                o4 = dst.rearrange("p (t h s) -> p t h s", t=NT, s=DH)
                u4 = sqk[:, 0:NT * nh * 32].rearrange("p (t h s) -> p t h s", t=NT, s=32)
                cs, sn = (const(x).rearrange("p (t s) -> p t s", t=NT).unsqueeze(2).broadcast_to([P, NT, nh, 32])
                          for x in ("cos", "sin"))
                lo, hi = slice(0, 32), slice(32, 64)
                for a, b, op in ((lo, hi, ALU.subtract), (hi, lo, ALU.add)):
                    V.tensor_tensor(o4[:, :, :, a], s4[:, :, :, a], cs, ALU.mult)
                    step(V.tensor_tensor(u4, s4[:, :, :, b], sn, ALU.mult))
                    step(V.tensor_tensor(o4[:, :, :, a], o4[:, :, :, a], u4, op))
            k4 = kR.rearrange("p (c h s) -> p c h s", c=4, h=2)
            w4 = kSw.rearrange("p (c h s) -> p c h s", c=4, h=2)
            V.tensor_copy(w4[:, :, 0, :], k4[:, :, 1, :])
            V.tensor_copy(w4[:, :, 1, :], k4[:, :, 0, :]).then_inc(roped, 1)

            def attention(blk, dst):
                first = blk * UNITS

                def logits(u):
                    b, h = (u - first) // AH, u % AH
                    st = stat[:, 4 * u:4 * u + 4]
                    dve.wait_ge(scaled, u + 1)
                    if blk == 0:
                        bias = const("window")[:, b * T:(b + 1) * T]
                    else:
                        bias = bias2[:, h * 384 + (2 - 2 * b) * 64:h * 384 + (2 - 2 * b) * 64 + T]
                    step(V.tensor_tensor(logit[u % 2][:, 0:T], logit[u % 2][:, 0:T], bias, ALU.add))
                    step(V.tensor_reduce(st[:, 3:4], logit[u % 2], X, ALU.max))
                    if blk == 0:
                        V.tensor_scalar(st[:, 0:1], st[:, 3:4], rowv("sink")[:, h:h + 1], -1.0, ALU.max,
                                        ALU.mult).then_inc(logits_ready, 1)
                    else:
                        V.tensor_scalar(st[:, 0:1], st[:, 3:4], -1.0, None, ALU.mult).then_inc(logits_ready, 1)

                def finish(u):
                    b, h = (u - first) // AH, u % AH
                    st = stat[:, 4 * u:4 * u + 4]
                    dve.wait_ge(probsT_filled, u + 1)
                    if u >= 2:
                        dve.wait_ge(head_filled, u - 1)
                    V.tensor_copy(probsT[u % 2], bank(2 + u % 2)).then_inc(probsT_stored, 1)
                    if blk == 0:
                        dve.wait_ge(sink_ready, u + 1)
                        step(V.tensor_tensor(st[:, 1:2], st[:, 1:2], st[:, 2:3], ALU.add))
                    step(V.reciprocal(st[:, 1:2], st[:, 1:2]))
                    dve.wait_ge(head_filled, u + 1)
                    V.tensor_scalar(dst[:, b * 512 + h * DH:b * 512 + (h + 1) * DH], bank(4 + u % 2, DH), st[:, 1:2],
                                    None, ALU.mult).then_inc(head_stored, 1)

                logits(first)
                for u in range(first, first + UNITS):
                    if u + 1 < first + UNITS:
                        logits(u + 1)
                    finish(u)

            attention(0, aN)
            dve.wait_ge(branch_filled, 2)
            dve.wait_ge(bank_emptied, UNITS_B1)
            for b in range(4):
                o = b * 512
                V.tensor_tensor(tmpm[0], bank(b), sigG[:, o:o + 512], ALU.mult)
                step(V.tensor_tensor(tmpm[1], bank(4 + b), sigG[:, 2048 + o:2048 + o + 512], ALU.mult))
                V.tensor_tensor(merged[:, o:o + 512], tmpm[0], tmpm[1], ALU.add).then_inc(merged_ready, 1)
                dve.wait_ge(merged_ready, b + 1)

            def residual(block_, part, base, src=0):
                for j in range(KD):
                    if src == 0:
                        dve.wait_ge(y_filled, base + 1 + j // 4)
                    x = xT[:, j * T:(j + 1) * T]
                    V.scalar_tensor_tensor(out=x, in0=bank(src + j // 2, T, (j % 2) * T), scalar=modc(block_, part, j),
                                           in1=x, op0=ALU.mult, op1=ALU.add).then_inc(x_updated, 1)

            residual(0, 2, 0)
            dve.wait_ge(x_updated, KD)
            squares(2, xT)
            norm(2, xT, hT, colv("g_ffn"), modp(0, 4))

            V.memset(cst[:, CONSTS["window"][0]:CONSTS["window"][0] + 512], 0.0).then_inc(zeros_ready, 1)

            def top16(src, val, idx):
                step(V.max(val[:, 0:8], src))
                step(V.max_index(idx[:, 0:8], val[:, 0:8], src))
                step(V.match_replace(src, val[:, 0:8], src, BIG_NEG))
                step(V.max(val[:, 8:16], src))
                step(V.max_index(idx[:, 8:16], val[:, 8:16], src))

            s3 = top1.rearrange("p (h q a) -> p h q a", h=RH, q=2)
            i3 = idx1f.rearrange("p (h q a) -> p h q a", h=RH, q=2)
            big3 = lambda t: t.rearrange("p (h a b) -> p h a b", h=RH, a=TOPK)
            shape = [P, RH, TOPK, TOPK]
            for t in range(NT):
                dve.wait_ge(rscores_stored, 4 * (t + 1))
                for hp in range(2 * RH):
                    top16(sc[t][:, hp * P:(hp + 1) * P], top1[:, hp * TOPK:(hp + 1) * TOPK],
                          idx1[:, hp * TOPK:(hp + 1) * TOPK])
                step(V.tensor_copy(idx1f, idx1))
                step(V.tensor_tensor(big3(cand), s3[:, :, 0, :].unsqueeze(3).broadcast_to(shape),
                                     s3[:, :, 1, :].unsqueeze(2).broadcast_to(shape), ALU.add))
                for h in range(RH):
                    top16(cand[:, h * 256:(h + 1) * 256], top2[:, h * TOPK:(h + 1) * TOPK],
                          pos[:, h * TOPK:(h + 1) * TOPK])
                tv = top2.rearrange("p (h k) -> p h k", h=RH)
                if t:
                    dve.wait_ge(choiceT_filled, 3 * t)
                cv = choice[2].rearrange("p (h k) -> p h k", h=RH)
                V.tensor_tensor(cv, tv, tv[:, :, 0:1].broadcast_to([P, RH, TOPK]), ALU.subtract).then_inc(top_ready, 1)
                step(V.tensor_scalar(posa, pos, 4, None, ALU.logical_shift_right))
                step(V.tensor_scalar(posb, pos, 15, None, ALU.bitwise_and))
                step(V.tensor_copy(posaf, posa))
                step(V.tensor_copy(posbf, posb))
                i16 = iota[:, 0:TOPK].unsqueeze(1).broadcast_to([P, RH * TOPK, TOPK])
                for q, pf in ((0, posaf), (1, posbf)):
                    step(V.tensor_tensor(tmpr.rearrange("p (n a) -> p n a", a=TOPK),
                                         pf.unsqueeze(2).broadcast_to([P, RH * TOPK, TOPK]), i16, ALU.is_equal))
                    step(V.tensor_tensor(big3(tmpr), big3(tmpr), i3[:, :, q, :].unsqueeze(2).broadcast_to(shape), ALU.mult))
                    step(V.tensor_reduce(choice[q], tmpr.rearrange("p (n a) -> p n a", a=TOPK), X, ALU.add))
                dve.wait_ge(texp_ready, t + 1)
                step(V.tensor_reduce(zsum[:, 0:RH], cv, X, ALU.add))
                step(V.reciprocal(zsum[:, 0:RH], zsum[:, 0:RH]))
                V.tensor_tensor(cv, cv, zsum[:, 0:RH].unsqueeze(2).broadcast_to([P, RH, TOPK]),
                                ALU.mult).then_inc(choice_ready, 1)
                dve.wait_ge(choice_ready, t + 1)

            dve.wait_ge(pick_ready, 6)
            groups = T // GROUP
            for half in range(2):
                def one_hots(g, s, half=half):
                    n = g * 2 + (half * groups + s)
                    if not (isinstance(g, int) and half == 0):
                        dve.wait_ge(gate_filled, n - 1)
                    o = g * (2 * GROUP) + s * GROUP
                    V.tensor_tensor(oh1[s].rearrange("p (m e) -> p m e", m=GROUP),
                                    iota[:, half * HALF_E1:(half + 1) * HALF_E1].unsqueeze(1)
                                    .broadcast_to([P, GROUP, HALF_E1]),
                                    pick[:, bass.ds(o, GROUP)].unsqueeze(2).broadcast_to([P, GROUP, HALF_E1]),
                                    ALU.is_equal).then_inc(oh1_ready, 1)
                    V.tensor_tensor(oh2[s].rearrange("p (m e) -> p m e", m=GROUP),
                                    iota.unsqueeze(1).broadcast_to([P, GROUP, P]),
                                    pick[:, bass.ds(o + T, GROUP)].unsqueeze(2).broadcast_to([P, GROUP, P]),
                                    ALU.is_equal).then_inc(oh2_ready, 1)

                for s in range(2):
                    one_hots(0, s)
                with dve.Fori(1, groups // 2) as g:
                    for s in range(2):
                        one_hots(g, s)
                dve.wait_ge(gate_stored, (half + 1) * groups)
                base = half * 2 * HALF_SLABS
                with dve.Fori(0, HALF_SLABS // 4) as i:
                    for s in range(8):
                        dve.wait_ge(gelu_ready, i * 8 + (base + s + 1))
                        w = gate[:, bass.ds(i * (16 * T) + s * 512, 512)]
                        V.tensor_tensor(w, w, gel[s % 2], ALU.mult).then_inc(weight_ready, 1)
            dve.wait_ge(peer_half, 2)
            residual(0, 5, 0, src=4)
            dve.wait_ge(x_updated, 2 * KD)

            dve.wait_ge(ctx2_loaded, 16)
            squares(3, hcT)
            squares(4, xT)
            norm(3, hcT, hcT, colv("g1"), modp(1, 1, 1))
            dve.wait_ge(norm_scaled, 4 * KD)
            norm(4, xT, hT, colv("g1"), modp(1, 1, 0))
            dve.wait_ge(small2_loaded, 48)
            b3 = bias2.rearrange("p (n k) -> p n k", k=64)
            step(V.tensor_tensor(b3, b3, const("near").unsqueeze(1).broadcast_to([P, 48, 64]), ALU.add))
            dve.wait_ge(bank_emptied, UNITS_B1 + UNITS_Q + UNITS_B2)
            cv2 = lambda t: t.rearrange("p (j t) -> p j t", j=2)
            step(V.tensor_tensor(ucv, gbc[:, 512:1024], hcv, ALU.mult))
            wc = colv("w_conv")
            for j in range(2):
                u, v = cv2(ucv)[:, j, :], cv2(vcv)[:, j, :]
                step(V.tensor_scalar(v, u, wc[:, 3 * j + 1:3 * j + 2], None, ALU.mult))
                step(V.scalar_tensor_tensor(out=v[:, 1:T], in0=u[:, 0:T - 1], scalar=wc[:, 3 * j:3 * j + 1],
                                            in1=v[:, 1:T], op0=ALU.mult, op1=ALU.add))
                step(V.scalar_tensor_tensor(out=v[:, 0:T - 1], in0=u[:, 1:T], scalar=wc[:, 3 * j + 2:3 * j + 3],
                                            in1=v[:, 0:T - 1], op0=ALU.mult, op1=ALU.add))
            V.tensor_tensor(catT[:, 1536:2048], gbc[:, 0:512], vcv, ALU.mult).then_inc(conv_ready, 1)
            attention(1, aN2)
            residual(1, 2, 2)
            dve.wait_ge(x_updated, 3 * KD)
            squares(5, xT)
            norm(5, xT, hT, colv("g2"), modp(1, 4))

            nr = NG + NE
            V.memset(lgp, BIG_NEG)
            for t in range(NT):
                dve.wait_ge(router_filled, t + 1)
                step(V.tensor_tensor(lg[:, 0:nr], bank(t, nr), rowv("b_router"), ALU.add))
                step(V.tensor_copy(lgp[:, 0:NG], lg[:, 0:NG]))
                step(V.max(m8, lgp))
                step(V.max_index(i8, m8, lgp))
                step(V.tensor_copy(gidx, i8[:, 0:1]))
                step(V.tensor_scalar(goh, iota[:, 0:NG], gidx, None, ALU.is_equal))
                V.tensor_scalar(gex, lg[:, 0:NG], m8[:, 0:1], None, ALU.subtract).then_inc(rexp_in, 1)
                el = lg[:, NG:nr].rearrange("p (g e) -> p g e", g=NG)
                es = esel4.rearrange("p (g e) -> p g e", g=NG)
                step(V.tensor_tensor(es, el, goh.unsqueeze(2).broadcast_to([P, NG, EPG]), ALU.mult))
                step(V.tensor_reduce(esel, esel4.rearrange("p (g e) -> p e g", g=NG), X, ALU.add))
                step(V.max(e8, esel))
                step(V.max_index(j8, e8, esel))
                step(V.tensor_copy(j8f, j8))
                V.tensor_scalar(pw[:, 0:2], e8[:, 0:2], e8[:, 0:1], None, ALU.subtract).then_inc(rexp_in, 1)
                dve.wait_ge(rexp_out, 2 * t + 2)
                step(V.tensor_tensor(pw[:, 2:3], pw[:, 2:3], gz, ALU.mult))
                step(V.reciprocal(pw[:, 2:3], pw[:, 2:3]))
                step(V.tensor_scalar(pw[:, 0:2], pw[:, 0:2], pw[:, 2:3], None, ALU.mult))
                for q in range(2):
                    step(V.tensor_scalar(c8[:, 8 * q:8 * q + 8], iota[:, 0:EPG], j8f[:, q:q + 1], pw[:, q:q + 1],
                                         ALU.is_equal, ALU.mult))
                step(V.tensor_tensor(c8[:, 0:8], c8[:, 0:8], c8[:, 8:16], ALU.add))
                step(V.tensor_tensor(comb32[:, t * NE:(t + 1) * NE].rearrange("p (g e) -> p g e", g=NG),
                                     goh.unsqueeze(2).broadcast_to([P, NG, EPG]),
                                     c8[:, 0:8].unsqueeze(1).broadcast_to([P, NG, EPG]), ALU.mult))
            for n in range(2 * NE // 4):
                if n >= 2:
                    dve.wait_ge(comb_filled, n - 1)
                V.tensor_tensor(diag[n % 2].rearrange("p (e m) -> p e m", e=4), ident.unsqueeze(1).broadcast_to([P, 4, P]),
                                comb32[:, 4 * n:4 * n + 4].unsqueeze(2).broadcast_to([P, 4, P]),
                                ALU.mult).then_inc(cdiag_ready, 1)
            dve.wait_ge(comb_stored, 2 * NE // 4)

            cview = comb.rearrange("p (e m) -> p e m", m=T)

            def hidden(e, par, first=False):
                if not first:
                    dve.wait_ge(down_done, e - 1)
                dve.wait_ge(silu_ready, e * 2 + 2)
                dve.wait_ge(up_filled, e * 4 + 4)
                hb = he[par]
                V.tensor_tensor(hb[:, 0:512], silg[:, 0:512], bank(2), ALU.mult)
                V.tensor_tensor(hb[:, 512:1024], silg[:, 512:1024], bank(3), ALU.mult).then_inc(hid_mul, 1)
                dve.wait_ge(hid_mul, e + 1)
                h4 = hb.rearrange("p (f m) -> p f m", m=T)
                V.tensor_tensor(h4, h4, cview[:, bass.ds(e, 1), :].broadcast_to([P, 4, T]), ALU.mult).then_inc(he_ready, 1)

            hidden(0, 0, True)
            hidden(1, 1, True)
            with dve.Fori(1, NE // 2) as i:
                for par in range(2):
                    hidden(i * 2 + par, par)
            dve.wait_ge(down_done, NE)
            residual(1, 5, 0, src=4)
            dve.wait_ge(x_updated, 4 * KD)
            squares(6, xT)
            norm(6, xT, yfin, colv("g_final"), None)


NORM_SCALED = [KD * i for i in range(6)] + [6 * KD]
NORM_DONE = [KD * i for i in range(7)]


def constants():
    f = np.float32
    c = np.zeros((P, N_CONST), f)

    def put(name, a):
        o, w = CONSTS[name]
        c[:, o:o + w] = np.asarray(a, f).reshape(P, w)

    p = np.arange(P)
    put("ident", np.eye(P))
    put("ones", np.ones((P, P)))
    put("tri0", p[:, None] <= p[None, :])
    put("tri1", p[:, None] >= p[None, :])
    put("seen0", np.where(p[None, :] <= p[:, None], 0.0, NEG))
    put("seen1", np.where(p[None, :] >= p[:, None], 0.0, NEG))
    q = p[:, None] + P * np.arange(NT)[None, :]
    k = np.arange(T)
    put("window", np.where(np.abs(k[None, None, :] - q[:, :, None]) <= P, 0.0, NEG))
    qc, kc = p[:, None] % 64, np.arange(64)[None, :]
    first = np.clip(qc - 8, 0, 48)
    put("near", np.where((kc >= first) & (kc < first + 16), 0.0, NEG))
    tok = q
    inv = (10000.0 ** (-np.arange(16, dtype=f) / f(16))).astype(f)
    r = (tok // 64)[:, :, None].astype(f) * inv
    w = (tok % 64)[:, :, None].astype(f) * inv
    ang = np.concatenate([r, w], axis=-1)
    put("cos", np.cos(ang.astype(np.float64)))
    put("sin", np.sin(ang.astype(np.float64)))
    put("iota", np.broadcast_to(p[None, :], (P, P)))
    th = 2 * np.pi * (tok[:, :, None] * k[None, None, :] % T) / T
    put("dft_c", np.cos(th) / 16.0)
    put("dft_s", np.sin(th) / 16.0)
    j = np.arange(P)
    same = (j[:, None] // 64) == (j[None, :] // 64)
    th = 2 * np.pi * ((j[:, None] % 64) * (j[None, :] % 64) % 64) / 64
    put("dch_c", np.where(same, np.cos(th), 0) / 8.0)
    put("dch_s", np.where(same, -np.sin(th), 0) / 8.0)
    return c


def kernel(**inputs):
    import concourse.bacc as bacc
    from concourse.bass_utils import run_bass_kernel_spmd

    a = {k: np.asarray(v) for k, v in inputs.items()}

    def by_rows(w):
        return w.reshape(-1, P, w.shape[-1]).transpose(1, 0, 2)

    slabs = np.zeros((N_SLABS, P, SLAB), np.float32)

    def put(n, w):
        w = by_rows(w).reshape(P, -1)
        slabs[n, :, :w.shape[1]] = w

    for m, name in enumerate(("w_ada", "w_ada_2")):
        for s in range(ADA_SLABS):
            put(m * ADA_SLABS + s, a[name][0][:, s * 512:(s + 1) * 512])
    w = a["w_in"][0]
    put(S_Q, w[:, 0:512])
    put(S_K, w[:, 512:1024])
    put(S_V, w[:, 1024:1536])
    put(S_O, w[:, 1536:2048])
    put(S_GKV, np.concatenate([w[:, 2048:2064], w[:, 2576:2832]], axis=1))
    put(S_AQ, w[:, 2064:2576])
    for s in range(4):
        put(S_MG + s, w[:, 2832 + s * 512:2832 + (s + 1) * 512])
        put(S_QUERY + s, a["peer_w_query"][0][:, s * 512:(s + 1) * 512])
    put(S_BM, a["w_branch_m"][0])
    put(S_BA, a["w_branch_a"][0])
    for s in range(2):
        put(S_OUT + s, a["w_out"][0][:, s * 512:(s + 1) * 512])
        put(S_OUT2 + s, a["w_out_2"][0][:, s * 512:(s + 1) * 512])
    u = a["peer_u"][0].reshape(2 * HALF_SLABS, 512, KD, P).transpose(0, 3, 2, 1).reshape(2 * HALF_SLABS, P, SLAB)
    v = a["peer_v"][0].reshape(2 * HALF_SLABS, 4, P, D).transpose(0, 2, 1, 3).reshape(2 * HALF_SLABS, P, SLAB)
    for half in range(2):
        s0 = S_PEER + 2 * half * HALF_SLABS
        slabs[s0:s0 + HALF_SLABS] = u[half * HALF_SLABS:(half + 1) * HALF_SLABS]
        slabs[s0 + HALF_SLABS:s0 + 2 * HALF_SLABS] = v[half * HALF_SLABS:(half + 1) * HALF_SLABS]
    w = a["w_in_2"][0]
    put(S_Q2, w[:, 256:768])
    put(S_K2, w[:, 768:1280])
    put(S_V2, w[:, 1280:1792])
    put(S_FH2, np.concatenate([w[:, 0:256], w[:, 2304:2560]], axis=1))
    put(S_G2, w[:, 1792:2304])
    for e in range(NE):
        put(S_MOE if e == 0 else S_MOE + 3 * e - 1, a["w_gate_2"][0, e])
        put(S_MOE + 1 if e == 0 else S_MOE + 3 * e, a["w_up_2"][0, e])
        put(N_SLABS - 1 if e == NE - 1 else S_MOE + 4 + 3 * e, a["w_down_2"][0, e])

    def column(v):
        return v.reshape(-1, P).T

    def tokens(x):
        return x.T.reshape(KD, P, T).transpose(1, 0, 2).reshape(P, KD * T)

    cond = np.stack([column(a[n].reshape(-1)) for n in ("c", "c_ctx", "c_2", "c_ctx_2")], axis=2).reshape(P, -1)
    cols = np.concatenate(
        [column(a[n].reshape(-1)) for n in ("b_ada", "b_ada_2", "norm_mix_g", "norm_ffn_g", "norm1_2", "norm2_2",
                                            "norm_final_2")]
        + [a["w_conv_2"][0].reshape(3, 2, P).transpose(2, 1, 0).reshape(P, 6)], axis=1)
    rows = np.concatenate([a[n].reshape(-1) for n in ("b_mgates", "mlstm_norm_g", "attn_q_norm_g", "attn_k_norm_g",
                                                      "attn_sink", "b_rg_2", "b_re_2")])
    rows = np.broadcast_to(rows, (P, N_ROW))
    subk = a["peer_sub_keys"][0].transpose(3, 0, 1, 2).reshape(P, -1)
    r2 = a["rpb_2"][0]
    shift = np.clip(np.arange(64)[None, :] - np.arange(64)[:, None] + 15, 0, 30)
    toe = r2[:, :, shift].transpose(2, 0, 1, 3)
    rpb = np.concatenate([toe[:, :, 5:11], toe[:, :, 4:10]], axis=0).reshape(P, -1)
    wr = by_rows(np.concatenate([a["w_rg_2"][0], a["w_re_2"][0]], axis=1)).reshape(P, -1)
    arrays = {
        "w_stream": slabs, "cond": cond, "x_t": tokens(a["x"][0]), "ctx_t": tokens(a["ctx"][0]),
        "ctx2_t": tokens(a["ctx_2"][0]), "consts": constants(), "cols": cols, "rows": rows, "sub_keys": subk,
        "rpb": rpb, "w_four": by_rows(a["w_fourier_2"][0]).reshape(P, -1), "w_router": wr,
    }
    arrays = {k: np.ascontiguousarray(v) for k, v in arrays.items()}
    nc = bacc.Bacc("TRN2", target_bir_lowering=False, num_devices=1)
    args = [nc.dram_tensor(k, v.shape, mybir.dt.from_np(v.dtype), kind="ExternalInput").ap() for k, v in arrays.items()]
    args.append(nc.dram_tensor("out", (P, KD * T), F32, kind="ExternalOutput").ap())
    two_block_kernel(nc, *args)
    r = run_bass_kernel_spmd(nc, [arrays], core_ids=[0])
    y = r.results[0]["out"]
    return np.ascontiguousarray(y.reshape(P, KD, T).transpose(2, 1, 0).reshape(1, T, D))
```

```python
from contextlib import ExitStack

import numpy as np

import concourse.bass as bass
from concourse import mybir

F32 = mybir.dt.float32
F32R = mybir.dt.float32r
U32 = mybir.dt.uint32
ALU = mybir.AluOpType
ACT = mybir.ActivationFunctionType
X = mybir.AxisListType.X

P = 128
D = 1024
KD = D // P
T = 256
NT = T // P
EPS = 1e-6
NEG = -1e30
BIG_NEG = -3.0e38
SLAB = 4096
SLOTS = 4

HEADS = 4
KEY_SCALE = float(P) ** -0.5
AH = 8
DH = 64
ATT_SCALE = float(DH) ** -0.5
UNITS = NT * AH

RH = 8
TOPK = 16
NKEY = 128
HALF_E1 = NKEY // 2
GROUP = 8

NG = 4
EPG = 8
NE = NG * EPG
QUAD = 4
ROOM = 32
QUADS = NE // QUAD
MAX_ROUNDS = T // ROOM
Q_SLABS = 12

ADA_SLABS = 6 * D // 512
ADA_FIRST = 4
S_ADA = 0
S_K, S_V, S_GKV, S_Q, S_AQ, S_O, S_MG = (ADA_FIRST + i for i in range(7))
S_ADA2 = S_MG + 4
S_BM = S_ADA2 + 2 * ADA_SLABS - ADA_FIRST
S_BA = S_BM + 1
S_OUT = S_BA + 1
S_QUERY = S_OUT + 2
S_PEER = S_QUERY + 4
HALF_SLABS = HALF_E1 // 4
S_K2 = S_PEER + 4 * HALF_SLABS
S_V2, S_Q2, S_FH2, S_G2 = (S_K2 + i for i in range(1, 5))
S_OUT2 = S_G2 + 1
S_MOE = S_OUT2 + 2
N_SLABS = S_MOE + QUADS * Q_SLABS

CONSTS = {}
_n = 0
for _name, _w in (("ident", P), ("ones", P), ("tri0", P), ("tri1", P), ("seen0", P), ("seen1", P),
                  ("window", NT * T), ("near", DH), ("cos", NT * 32), ("sin", NT * 32), ("iota", P),
                  ("dft_c", NT * T), ("dft_s", NT * T), ("dch_c", P), ("dch_s", P), ("pairs", 2)):
    CONSTS[_name] = (_n, _w)
    _n += _w
N_CONST = _n

COLS = {}
_n = 0
for _name, _w in (("b_ada", 2 * 6 * KD), ("g_mix", KD), ("g_ffn", KD), ("g1", KD), ("g2", KD),
                  ("g_final", KD), ("w_conv", 6)):
    COLS[_name] = (_n, _w)
    _n += _w
N_COL = _n
ROWS = {}
_n = 0
for _name, _w in (("b_gates", 16), ("g_mlstm", 512), ("g_q", DH), ("g_k", DH), ("sink", AH),
                  ("b_router", NG + NE)):
    ROWS[_name] = (_n, _w)
    _n += _w
N_ROW = _n


def ada_slab(n):
    return S_ADA + n if n < ADA_FIRST else S_ADA2 + n - ADA_FIRST


def two_block_kernel(nc, w_stream, cond, x_t, ctx_t, ctx2_t, consts, cols, rows, sub_keys, rpb,
                     w_four, w_router, out):
    with ExitStack() as ctx:
        def sb(name, n, dt=F32):
            return ctx.enter_context(nc.sbuf_tensor(name, [P, n], dt))

        def sem(name):
            return ctx.enter_context(nc.semaphore(name))

        def placed(name, n, dt=F32):
            o = -(-nc.sbuf_base // 32) * 32
            return sb(name, n, dt), o

        def over(name, n, offset):
            return nc.alloc_sbuf_tensor_at(name, [P, n], F32R, offset=offset)

        slab, slab_lo = [], []
        for i in range(SLOTS):
            t, o = placed(f"slab{i}", SLAB)
            slab.append(t)
            slab_lo.append(over(f"slab_lo{i}", SLAB, o))
        big, o_big = placed("big", 20080)
        scratch = sb("scratch", 4096)
        xT = sb("xT", KD * T)
        hT, o_hT = placed("hT", KD * T)
        hcT, o_hcT = placed("hcT", KD * T)
        cst = sb("cst", N_CONST)
        col = sb("col", N_COL)
        row = sb("row", N_ROW)
        conds = sb("conds", KD * 2 * ROOM)
        mod = sb("mod", 2 * 6 * KD * 2)
        gain = sb("gain", KD)
        rstd = sb("rstd", T)
        stat = sb("stat", 4 * 2 * UNITS)
        small = sb("small", 640)
        pick = sb("pick", 3 * T)
        ps = ctx.enter_context(nc.psum_tensor("ps", [P, 8 * 512], F32))

        def bank(b, n=512, at=0):
            return ps[:, b * 512 + at:b * 512 + at + n]

        def const(name):
            o, w = CONSTS[name]
            return cst[:, o:o + w]

        def colv(name):
            o, w = COLS[name]
            return col[:, o:o + w]

        def rowv(name):
            o, w = ROWS[name]
            return row[:, o:o + w]

        def at(t, o, n):
            return t[:, o:o + n]

        ident, ones, iota = const("ident"), const("ones"), const("iota")

        def modc(block, part, j, who=0):
            c = ((block * 6 + part) * KD + j) * 2 + who
            return mod[:, c:c + 1]

        def modp(block, part, who=0):
            c = (block * 6 + part) * KD * 2 + who
            return mod[:, c:c + 2 * KD - 1:2]

        qT = at(big, 0, 1024)
        kN = at(big, 1024, 2048)
        kTl = at(big, 3072, 1024)
        vA = at(big, 4096, 4 * HEADS * 129).rearrange("p (c h v) -> p c h v", c=4, h=HEADS)
        sigO = at(big, 6160, 1024)
        gat = at(big, 7184, 64)
        aqN = at(big, 7248, 1024)
        akN = at(big, 8272, 512)
        avN = at(big, 8784, 512)
        qR = at(big, 9296, 1024)
        kR = at(big, 10320, 512)
        kSw = at(big, 10832, 512)
        qTa = at(big, 11344, 1024)
        kTa = at(big, 12368, 1024)
        hN = at(big, 13392, 1024)
        pair = [at(big, 14416, 512), at(big, 14928, 512)]
        state = [[at(big, 15440 + (2 * v + d) * 516, 516).rearrange("p (h v) -> p h v", h=HEADS)
                  for d in range(2)] for v in range(2)]
        t1 = at(big, 17504, 516).rearrange("p (h v) -> p h v", h=HEADS)
        t2 = at(big, 18020, 516).rearrange("p (h v) -> p h v", h=HEADS)
        probsT = [at(big, 19052, 512), at(big, 19564, 512)]
        decay = hcT
        logit = [at(hT, 0, 512), at(hT, 512, 512)]
        probs = [at(hT, 1024, 512), at(hT, 1536, 512)]
        aN = at(big, 0, 1024)
        mT = at(big, 1024, 1024)
        aT = at(big, 2048, 1024)
        merged = at(big, 3072, 2048)
        tmpm = [at(big, 5120, 512), at(big, 5632, 512)]
        sigG = scratch
        qTr = at(big, 0, 4096)
        subk = at(big, 4096, 2048)
        sc = [at(scratch, 0, 2048), at(scratch, 2048, 2048)]
        R0 = HALF_E1 * T + 2048
        top1 = at(big, R0, 256)
        idx1 = at(big, R0 + 256, 256)
        top2 = at(big, R0 + 512, 128)
        pos = at(big, R0 + 640, 128)
        posa = at(big, R0 + 768, 128)
        choice = [at(conds, 0, 384), at(small, 0, 384)]
        zsum = at(conds, 384, 16)
        gate = at(big, 0, HALF_E1 * T)
        CHUNK = 1024
        h_hi = over("h_hi", KD * T, o_hcT)
        h_lo = over("h_lo", KD * T, o_hT)
        w_hi = [over(f"w_hi{i}", CHUNK, o_big + 4 * (16384 + i * CHUNK)) for i in range(2)]
        g_hi = [over(f"g_hi{i}", T, o_big + 4 * (18432 + i * T)) for i in range(2)]
        g_lo = [over(f"g_lo{i}", T, o_big + 4 * (18944 + i * T)) for i in range(2)]
        oh2 = [at(scratch, 0, 1024), at(scratch, 1024, 1024)]
        oh1 = [at(scratch, 2048, 512), at(scratch, 2560, 512)]
        kT2 = at(big, 0, 2048)
        vN2 = at(big, 2048, 2048)
        qT2 = at(big, 4096, 1024)
        fN = at(big, 5120, 512)
        hcv = at(big, 5632, 512)
        gbc = at(big, 6144, 1024)
        tCS = at(big, 7168, 1024)
        foT = at(big, 8192, 512)
        catT = at(big, 8704, 2048)
        aN2 = at(big, 10752, 1024)
        ucv = at(big, 11776, 512)
        vcv = at(big, 12288, 512)
        bias2 = at(big, 12800, 3072)
        wf = at(big, 15872, 512)
        wr = at(big, 16384, KD * (NG + NE))
        xN = at(big, 0, NT * D)
        sel = at(big, 2048, 256)
        selw = at(big, 2304, 256)
        selT = at(big, 2560, 256)
        xg = at(big, 2816, 1024)
        silg = at(big, 3840, 512)
        he = at(big, 4352, 512)
        heT = at(big, 4864, 512)
        ye = at(big, 5376, 1024)
        yfin = at(big, 0, 2048)
        M0 = 13312
        lg = at(big, M0, 40)
        lgp = at(big, M0 + 40, 8)
        m8 = at(big, M0 + 48, 8)
        i8 = at(big, M0 + 56, 8).bitcast(U32)
        gidx = at(big, M0 + 64, 1)
        goh = at(big, M0 + 68, 4)
        gex = at(big, M0 + 76, 4)
        gz = at(big, M0 + 80, 1)
        esel = at(big, M0 + 88, 8)
        esel4 = at(big, M0 + 96, 32)
        e8 = at(big, M0 + 128, 8)
        j8 = at(big, M0 + 136, 8).bitcast(U32)
        j8f = at(big, M0 + 144, 8)
        pw = at(big, M0 + 152, 4)
        s8 = at(big, M0 + 160, 16)
        c8 = at(big, M0 + 176, 16)
        comb32 = at(big, M0 + 192, 64)
        sel32 = at(big, M0 + 256, 64)
        place = at(big, M0 + 320, 64)
        most = at(big, M0 + 384, 1)
        roundf = at(big, M0 + 392, 8)
        rounds = at(big, M0 + 400, 2).bitcast(U32)
        slab_loaded = [sem(f"slab_loaded{i}") for i in range(SLOTS)]
        slab_used = sem("slab_used")
        cond_loaded = sem("cond_loaded")
        inputs_loaded = sem("inputs_loaded")
        subk_loaded = sem("subk_loaded")
        ctx2_loaded = sem("ctx2_loaded")
        small2_loaded = sem("small2_loaded")
        out_stored = sem("out_stored")
        cond_ready = sem("cond_ready")
        mod_filled = sem("mod_filled")
        mod_stored = sem("mod_stored")
        norm_sq = sem("norm_sq")
        norm_sum = sem("norm_sum")
        norm_inv = sem("norm_inv")
        norm_rstd = sem("norm_rstd")
        norm_scaled = sem("norm_scaled")
        norm_done = sem("norm_done")
        bank_filled = sem("bank_filled")
        bank_emptied = sem("bank_emptied")
        gates_biased = sem("gates_biased")
        soft_ready = sem("soft_ready")
        lf_ready = sem("lf_ready")
        cums_filled = sem("cums_filled")
        diag_ready = sem("diag_ready")
        rrow_filled = sem("rrow_filled")
        rrow_used = sem("rrow_used")
        exps_in = sem("exps_in")
        exps_out = sem("exps_out")
        kw_ready = sem("kw_ready")
        cloc_filled = sem("cloc_filled")
        cloc_used = sem("cloc_used")
        kT_filled = sem("kT_filled")
        kT_stored = sem("kT_stored")
        qk_filled = sem("qk_filled")
        decay_in = sem("decay_in")
        decay_out = sem("decay_out")
        smat_ready = sem("smat_ready")
        smatT_filled = sem("smatT_filled")
        smatT_stored = sem("smatT_stored")
        num_filled = sem("num_filled")
        num_used = sem("num_used")
        hms_ready = sem("hms_ready")
        hrstd_ready = sem("hrstd_ready")
        m_ready = sem("m_ready")
        turn_filled = sem("turn_filled")
        turn_stored = sem("turn_stored")
        qkms_ready = sem("qkms_ready")
        qkrstd_ready = sem("qkrstd_ready")
        roped = sem("roped")
        scores_filled = sem("scores_filled")
        scaled = sem("scaled")
        logits_ready = sem("logits_ready")
        probs_ready = sem("probs_ready")
        sink_ready = sem("sink_ready")
        probsT_filled = sem("probsT_filled")
        probsT_stored = sem("probsT_stored")
        head_filled = sem("head_filled")
        head_stored = sem("head_stored")
        branch_filled = sem("branch_filled")
        merged_ready = sem("merged_ready")
        y_filled = sem("y_filled")
        x_updated = sem("x_updated")
        rscores_filled = sem("rscores_filled")
        rscores_stored = sem("rscores_stored")
        top_ready = sem("top_ready")
        texp_ready = sem("texp_ready")
        choice_ready = sem("choice_ready")
        choiceT_filled = sem("choiceT_filled")
        pick_ready = sem("pick_ready")
        oh1_ready = sem("oh1_ready")
        oh2_ready = sem("oh2_ready")
        ohw_ready = sem("ohw_ready")
        gate_filled = sem("gate_filled")
        gate_stored = sem("gate_stored")
        h_hi_ready = sem("h_hi_ready")
        h_lo_ready = sem("h_lo_ready")
        hi_ready = sem("hi_ready")
        lo_ready = sem("lo_ready")
        ghi_ready = sem("ghi_ready")
        glo_ready = sem("glo_ready")
        chunk_used = sem("chunk_used")
        gelu_ready = sem("gelu_ready")
        weight_ready = sem("weight_ready")
        peer_half = sem("peer_half")
        conv_ready = sem("conv_ready")
        four_filled = sem("four_filled")
        four_stored = sem("four_stored")
        router_filled = sem("router_filled")
        rexp_in = sem("rexp_in")
        rexp_out = sem("rexp_out")
        adarow_filled = sem("adarow_filled")
        adarow_stored = sem("adarow_stored")
        counts_filled = sem("counts_filled")
        sel32_ready = sem("sel32_ready")
        rounds_ready = sem("rounds_ready")
        sel_ready = sem("sel_ready")
        gathered = sem("gathered")
        xg_low = sem("xg_low")
        xg_high = sem("xg_high")
        hidden_filled = sem("hidden_filled")
        silu_ready = sem("silu_ready")
        he_ready = sem("he_ready")
        heT_filled = sem("heT_filled")
        heT_ready = sem("heT_ready")
        down_filled = sem("down_filled")
        ye_low = sem("ye_low")
        ye_high = sem("ye_high")
        scattered = sem("scattered")
        sel_made = sem("sel_made")
        place_moved = sem("place_moved")
        experts_done = sem("experts_done")
        zeros_ready = sem("zeros_ready")
        dve_step = sem("dve_step")
        act_step = sem("act_step")
        pool_step = sem("pool_step")

        block = ctx.enter_context(nc.Block())

        CHUNKS = 4 * HALF_SLABS

        UNITS_B1 = 4 + 4 + 4 + 2 + 2 + 2 + 8
        UNITS_Q = 8
        UNITS_B2 = 14

        @block.sync
        def _(sp):
            def load(n, slot, value):
                if value is not None:
                    sp.wait_ge(slab_used, value)
                sp.dma_start(slab[slot][:, :], w_stream[n]).then_inc(slab_loaded[slot], 16)

            for s in range(SLOTS):
                load(s, s, None)
            whole = S_MOE // SLOTS
            with sp.Fori(1, whole) as i:
                for s in range(SLOTS):
                    load(i * SLOTS + s, s, i * SLOTS + (s - SLOTS + 1))
            for n in range(whole * SLOTS, S_MOE):
                load(n, n % SLOTS, n - SLOTS + 1)

            def expert_round(r):
                turns = QUADS * Q_SLABS // SLOTS
                with sp.Fori(0, turns) as i:
                    for s in range(SLOTS):
                        n = i * SLOTS + (S_MOE + s)
                        used_before = n - SLOTS + 1 + r * (turns * SLOTS)
                        load(n, (S_MOE + s) % SLOTS, used_before)

            expert_round(0)
            sp.wait_ge(rounds_ready, 1)
            n_rounds = sp.value_load(rounds[0:1, 0:1], min_val=1, max_val=MAX_ROUNDS)
            with sp.If(n_rounds > 1):
                with sp.Fori(1, n_rounds) as r:
                    expert_round(r)

        def low_part(engine, ops, q, i):
            n = S_PEER + q // 4
            o = (q % 4) * CHUNK
            engine.wait_ge(hi_ready, i * 16 + (q + 1))
            ops.tensor_tensor(slab_lo[n % SLOTS][:, o:o + CHUNK], slab[n % SLOTS][:, o:o + CHUNK],
                              w_hi[q % 2][:, :].bitcast(F32), ALU.subtract).then_inc(lo_ready, 1)

        @block.gpsimd
        def _(pool):
            with pool.Fori(0, CHUNKS // 16) as i:
                for j in range(16):
                    low_part(pool, nc.gpsimd, j, i)
            pool.wait_ge(pick_ready, NT)
            groups = T // GROUP
            for half in range(2):
                with pool.Fori(0, groups // 2) as g:
                    for s in range(2):
                        pool.wait_ge(oh1_ready, g * 2 + (half * groups + s + 1))
                        o1 = oh1[s].rearrange("p (m e) -> p m e", m=GROUP)
                        nc.gpsimd.tensor_tensor(
                            o1, o1, pick[:, bass.ds(g * (2 * GROUP) + (s * GROUP + 2 * T), GROUP)].unsqueeze(2)
                            .broadcast_to([P, GROUP, HALF_E1]), ALU.mult).then_inc(ohw_ready, 1)

        @block.scalar
        def _(act):
            steps = [0]

            def step(ins):
                steps[0] += 1
                ins.then_inc(act_step, 1)
                act.wait_ge(act_step, steps[0])

            act.dma_start(conds[:, :], cond).then_inc(cond_loaded, 16)
            for dst, src in ((cst, consts), (col, cols), (row, rows), (xT, x_t), (hcT, ctx_t)):
                act.dma_start(dst[:, :], src).then_inc(inputs_loaded, 16)
            act.wait_ge(cond_loaded, 16)
            nc.scalar.activation(conds[:, :], conds[:, :], ACT.Silu).then_inc(cond_ready, 1)

            def ada_row(n, buf):
                act.wait_ge(adarow_filled, n + 1)
                nc.scalar.activation(buf, bank(6), ACT.Copy).then_inc(adarow_stored, 1)

            for n in range(ADA_FIRST):
                ada_row(n, big[:, 0:512])

            def norm(i, dst, shift):
                act.wait_ge(norm_inv, i + 1)
                nc.scalar.activation(rstd[:, :], rstd[:, :], ACT.Sqrt).then_inc(norm_rstd, 1)
                if shift is not None:
                    for k in range(KD):
                        act.wait_ge(norm_scaled, NORM_SCALED[i] + k + 1)
                        nc.scalar.activation(dst[:, k * T:(k + 1) * T], dst[:, k * T:(k + 1) * T],
                                             ACT.Identity, bias=shift(k)).then_inc(norm_done, 1)

            unit = [0]

            def empty(dst, func=ACT.Copy, scale=1.0, src=None):
                u = unit[0]
                unit[0] += 1
                act.wait_ge(bank_filled, u + 1)
                nc.scalar.activation(dst, bank(u % 8) if src is None else src(u % 8), func,
                                     scale=scale).then_inc(bank_emptied, 1)

            norm(0, hT, lambda k: modc(0, 0, k, 0))
            norm(1, hcT, lambda k: modc(0, 0, k, 1))
            for c in range(4):
                empty(kN[:, c * 512:(c + 1) * 512], scale=KEY_SCALE)
            for c in range(4):
                empty(vA[:, c, :, 0:P], src=lambda b: bank(b).rearrange("p (h v) -> p h v", h=HEADS))
            for c in range(4):
                u = unit[0]
                unit[0] += 1
                act.wait_ge(bank_filled, u + 1)
                nc.scalar.activation(gat[:, c * 16:(c + 1) * 16], bank(u % 8, 16), ACT.Copy)
                nc.scalar.activation(akN[:, c * P:(c + 1) * P], bank(u % 8, P, 16), ACT.Copy)
                nc.scalar.activation(avN[:, c * P:(c + 1) * P], bank(u % 8, P, 16 + P),
                                     ACT.Copy).then_inc(bank_emptied, 1)
            for c in range(2):
                empty(qT[:, c * 512:(c + 1) * 512])
            for c in range(2):
                empty(aqN[:, c * 512:(c + 1) * 512])
            for c in range(2):
                empty(sigO[:, c * 512:(c + 1) * 512], ACT.Sigmoid)
            for c in range(8):
                empty(sigG[:, c * 512:(c + 1) * 512], ACT.Sigmoid)

            soft = small[:, 64:96]
            act.wait_ge(gates_biased, 1)
            step(nc.scalar.activation(soft, small[:, 32:64], ACT.Abs))
            step(nc.scalar.activation(soft, soft, ACT.Exp, scale=-1.0))
            nc.scalar.activation(soft, soft, ACT.Ln, bias=1.0).then_inc(soft_ready, 1)
            for c in range(2):
                act.wait_ge(kT_filled, c + 1)
                nc.scalar.activation(
                    kTl.rearrange("p (h t) -> p h t", h=HEADS)[:, :, c * P:(c + 1) * P],
                    bank(6 + c).rearrange("p (h t) -> p h t", h=HEADS), ACT.Copy).then_inc(kT_stored, 1)
            for n in range(ADA_FIRST, ADA_FIRST + 4):
                ada_row(n, probsT[0])
            act.wait_ge(exps_in, 1)
            nc.scalar.activation(small[:, 400:504], small[:, 296:400], ACT.Exp).then_inc(exps_out, 1)
            act.wait_ge(decay_in, 4)
            nc.scalar.activation(decay[:, :], decay[:, :], ACT.Exp).then_inc(decay_out, 1)
            for n in range(ADA_FIRST + 4, ADA_SLABS):
                ada_row(n, probsT[0])
            for n in range(4):
                act.wait_ge(smatT_filled, n + 1)
                if n >= 2:
                    act.wait_ge(num_filled, n - 1)
                else:
                    act.wait_ge(cloc_filled, 6)
                nc.scalar.activation(pair[n % 2], bank(1 + n % 2), ACT.Copy).then_inc(smatT_stored, 1)
            act.wait_ge(hms_ready, 1)
            nc.scalar.activation(small[:, 512:520], small[:, 512:520], ACT.Sqrt).then_inc(hrstd_ready, 1)
            act.wait_ge(qkms_ready, 1)
            nc.scalar.activation(small[:, 520:544], small[:, 520:544], ACT.Sqrt).then_inc(qkrstd_ready, 1)

            def turned(n, dst):
                act.wait_ge(turn_filled, n + 1)
                nc.scalar.activation(dst, bank(n % 8), ACT.Copy).then_inc(turn_stored, 1)

            for n in range(2):
                turned(n, qTa[:, n * 512:(n + 1) * 512])
            for n in range(2):
                turned(2 + n, kTa[:, n * 512:(n + 1) * 512])

            def attention(blk):
                def scale(u):
                    act.wait_ge(scores_filled, u + 1)
                    nc.scalar.activation(logit[u % 2], bank(u % 2), ACT.Copy,
                                         scale=ATT_SCALE).then_inc(scaled, 1)

                def softmax(u):
                    st = stat[:, 4 * u:4 * u + 4]
                    act.wait_ge(logits_ready, u + 1)
                    if u >= 2:
                        act.wait_ge(probsT_filled, u - 1)
                    nc.scalar.activation(probs[u % 2], logit[u % 2], ACT.Exp, bias=st[:, 0:1],
                                         accum_out=st[:, 1:2]).then_inc(probs_ready, 1)
                    if blk == 0:
                        h = u % AH
                        nc.scalar.activation(st[:, 2:3], rowv("sink")[:, h:h + 1], ACT.Exp,
                                             bias=st[:, 0:1]).then_inc(sink_ready, 1)

                first = blk * UNITS
                scale(first)
                scale(first + 1)
                for u in range(first, first + UNITS):
                    softmax(u)
                    if u + 2 < first + UNITS:
                        scale(u + 2)
                    if blk == 0 and u < ADA_SLABS:
                        ada_row(ADA_SLABS + u, hcT[:, 0:512])

            attention(0)
            for n in range(2):
                turned(4 + n, mT[:, n * 512:(n + 1) * 512])
            for n in range(2):
                turned(6 + n, aT[:, n * 512:(n + 1) * 512])
            act.wait_ge(y_filled, 2)
            act.dma_start(subk, sub_keys).then_inc(subk_loaded, 16)
            norm(2, hT, lambda k: modc(0, 3, k, 0))
            act.wait_ge(norm_done, 3 * KD)
            nc.scalar.activation(h_hi[:, :], hT[:, :], ACT.Copy).then_inc(h_hi_ready, 1)
            for c in range(8):
                empty(qTr[:, c * 512:(c + 1) * 512])
            for t in range(NT):
                for b in range(4):
                    act.wait_ge(rscores_filled, t * 4 + b + 1)
                    nc.scalar.activation(sc[t][:, b * 512:(b + 1) * 512], bank(4 * t + b),
                                         ACT.Copy).then_inc(rscores_stored, 1)
            def high(q, i=0):
                n = S_PEER + q // 4
                act.wait_ge(slab_loaded[n % SLOTS], i * 16 + 16 * (n // SLOTS + 1))
                if not (isinstance(i, int) and q < 2):
                    act.wait_ge(chunk_used, i * 16 + (q - 1))
                nc.scalar.activation(w_hi[q % 2][:, :], slab[n % SLOTS][:, (q % 4) * CHUNK:(q % 4 + 1) * CHUNK],
                                     ACT.Copy).then_inc(hi_ready, 1)

            def activations(half):
                q0 = 2 * half * CHUNKS

                def turn_(i):
                    for p in range(8):
                        high(q0 + 2 * p + 2, i)
                        high(q0 + 2 * p + 3, i)
                        act.wait_ge(chunk_used, i * 16 + (q0 + 2 * p + 2))
                        if half:
                            act.wait_ge(peer_half, half)
                        nc.scalar.activation(gate[:, bass.ds(i * (16 * T) + p * 512, 512)] if not isinstance(i, int)
                                             else gate[:, i * 16 * T + p * 512:i * 16 * T + (p + 1) * 512],
                                             bank(p % 4), ACT.Gelu_apprx_tanh).then_inc(gelu_ready, 1)

                if half == 0:
                    high(0)
                    high(1)
                with act.Fori(0, CHUNKS // 16) as i:
                    turn_(i)

            def weights_high(half):
                q0 = (2 * half + 1) * CHUNKS
                act.wait_ge(weight_ready, (half + 1) * (T // GROUP))

                def weight_high(q, i=0):
                    o = (q - q0) * T
                    src = gate[:, bass.ds(i * (16 * T) + o, T)] if not isinstance(i, int) else \
                        gate[:, i * 16 * T + o:i * 16 * T + o + T]
                    act.wait_ge(chunk_used, i * 16 + (q - 1))
                    nc.scalar.activation(g_hi[q % 2][:, :], src, ACT.Copy).then_inc(ghi_ready, 1)

                weight_high(q0)
                weight_high(q0 + 1)
                last = CHUNKS // 16 - 1
                with act.Fori(0, last) as i:
                    for j in range(2, 18):
                        high(q0 + j, i)
                        weight_high(q0 + j, i)
                for j in range(2, 18):
                    if half == 0 or j < 16:
                        high(q0 + j, last)
                    if j < 16:
                        weight_high(q0 + j, last)

            activations(0)
            act.wait_ge(top_ready, NT)
            for t in range(NT):
                nc.scalar.activation(choice[t][:, 256:384], choice[t][:, 256:384], ACT.Exp).then_inc(texp_ready, 1)
            pview = pick.rearrange("p (i m) -> p i m", i=3)
            for t in range(NT):
                act.wait_ge(choiceT_filled, t + 1)
                nc.scalar.activation(pview[:, :, t * P:(t + 1) * P], bank(t, 384).rearrange("p (i m) -> p i m", i=3),
                                     ACT.Copy).then_inc(pick_ready, 1)
            weights_high(0)
            activations(1)
            act.dma_start(hcT[:, :], ctx2_t).then_inc(ctx2_loaded, 16)
            weights_high(1)

            act.wait_ge(peer_half, 2)
            for dst, src in ((bias2, rpb), (wf, w_four), (wr, w_router)):
                act.dma_start(dst, src).then_inc(small2_loaded, 16)
            norm(3, hcT, lambda k: modc(1, 0, k, 1))
            norm(4, hT, lambda k: modc(1, 0, k, 0))
            for c in range(4):
                empty(kT2[:, c * 512:(c + 1) * 512])
            for c in range(4):
                empty(vN2[:, c * 512:(c + 1) * 512])
            for c in range(2):
                empty(qT2[:, c * 512:(c + 1) * 512])
            empty(fN)
            empty(hcv)
            for c in range(2):
                empty(gbc[:, c * 512:(c + 1) * 512])
            for n, dst in enumerate((tCS[:, 0:512], tCS[:, 512:1024], foT, catT[:, 0:512])):
                act.wait_ge(four_filled, n + 1)
                nc.scalar.activation(dst, bank(n % 2), ACT.Copy).then_inc(four_stored, 1)
            attention(1)
            for n in range(2):
                turned(8 + n, catT[:, (1 + n) * 512:(2 + n) * 512])
            norm(5, hT, lambda k: modc(1, 3, k, 0))
            for t in range(NT):
                act.wait_ge(rexp_in, 2 * t + 1)
                nc.scalar.activation(gex, gex, ACT.Exp, accum_out=gz).then_inc(rexp_out, 1)
                act.wait_ge(rexp_in, 2 * t + 2)
                nc.scalar.activation(pw[:, 0:2], pw[:, 0:2], ACT.Exp,
                                     accum_out=pw[:, 2:3]).then_inc(rexp_out, 1)
            for n in range(4):
                turned(10 + n, xN[:, n * 512:(n + 1) * 512])
            act.wait_ge(rounds_ready, 1)
            n_rounds = act.value_load(rounds[0:1, 0:1], min_val=1, max_val=MAX_ROUNDS)
            with act.Fori(0, n_rounds) as r:
                with act.Fori(0, QUADS) as q:
                    t = r * QUADS + q
                    act.wait_ge(gathered, t + 2)
                    act.wait_ge(scattered, t + 1)
                    nc.scalar.activation(selT, bank(2, 256), ACT.Copy)
                    nc.scalar.activation(xg[:, 512:1024], bank(0), ACT.Copy).then_inc(xg_high, 1)
                    act.wait_ge(hidden_filled, t * 2 + 1)
                    nc.scalar.activation(silg, bank(0), ACT.Silu).then_inc(silu_ready, 1)
                    act.wait_ge(down_filled, t + 1)
                    nc.scalar.activation(ye[:, 512:1024], bank(1), ACT.Copy).then_inc(ye_high, 1)
            norm(6, None, None)
            act.wait_ge(norm_done, NORM_DONE[6] + KD)
            act.dma_start(out, yfin).then_inc(out_stored, 16)
            act.wait_ge(out_stored, 16)

        @block.tensor
        def _(pe):
            def weights(n, i=None):
                v = 16 * (n // SLOTS + 1)
                pe.wait_ge(slab_loaded[n % SLOTS], v if i is None else i * 16 + v)
                return slab[n % SLOTS]

            spent = [False]

            def release():
                pe.sem_inc(slab_used, 1)

            def mm(*a, signal=None, **kw):
                ins = nc.tensor.matmul(*a, **kw)
                if signal is not None:
                    ins.then_inc(signal, 1)
                elif spent[0]:
                    ins.then_inc(slab_used, 1)
                    spent[0] = False

            def slab_done():
                assert not spent[0]
                spent[0] = True

            def chain(dst, pairs, signal=None):
                for k, (a, b) in enumerate(pairs):
                    last = k == len(pairs) - 1
                    mm(dst, a, b, start=k == 0, stop=last, signal=signal if last else None)

            pe.wait_ge(cond_ready, 1)
            cnd = conds.rearrange("p (k m c) -> p k m c", k=KD, m=2)

            def ada(n, buf):
                w = weights(ada_slab(n)).rearrange("p (k n) -> p k n", k=KD)
                for k in range(KD):
                    j = k % 4
                    mm(ps[32 * j:32 * j + 32, 6 * 512:7 * 512], cnd[:, k, n // ADA_SLABS, :], w[:, k, :],
                       start=k < 4, stop=k >= 4, signal=adarow_filled if k == KD - 1 else None)
                slab_done()
                pe.wait_ge(adarow_stored, n + 1)
                if n:
                    pe.wait_ge(mod_stored, n)
                for j in range(4):
                    mm(bank(7, 2, 2 * j), buf[:, j * P:(j + 1) * P], const("pairs"), start=True, stop=True,
                       signal=mod_filled if j == 3 else None)

            pe.wait_ge(inputs_loaded, 16 * 5)
            for n in range(ADA_FIRST):
                ada(n, big[:, 0:512])
            pe.wait_ge(mod_stored, ADA_FIRST)

            def norm(i):
                b = 6 + i % 2
                sq = scratch[:, (i % 2) * 2048:(i % 2) * 2048 + 2048]
                pe.wait_ge(norm_sq, i + 1)
                chain(bank(b, T), [(ones, sq[:, k * T:(k + 1) * T]) for k in range(KD)], norm_sum)

            norm(0)
            norm(1)
            unit = [0]

            def fill(parts, after=None):
                u = unit[0]
                unit[0] += 1
                if u >= 8:
                    pe.wait_ge(bank_emptied, u - 7)
                for i, (o, n, pairs) in enumerate(parts):
                    chain(bank(u % 8, n, o), pairs, bank_filled if i == len(parts) - 1 else None)

            def by_token(h, t, w, n):
                return [(0, n, [(h[:, k * T + t * P:k * T + (t + 1) * P], w[:, k, 0:n]) for k in range(KD)])]

            def by_feature(h, w, j):
                return [(w[:, k, j * P:(j + 1) * P], h[:, k * T:(k + 1) * T]) for k in range(KD)]

            def k_view(n, width=512):
                return weights(n)[:, 0:KD * width].rearrange("p (k n) -> p k n", k=KD)

            pe.wait_ge(norm_done, 2 * KD)
            tiles = ((hcT, 0), (hcT, 1), (hT, 0), (hT, 1))
            for s, width in ((S_K, 512), (S_V, 512), (S_GKV, 272)):
                w = k_view(s, width)
                for h, t in tiles:
                    fill(by_token(h, t, w, width))
                slab_done()
            w = k_view(S_Q)
            for j in range(0, 4, 2):
                fill([(0, T, by_feature(hT, w, j)), (T, T, by_feature(hT, w, j + 1))])
            slab_done()
            for s in (S_AQ, S_O):
                w = k_view(s)
                for t in range(NT):
                    fill(by_token(hT, t, w, 512))
                slab_done()
            for s in range(S_MG, S_MG + 4):
                w = k_view(s)
                for j in range(0, 4, 2):
                    fill([(0, T, by_feature(hT, w, j)), (T, T, by_feature(hT, w, j + 1))])
                slab_done()
            pe.wait_ge(bank_emptied, unit[0])

            pe.wait_ge(lf_ready, 1)
            lf = small[:, 96:128]
            for d in range(2):
                nc.tensor.matmul(bank(0, 16, 16 * d), const(f"tri{d}"), lf[:, 16 * d:16 * d + 16],
                                 start=True, stop=True)
            nc.tensor.matmul(bank(0, 32, 32), ones, lf, start=True, stop=True).then_inc(cums_filled, 1)
            for c in range(2):
                for h in range(HEADS):
                    ins = nc.tensor.transpose(bank(6 + c, P, h * P), kN[:, (2 + c) * 512 + h * P:(2 + c) * 512 + (h + 1) * P],
                                              ident)
                ins.then_inc(kT_filled, 1)
            for n in range(8):
                pe.wait_ge(diag_ready, n + 1)
                if n >= 2:
                    pe.wait_ge(rrow_used, n - 1)
                nc.tensor.matmul(bank(1 + n % 2), ones, pair[n % 2], start=True, stop=True).then_inc(rrow_filled, 1)
                if n == 0:
                    pe.wait_ge(kT_stored, 2)
                if n % 2:
                    ada(ADA_FIRST + n // 2, probsT[0])
            for c in range(2):
                pe.wait_ge(kT_stored, c + 1)
                for h in range(HEADS):
                    o = h * T + c * P
                    ins = nc.tensor.matmul(bank(3 * c, P, h * P), qT[:, o:o + P], kTl[:, o:o + P],
                                           start=True, stop=True)
                ins.then_inc(qk_filled, 1)
            for n in range(6):
                p, d = n // 2, n % 2
                c = (p, p ^ 1)[d]
                pe.wait_ge(kw_ready, n + 1)
                if n >= 1:
                    pe.wait_ge(cloc_used, n)
                for h in range(HEADS):
                    ins = nc.tensor.matmul(ps[:, 4 * 512 + h * 256:4 * 512 + h * 256 + 129],
                                           pair[n % 2][:, h * P:(h + 1) * P], vA[:, c, h, :], start=True, stop=True)
                ins.then_inc(cloc_filled, 1)
                if 1 <= n <= 4:
                    ada(ADA_FIRST + 3 + n, probsT[0])
            pe.wait_ge(mod_stored, ADA_SLABS)
            for n in range(4):
                p, d = n // 2, n % 2
                lc = (p, p ^ 1)[d]
                pe.wait_ge(smat_ready, n + 1)
                for h in range(HEADS):
                    o = (2 * d + p) * 512 + h * P
                    ins = nc.tensor.transpose(bank(1 + n % 2, P, h * P), decay[:, o:o + P], ident)
                ins.then_inc(smatT_filled, 1)
                if n == 0:
                    pe.wait_ge(cloc_used, 6)
                else:
                    pe.wait_ge(num_used, n)
                for h in range(HEADS):
                    nc.tensor.matmul(ps[:, 4 * 512 + h * 256:4 * 512 + h * 256 + 129],
                                     qT[:, h * T + lc * P:h * T + (lc + 1) * P], state[p][d][:, h, :],
                                     start=True, stop=True)
                pe.wait_ge(smatT_stored, n + 1)
                for h in range(HEADS):
                    ins = nc.tensor.matmul(ps[:, 6 * 512 + h * 256:6 * 512 + h * 256 + 129],
                                           pair[n % 2][:, h * P:(h + 1) * P], vA[:, 2 + lc, h, :],
                                           start=True, stop=True)
                ins.then_inc(num_filled, 1)

            def turn(n, srcs):
                for j, s in enumerate(srcs):
                    ins = nc.tensor.transpose(bank(n % 8, P, j * P), s, ident)
                ins.then_inc(turn_filled, 1)

            pe.wait_ge(num_used, 4)
            pe.wait_ge(roped, 1)
            for n in range(2):
                turn(n, [qR[:, t * 512 + pr * P:t * 512 + (pr + 1) * P]
                         for pr in (2 * n, 2 * n + 1) for t in range(NT)])
            for n, k in enumerate((kR, kSw)):
                turn(2 + n, [k[:, c * P:(c + 1) * P] for c in (2, 3, 0, 1)])

            def attention(blk):
                first = blk * UNITS

                def keys(h):
                    if blk == 0:
                        kv, base = h // 4, h % 2
                        return kTa[DH * base:DH * base + DH, (0 if kv == base else 512):(512 if kv == base else 1024)]
                    return kT2[DH * (h % 2):DH * (h % 2) + DH, (h // 2) * 512:(h // 2 + 1) * 512]

                def queries(b, h):
                    q = qTa if blk == 0 else qT2
                    o = (h // 2) * T + b * P
                    return q[DH * (h % 2):DH * (h % 2) + DH, o:o + P]

                def values(c, h):
                    if blk == 0:
                        o = (2, 3, 0, 1)[c] * P
                        return avN[:, o:o + P]
                    return vN2[:, c * 512 + (h // 2) * P:c * 512 + (h // 2 + 1) * P]

                def scores(u):
                    b, h = (u - first) // AH, u % AH
                    if u >= 2:
                        pe.wait_ge(scaled, u - 1)
                    nc.tensor.matmul(bank(u % 2), queries(b, h), keys(h), start=True,
                                     stop=True).then_inc(scores_filled, 1)

                def turn_probs(u):
                    pe.wait_ge(probs_ready, u + 1)
                    if u >= 2:
                        pe.wait_ge(probsT_stored, u - 1)
                    for c in range(4):
                        ins = nc.tensor.transpose(bank(2 + u % 2, P, c * P), probs[u % 2][:, c * P:(c + 1) * P], ident)
                    ins.then_inc(probsT_filled, 1)

                def apply(u):
                    h = u % AH
                    pe.wait_ge(probsT_stored, u + 1)
                    if u >= 2:
                        pe.wait_ge(head_stored, u - 1)
                    chain(bank(4 + u % 2, P), [(probsT[u % 2][:, c * P:(c + 1) * P], values(c, h))
                                               for c in range(4)], head_filled)

                scores(first)
                scores(first + 1)
                for u in range(first, first + UNITS):
                    turn_probs(u)
                    if u > first:
                        apply(u - 1)
                    if u + 2 < first + UNITS:
                        scores(u + 2)
                    if blk == 0 and u < ADA_SLABS:
                        ada(ADA_SLABS + u, hcT[:, 0:512])
                apply(first + UNITS - 1)

            pe.wait_ge(turn_stored, 4)
            attention(0)
            pe.wait_ge(m_ready, 1)
            pe.wait_ge(head_stored, UNITS)
            for i, src in enumerate((hN, aN)):
                for n in range(2):
                    turn(4 + 2 * i + n, [src[:, t * 512 + j * P:t * 512 + (j + 1) * P]
                                         for j in (2 * n, 2 * n + 1) for t in range(NT)])
            pe.wait_ge(turn_stored, 8)
            for i, src in enumerate((mT, aT)):
                w = weights(S_BM + i).rearrange("p (k n) -> p k n", k=4)
                for b in range(4):
                    for j in range(2):
                        o = (2 * b + j) * P
                        chain(bank(4 * i + b, T, j * T), [(w[:, k, o:o + P], src[:, k * T:(k + 1) * T]) for k in range(4)],
                              branch_filled if (b, j) == (3, 1) else None)
                slab_done()

            def project_out(s0, src):
                for half in range(2):
                    w = weights(s0 + half).rearrange("p (k n) -> p k n", k=KD)
                    for b in range(2):
                        for j in range(2):
                            chain(bank(2 * half + b, T, j * T), by_feature(src, w, 2 * b + j),
                                  y_filled if b and j else None)
                    slab_done()

            pe.wait_ge(merged_ready, 4)
            project_out(S_OUT, merged)

            norm(2)
            pe.wait_ge(norm_done, 3 * KD)
            for s in range(4):
                w = k_view(S_QUERY + s)
                for j in range(0, 4, 2):
                    fill([(0, T, by_feature(hT, w, j)), (T, T, by_feature(hT, w, j + 1))])
                slab_done()
            pe.wait_ge(bank_emptied, unit[0])
            pe.wait_ge(subk_loaded, 16)
            for t in range(NT):
                for b in range(4):
                    for j in range(4):
                        hp = 4 * b + j
                        ins = nc.tensor.matmul(bank(4 * t + b, P, j * P), qTr[:, hp * T + t * P:hp * T + (t + 1) * P],
                                               subk[:, hp * P:(hp + 1) * P], start=True, stop=True)
                    ins.then_inc(rscores_filled, 1)
            pe.wait_ge(rscores_stored, 8)
            zeros512 = cst[:, CONSTS["window"][0]:CONSTS["window"][0] + 512]
            pe.wait_ge(zeros_ready, 1)

            def open_sums():
                for b in range(4):
                    mm(bank(4 + b), ones, zeros512, start=True, stop=True)

            open_sums()
            groups = T // GROUP
            for half in range(2):
                base = S_PEER + half * 2 * HALF_SLABS

                def split_product(dst, q, o, high, low, start, i=None, **kw):
                    n = S_PEER + q // 4
                    wl = slab_lo[n % SLOTS][:, (q % 4) * CHUNK + o:(q % 4) * CHUNK + o + P]
                    wh = w_hi[q % 2][:, o:o + P]
                    mm(dst, wh, high, start=start, stop=False, **kw)
                    mm(dst, wh, low, start=False, stop=False, **kw)
                    return wl, high

                def activations(i, q0=4 * (base - S_PEER), half=half):
                    for j in range(16):
                        q = q0 + j
                        pe.wait_ge(lo_ready, i * 16 + (q + 1))
                        if j % 2 == 0 and not (isinstance(i, int) and half == 0 and j < 8):
                            pe.wait_ge(gelu_ready, i * 8 + (half * CHUNKS // 2 + j // 2 - 3))
                        dst = bank((j // 2) % 4, T, (j % 2) * T)
                        for k in range(KD):
                            hk = slice(k * T, (k + 1) * T)
                            wl, hh = split_product(dst, q, k * P, h_hi[:, hk], h_lo[:, hk], k == 0)
                            mm(dst, wl, hh, start=False, stop=k == KD - 1, signal=chunk_used if k == KD - 1 else None)
                        if j % 4 == 3:
                            slab_done()

                pe.wait_ge(h_lo_ready, 1)
                activations(0)
                with pe.Fori(1, HALF_SLABS // 4) as i:
                    activations(i)
                pe.wait_ge(gelu_ready, (half + 1) * 2 * HALF_SLABS)
                if half == 0:
                    for t in range(NT):
                        pe.wait_ge(choice_ready, t + 1)
                        for i in range(3):
                            ins = nc.tensor.transpose(bank(t, P, i * P), choice[t][:, i * P:(i + 1) * P], ident)
                        ins.then_inc(choiceT_filled, 1)
                    pe.wait_ge(pick_ready, NT)

                def gates(g, s, half=half):
                    n = g * 2 + (half * groups + s)
                    pe.wait_ge(ohw_ready, n + 1)
                    pe.wait_ge(oh2_ready, n + 1)
                    if not (isinstance(g, int) and half == 0):
                        pe.wait_ge(weight_ready, n - 1)
                    for m in range(GROUP):
                        n2 = min(2, GROUP - m) * HALF_E1
                        mm(bank(s, n2, m * HALF_E1), oh2[s][:, m * P:(m + 1) * P],
                           oh1[s][:, m * HALF_E1:m * HALF_E1 + n2], start=True, stop=True,
                           signal=gate_filled if m == GROUP - 1 else None)

                for s in range(2):
                    gates(0, s)
                with pe.Fori(1, groups // 2) as g:
                    for s in range(2):
                        gates(g, s)
                pe.wait_ge(weight_ready, (half + 1) * groups)

                def combine(i, q0=(2 * half + 1) * CHUNKS):
                    for j in range(16):
                        q = q0 + j
                        pe.wait_ge(lo_ready, i * 16 + (q + 1))
                        pe.wait_ge(glo_ready, i * 16 + (half * CHUNKS + j + 1))
                        for c in range(KD):
                            dst = bank(4 + c // 2, T, (c % 2) * T)
                            wl, gh = split_product(dst, q, c * P, g_hi[q % 2][:, :], g_lo[q % 2][:, :], False,
                                                   skip_group_check=True)
                            mm(dst, wl, gh, start=False, stop=True, skip_group_check=True,
                               signal=chunk_used if c == KD - 1 else None)
                        if j % 4 == 3:
                            slab_done()

                combine(0)
                with pe.Fori(1, HALF_SLABS // 4) as i:
                    combine(i)
                mm(bank(0, P), ones, ident, start=True, stop=True, signal=peer_half)

            norm(3)
            norm(4)
            pe.wait_ge(norm_done, 5 * KD)
            w = k_view(S_K2)
            for j in range(4):
                fill([(0, T, by_feature(hT, w, j)), (T, T, by_feature(hcT, w, j))])
            slab_done()
            w = k_view(S_V2)
            for h, t in ((hT, 0), (hT, 1), (hcT, 0), (hcT, 1)):
                fill(by_token(h, t, w, 512))
            slab_done()
            w = k_view(S_Q2)
            for j in range(0, 4, 2):
                fill([(0, T, by_feature(hT, w, j)), (T, T, by_feature(hT, w, j + 1))])
            slab_done()
            w = k_view(S_FH2)
            fill([(t * T, T, [(hT[:, k * T + t * P:k * T + (t + 1) * P], w[:, k, 0:T]) for k in range(KD)])
                  for t in range(NT)])
            fill([(0, T, by_feature(hT, w, 2)), (T, T, by_feature(hT, w, 3))])
            slab_done()
            w = k_view(S_G2)
            for j in range(0, 4, 2):
                fill([(0, T, by_feature(hT, w, j)), (T, T, by_feature(hT, w, j + 1))])
            slab_done()
            pe.wait_ge(bank_emptied, unit[0])
            pe.wait_ge(small2_loaded, 48)
            for n, name in enumerate(("dft_c", "dft_s")):
                tab = const(name)
                for j in range(2):
                    chain(bank(n, T, j * T), [(fN[:, t * T + j * P:t * T + (j + 1) * P], tab[:, t * T:(t + 1) * T])
                                              for t in range(NT)], four_filled if j else None)
            pe.wait_ge(four_stored, 2)
            for j in range(2):
                chain(bank(0, T, j * T), [(const("dch_c"), tCS[:, j * T:(j + 1) * T]),
                                          (const("dch_s"), tCS[:, 512 + j * T:512 + (j + 1) * T])],
                      four_filled if j else None)
            pe.wait_ge(four_stored, 3)
            for j in range(2):
                chain(bank(1, T, j * T), [(wf[:, k * T + j * P:k * T + (j + 1) * P], foT[:, k * T:(k + 1) * T])
                                          for k in range(2)], four_filled if j else None)
            pe.wait_ge(four_stored, 4)
            attention(1)
            pe.wait_ge(head_stored, 2 * UNITS)
            for n in range(2):
                turn(8 + n, [aN2[:, t * 512 + j * P:t * 512 + (j + 1) * P] for j in (2 * n, 2 * n + 1) for t in range(NT)])
            pe.wait_ge(turn_stored, 10)
            pe.wait_ge(conv_ready, 1)
            project_out(S_OUT2, catT)
            norm(5)
            pe.wait_ge(norm_done, 6 * KD)
            nr = NG + NE
            for t in range(NT):
                chain(bank(t, nr), [(hT[:, k * T + t * P:k * T + (t + 1) * P], wr[:, k * nr:(k + 1) * nr])
                                    for k in range(KD)], router_filled)
            for n in range(4):
                turn(10 + n, [hT[:, (4 * (n % 2) + k) * T + (n // 2) * P:(4 * (n % 2) + k) * T + (n // 2 + 1) * P]
                              for k in range(4)])
            pe.wait_ge(sel32_ready, 1)
            mm(bank(6, NE), const("tri0"), sel32[:, 0:NE], start=True, stop=True)
            chain(bank(6, NE, NE), [(ones, sel32[:, 0:NE]), (const("tri0"), sel32[:, NE:2 * NE])])
            chain(bank(6, NE, 2 * NE), [(ones, sel32[:, 0:NE]), (ones, sel32[:, NE:2 * NE])], counts_filled)
            pe.wait_ge(rounds_ready, 1)
            pe.wait_ge(turn_stored, 14)
            open_sums()
            mm(bank(0, P), ones, ident, start=True, stop=True, signal=gathered)
            mm(bank(0, P), ones, ident, start=True, stop=True, signal=scattered)
            n_rounds = pe.value_load(rounds[0:1, 0:1], min_val=1, max_val=MAX_ROUNDS)
            with pe.Fori(0, n_rounds) as r:
                with pe.Fori(0, QUADS) as q:
                    t = r * QUADS + q
                    ring = r * (QUADS * Q_SLABS // SLOTS) + q * (Q_SLABS // SLOTS)
                    pe.wait_ge(sel_ready, t + 1)
                    for b in range(NT):
                        nc.tensor.transpose(bank(2, P, b * P), selw[:, b * P:(b + 1) * P], ident)
                    for k in range(KD):
                        chain(bank((3, 0)[k // 4], P, (k % 4) * P),
                              [(xN[:, b * D + k * P:b * D + (k + 1) * P], sel[:, b * P:(b + 1) * P]) for b in range(NT)],
                              gathered if k == KD - 1 else None)
                    pe.wait_ge(xg_low, t + 1)
                    pe.wait_ge(xg_high, t + 1)
                    for b in range(2):
                        for s in range(4):
                            w = weights(S_MOE + 4 * b + s, ring).rearrange("p (e k n) -> p e k n", e=QUAD, k=2)
                            for k2 in range(2):
                                for e in range(QUAD):
                                    k = 2 * s + k2
                                    mm(ps[32 * e:32 * e + 32, b * 512:(b + 1) * 512],
                                       xg[:, k * P + e * ROOM:k * P + (e + 1) * ROOM], w[:, e, k2, :],
                                       start=k == 0, stop=k == KD - 1,
                                       signal=hidden_filled if (k, e) == (KD - 1, QUAD - 1) else None)
                            slab_done()
                    pe.wait_ge(he_ready, t + 1)
                    for f in range(4):
                        ins = nc.tensor.transpose(bank(2, P, f * P), he[:, f * P:(f + 1) * P], ident)
                    ins.then_inc(heT_filled, 1)
                    pe.wait_ge(heT_ready, t + 1)
                    for f in range(4):
                        w = weights(S_MOE + 8 + f, ring).rearrange("p (e n) -> p e n", e=QUAD)
                        for b in range(2):
                            for e in range(QUAD):
                                o = (3, 1)[b] * 512
                                mm(ps[32 * e:32 * e + 32, o:o + 512],
                                   heT[:, f * P + e * ROOM:f * P + (e + 1) * ROOM], w[:, e, b * 512:(b + 1) * 512],
                                   start=f == 0, stop=f == 3,
                                   signal=down_filled if (f, b, e) == (3, 1, QUAD - 1) else None)
                        if f < 3:
                            slab_done()
                    pe.wait_ge(down_filled, t + 1)
                    release()
                    pe.wait_ge(ye_low, t + 1)
                    pe.wait_ge(ye_high, t + 1)
                    for c in range(KD):
                        mm(bank(4 + c // 2, T, (c % 2) * T), ye[:, c * P:(c + 1) * P], selT, start=False, stop=True,
                           skip_group_check=True, signal=scattered if c == KD - 1 else None)
            mm(bank(0, P), ones, ident, start=True, stop=True, signal=experts_done)
            norm(6)

        @block.vector
        def _(dve):
            V = nc.vector
            steps = [0]

            def step(ins):
                steps[0] += 1
                ins.then_inc(dve_step, 1)
                dve.wait_ge(dve_step, steps[0])

            dve.wait_ge(inputs_loaded, 16 * 5)

            def squares(i, src):
                sq = scratch[:, (i % 2) * 2048:(i % 2) * 2048 + 2048]
                V.tensor_tensor(sq, src[:, :], src[:, :], ALU.mult).then_inc(norm_sq, 1)

            def norm(i, src, dst, g, scale):
                b = 6 + i % 2
                dve.wait_ge(norm_sum, i + 1)
                step(V.tensor_scalar(rstd[:, :], bank(b, T), 1.0 / D, EPS, ALU.mult, ALU.add))
                V.reciprocal(rstd[:, :], rstd[:, :]).then_inc(norm_inv, 1)
                if scale is None:
                    step(V.tensor_copy(gain[:, :], g))
                else:
                    step(V.tensor_scalar(gain[:, :], scale, 1.0, None, ALU.add))
                    step(V.tensor_tensor(gain[:, :], gain[:, :], g, ALU.mult))
                dve.wait_ge(norm_rstd, i + 1)
                for k in range(KD):
                    V.scalar_tensor_tensor(out=dst[:, k * T:(k + 1) * T], in0=src[:, k * T:(k + 1) * T],
                                           scalar=gain[:, k:k + 1], in1=rstd[:, :], op0=ALU.mult,
                                           op1=ALU.mult).then_inc(norm_scaled if scale is not None else norm_done, 1)

            squares(0, xT)
            squares(1, hcT)
            md = mod.rearrange("p (n c) -> p n c", c=2)
            def ada(n):
                dve.wait_ge(mod_filled, n + 1)
                V.tensor_tensor(md[:, 4 * n:4 * n + 4, :], bank(7, 8).rearrange("p (j c) -> p j c", c=2),
                                colv("b_ada")[:, 4 * n:4 * n + 4].unsqueeze(2).broadcast_to([P, 4, 2]),
                                ALU.add).then_inc(mod_stored, 1)

            for n in range(ADA_FIRST):
                ada(n)
            dve.wait_ge(mod_stored, ADA_FIRST)
            norm(0, xT, hT, colv("g_mix"), modp(0, 1, 0))
            dve.wait_ge(norm_scaled, KD)
            norm(1, hcT, hcT, colv("g_mix"), modp(0, 1, 1))

            L2 = small
            li, fg, soft, lf = L2[:, 0:32], L2[:, 32:64], L2[:, 64:96], L2[:, 96:128]
            cum, tot, rr = L2[:, 128:160], L2[:, 160:192], L2[:, 192:224]
            rmax = L2[:, 224:256]
            lmax = L2[:, 256:272]
            mst = L2[:, 272:296]
            exin, exout = L2[:, 296:400], L2[:, 400:504]
            v3 = lambda t: t.rearrange("p (d c h) -> p d c h", d=2, c=4)
            g4 = gat.rearrange("p (c d g h) -> p c d g h", c=4, d=2, g=2)
            bg = rowv("b_gates").rearrange("p (d g h) -> p d g h", d=2, g=2)
            dve.wait_ge(bank_emptied, 12)
            dve.wait_ge(norm_done, 2 * KD)
            for gi, dst in ((0, li), (1, fg)):
                for d in range(2):
                    for p in range(4):
                        c = (p, p ^ 1)[d]
                        ins = V.tensor_tensor(v3(dst)[:, d, p, :], g4[:, c, d, gi, :], bg[:, d, gi, :], ALU.add)
            ins.then_inc(gates_biased, 1)
            dve.wait_ge(gates_biased, 1)
            V.memset(vA[:, :, :, P:P + 1], 1.0)
            step(V.tensor_scalar(lf, fg, 0.0, None, ALU.min))
            dve.wait_ge(soft_ready, 1)
            V.tensor_tensor(lf, lf, soft, ALU.subtract).then_inc(lf_ready, 1)
            dve.wait_ge(cums_filled, 1)
            V.tensor_copy(cum, bank(0, 32))
            step(V.tensor_copy(tot, bank(0, 32, 32)))
            step(V.tensor_tensor(rr, li, cum, ALU.subtract))
            idb = ident.unsqueeze(1).broadcast_to([P, HEADS, P])
            h3 = lambda t: t.rearrange("p (h s) -> p h s", h=HEADS)

            def place_diag(n):
                if n >= 2:
                    dve.wait_ge(rrow_filled, n - 1)
                V.tensor_tensor(h3(pair[n % 2]), idb, rr[:, 4 * n:4 * n + 4].unsqueeze(2).broadcast_to([P, HEADS, P]),
                                ALU.mult).then_inc(diag_ready, 1)

            place_diag(0)
            dve.wait_ge(bank_filled, UNITS_B1)
            for n in range(8):
                d, p = n // 4, n % 4
                if n + 1 < 8:
                    place_diag(n + 1)
                dve.wait_ge(rrow_filled, n + 1)
                rowb = bank(1 + n % 2).rearrange("p (h s) -> p h s", h=HEADS)
                ins = V.tensor_reduce(rmax[:, 4 * n:4 * n + 4], rowb, X, ALU.max)
                if p >= 2:
                    dst = h3(decay[:, (2 * d + p - 2) * 512:(2 * d + p - 1) * 512])
                    ins = V.tensor_tensor(dst, rowb, const(f"seen{d}").unsqueeze(1).broadcast_to([P, HEADS, P]), ALU.add)
                ins.then_inc(rrow_used, 1)
                if n % 2:
                    ada(ADA_FIRST + n // 2)
            dve.wait_ge(rrow_used, 8)
            for n in range(4):
                ins = V.tensor_reduce(lmax[:, 4 * n:4 * n + 4], h3(decay[:, n * 512:(n + 1) * 512]), X, ALU.max)
            ex = lambda q: exin[:, 8 * q:8 * q + 8].rearrange("p (d h) -> p d h", d=2)
            eo = lambda q: exout[:, 8 * q:8 * q + 8].rearrange("p (d h) -> p d h", d=2)
            ms = lambda q: mst[:, 8 * q:8 * q + 8].rearrange("p (d h) -> p d h", d=2)
            lm = lmax.rearrange("p (d c h) -> p d c h", d=2, c=2)
            step(ins)
            for p in range(3):
                if p == 0:
                    step(V.tensor_copy(ex(0), v3(tot)[:, :, 0, :]))
                else:
                    step(V.tensor_tensor(ex(3 * p), v3(tot)[:, :, p, :], ms(p - 1), ALU.add))
                step(V.tensor_tensor(ex(3 * p + 1), v3(tot)[:, :, p, :], v3(rmax)[:, :, p, :], ALU.add))
                step(V.tensor_tensor(ms(p), ex(3 * p), ex(3 * p + 1), ALU.max))
                step(V.tensor_tensor(ex(3 * p), ex(3 * p), ms(p), ALU.subtract))
                step(V.tensor_tensor(ex(3 * p + 1), ex(3 * p + 1), ms(p), ALU.subtract))
                step(V.tensor_tensor(ex(3 * p + 2), v3(rr)[:, :, p, :], v3(rmax)[:, :, p, :], ALU.subtract))
            for q in range(2):
                step(V.tensor_tensor(lm[:, :, q, :], lm[:, :, q, :], ms(q + 1), ALU.max))
                step(V.tensor_tensor(ex(9 + q), ms(q + 1), lm[:, :, q, :], ALU.subtract))
                step(V.tensor_tensor(ex(11 + q), v3(cum)[:, :, 2 + q, :], lm[:, :, q, :], ALU.add))
                step(V.tensor_scalar(ex(11 + q), ex(11 + q), -1.0, None, ALU.mult))
            V.engine_nop().then_inc(exps_in, 1)
            for n in range(4):
                dd = h3(decay[:, n * 512:(n + 1) * 512])
                V.tensor_tensor(dd, dd, lmax[:, 4 * n:4 * n + 4].unsqueeze(2).broadcast_to([P, HEADS, P]),
                                ALU.subtract).then_inc(decay_in, 1)
            dve.wait_ge(exps_out, 1)
            bc = lambda a: a.unsqueeze(2).broadcast_to([P, HEADS, 129])
            ps4 = lambda b: ps[:, b * 512:(b + 2) * 512].rearrange("p (h v) -> p h v", h=HEADS)[:, :, 0:129]

            def weight_keys(n):
                p, d = n // 2, n % 2
                c = (p, p ^ 1)[d]
                if n >= 2:
                    dve.wait_ge(cloc_filled, n - 1)
                else:
                    dve.wait_ge(rrow_filled, 8)
                V.tensor_tensor(h3(pair[n % 2]), h3(kN[:, c * 512:(c + 1) * 512]),
                                eo(3 * p + 2)[:, d, :].unsqueeze(2).broadcast_to([P, HEADS, P]),
                                ALU.mult).then_inc(kw_ready, 1)

            weight_keys(0)
            for n in range(6):
                p, d = n // 2, n % 2
                if n + 1 < 6:
                    weight_keys(n + 1)
                dve.wait_ge(cloc_filled, n + 1)
                old, new = eo(3 * p)[:, d, :], eo(3 * p + 1)[:, d, :]
                src, dst = (state[0][d], state[0][d]) if p < 2 else (state[0][d], state[1][d])
                if p == 0:
                    V.tensor_tensor(dst, ps4(4), bc(new), ALU.mult).then_inc(cloc_used, 1)
                    dve.wait_ge(cloc_used, n + 1)
                else:
                    V.tensor_tensor(t1, ps4(4), bc(new), ALU.mult).then_inc(cloc_used, 1)
                    step(V.tensor_tensor(dst, src, bc(old), ALU.mult))
                    dve.wait_ge(cloc_used, n + 1)
                    step(V.tensor_tensor(dst, dst, t1, ALU.add))
                if 1 <= n <= 4:
                    ada(ADA_FIRST + 3 + n)
            dve.wait_ge(decay_out, 1)
            dve.wait_ge(qk_filled, 2)
            for n in range(4):
                p, d = n // 2, n % 2
                lc = (p, p ^ 1)[d]
                o = (2 * d + p) * 512
                V.tensor_tensor(decay[:, o:o + 512], bank(3 * lc), decay[:, o:o + 512], ALU.mult).then_inc(smat_ready, 1)
            for n in range(4):
                p, d = n // 2, n % 2
                lc = (p, p ^ 1)[d]
                dve.wait_ge(num_filled, n + 1)
                step(V.tensor_tensor(t1, ps4(4), bc(eo(9 + p)[:, d, :]), ALU.mult))
                V.tensor_tensor(t1, t1, ps4(6), ALU.add).then_inc(num_used, 1)
                dve.wait_ge(num_used, n + 1)
                den, den2 = small[:, 608:612], small[:, 612:616]
                step(V.tensor_scalar(den2, t1[:, :, P], -1.0, None, ALU.mult))
                step(V.tensor_tensor(den, t1[:, :, P], den2, ALU.max))
                step(V.tensor_tensor(den, den, eo(11 + p)[:, d, :], ALU.max))
                step(V.reciprocal(den, den))
                hb = den.unsqueeze(2).broadcast_to([P, HEADS, P])
                dst = h3(hN[:, lc * 512:(lc + 1) * 512])
                if p == 0:
                    step(V.tensor_tensor(dst, t1[:, :, 0:P], hb, ALU.mult))
                else:
                    step(V.tensor_tensor(t1[:, :, 0:P], t1[:, :, 0:P], hb, ALU.mult))
                    step(V.tensor_tensor(dst, dst, t1[:, :, 0:P], ALU.add))
            sqh = at(big, 14416, 1024)
            h8 = lambda t: t.rearrange("p (h s) -> p h s", s=P)
            rs8 = small[:, 512:520]
            step(V.tensor_tensor(sqh, hN, hN, ALU.mult))
            step(V.tensor_reduce(rs8, h8(sqh), X, ALU.add))
            step(V.tensor_scalar(rs8, rs8, 1.0 / P, EPS, ALU.mult, ALU.add))
            V.reciprocal(rs8, rs8).then_inc(hms_ready, 1)
            sqk = at(big, 16464, 1536)
            rq = small[:, 520:544]
            step(V.tensor_tensor(sqk[:, 0:1024], aqN, aqN, ALU.mult))
            step(V.tensor_tensor(sqk[:, 1024:1536], akN, akN, ALU.mult))
            step(V.tensor_reduce(rq, sqk.rearrange("p (h s) -> p h s", s=DH), X, ALU.add))
            step(V.tensor_scalar(rq, rq, 1.0 / DH, EPS, ALU.mult, ALU.add))
            V.reciprocal(rq, rq).then_inc(qkms_ready, 1)
            dve.wait_ge(hrstd_ready, 1)
            step(V.tensor_tensor(h8(hN), h8(hN), rs8.unsqueeze(2).broadcast_to([P, 8, P]), ALU.mult))
            h2 = lambda t: t.rearrange("p (t f) -> p t f", t=NT)
            step(V.tensor_tensor(h2(hN), h2(hN), rowv("g_mlstm").unsqueeze(1).broadcast_to([P, NT, 512]), ALU.mult))
            dve.wait_ge(bank_emptied, 18)
            V.tensor_tensor(hN, hN, sigO, ALU.mult).then_inc(m_ready, 1)
            dve.wait_ge(qkrstd_ready, 1)
            d64 = lambda t: t.rearrange("p (h s) -> p h s", s=DH)
            for t, nh, r, g in ((aqN, 16, rq[:, 0:16], "g_q"), (akN, 8, rq[:, 16:24], "g_k")):
                step(V.tensor_tensor(d64(t), d64(t), r.unsqueeze(2).broadcast_to([P, nh, DH]), ALU.mult))
                step(V.tensor_tensor(d64(t), d64(t), rowv(g).unsqueeze(1).broadcast_to([P, nh, DH]), ALU.mult))
            step(V.tensor_copy(kR[:, 0:256], akN[:, 0:256]))
            for src, dst, nh in ((aqN, qR, AH), (akN[:, 256:512], kR[:, 256:512], 2)):
                s4 = src.rearrange("p (t h s) -> p t h s", t=NT, s=DH)
                o4 = dst.rearrange("p (t h s) -> p t h s", t=NT, s=DH)
                u4 = sqk[:, 0:NT * nh * 32].rearrange("p (t h s) -> p t h s", t=NT, s=32)
                cs, sn = (const(x).rearrange("p (t s) -> p t s", t=NT).unsqueeze(2).broadcast_to([P, NT, nh, 32])
                          for x in ("cos", "sin"))
                lo, hi = slice(0, 32), slice(32, 64)
                for a, b, op in ((lo, hi, ALU.subtract), (hi, lo, ALU.add)):
                    V.tensor_tensor(o4[:, :, :, a], s4[:, :, :, a], cs, ALU.mult)
                    step(V.tensor_tensor(u4, s4[:, :, :, b], sn, ALU.mult))
                    step(V.tensor_tensor(o4[:, :, :, a], o4[:, :, :, a], u4, op))
            k4 = kR.rearrange("p (c h s) -> p c h s", c=4, h=2)
            w4 = kSw.rearrange("p (c h s) -> p c h s", c=4, h=2)
            V.tensor_copy(w4[:, :, 0, :], k4[:, :, 1, :])
            V.tensor_copy(w4[:, :, 1, :], k4[:, :, 0, :]).then_inc(roped, 1)

            def attention(blk, dst):
                first = blk * UNITS

                def logits(u):
                    b, h = (u - first) // AH, u % AH
                    st = stat[:, 4 * u:4 * u + 4]
                    dve.wait_ge(scaled, u + 1)
                    if blk == 0:
                        bias = const("window")[:, b * T:(b + 1) * T]
                    else:
                        bias = bias2[:, h * 384 + (2 - 2 * b) * 64:h * 384 + (2 - 2 * b) * 64 + T]
                    step(V.tensor_tensor(logit[u % 2][:, 0:T], logit[u % 2][:, 0:T], bias, ALU.add))
                    step(V.tensor_reduce(st[:, 3:4], logit[u % 2], X, ALU.max))
                    if blk == 0:
                        V.tensor_scalar(st[:, 0:1], st[:, 3:4], rowv("sink")[:, h:h + 1], -1.0, ALU.max,
                                        ALU.mult).then_inc(logits_ready, 1)
                    else:
                        V.tensor_scalar(st[:, 0:1], st[:, 3:4], -1.0, None, ALU.mult).then_inc(logits_ready, 1)

                def store_turned(u):
                    dve.wait_ge(probsT_filled, u + 1)
                    if u >= 2:
                        dve.wait_ge(head_filled, u - 1)
                    V.tensor_copy(probsT[u % 2], bank(2 + u % 2)).then_inc(probsT_stored, 1)

                def finish(u):
                    b, h = (u - first) // AH, u % AH
                    st = stat[:, 4 * u:4 * u + 4]
                    if blk == 0:
                        dve.wait_ge(sink_ready, u + 1)
                        step(V.tensor_tensor(st[:, 1:2], st[:, 1:2], st[:, 2:3], ALU.add))
                    step(V.reciprocal(st[:, 1:2], st[:, 1:2]))
                    dve.wait_ge(head_filled, u + 1)
                    half = (h // 4 if blk == 0 else h % 2) * DH
                    V.tensor_scalar(dst[:, b * 512 + h * DH:b * 512 + (h + 1) * DH], bank(4 + u % 2, DH, half),
                                    st[:, 1:2], None, ALU.mult).then_inc(head_stored, 1)

                logits(first)
                for u in range(first, first + UNITS):
                    if u + 1 < first + UNITS:
                        logits(u + 1)
                    store_turned(u)
                    if u > first:
                        finish(u - 1)
                    if blk == 0 and 1 <= u <= ADA_SLABS:
                        ada(ADA_SLABS + u - 1)
                finish(first + UNITS - 1)

            attention(0, aN)
            dve.wait_ge(branch_filled, 2)
            dve.wait_ge(bank_emptied, UNITS_B1)
            for b in range(4):
                o = b * 512
                V.tensor_tensor(tmpm[0], bank(b), sigG[:, o:o + 512], ALU.mult)
                step(V.tensor_tensor(tmpm[1], bank(4 + b), sigG[:, 2048 + o:2048 + o + 512], ALU.mult))
                V.tensor_tensor(merged[:, o:o + 512], tmpm[0], tmpm[1], ALU.add).then_inc(merged_ready, 1)
                dve.wait_ge(merged_ready, b + 1)

            def residual(block_, part, base, src=0):
                for j in range(KD):
                    if src == 0:
                        dve.wait_ge(y_filled, base + 1 + j // 4)
                    x = xT[:, j * T:(j + 1) * T]
                    V.scalar_tensor_tensor(out=x, in0=bank(src + j // 2, T, (j % 2) * T), scalar=modc(block_, part, j),
                                           in1=x, op0=ALU.mult, op1=ALU.add).then_inc(x_updated, 1)

            residual(0, 2, 0)
            dve.wait_ge(x_updated, KD)
            squares(2, xT)
            norm(2, xT, hT, colv("g_ffn"), modp(0, 4))

            V.memset(cst[:, CONSTS["window"][0]:CONSTS["window"][0] + 512], 0.0).then_inc(zeros_ready, 1)

            def top16(src, val, idx):
                step(V.max(val[:, 0:8], src))
                step(V.max_index(idx[:, 0:8], val[:, 0:8], src))
                step(V.match_replace(src, val[:, 0:8], src, BIG_NEG))
                step(V.max(val[:, 8:16], src))
                step(V.max_index(idx[:, 8:16], val[:, 8:16], src))

            s3 = top1.rearrange("p (h q a) -> p h q a", h=RH, q=2)
            i3 = idx1.rearrange("p (h q a) -> p h q a", h=RH, q=2)
            big3 = lambda t: t.rearrange("p (h a b) -> p h a b", h=RH, a=TOPK)
            shape = [P, RH, TOPK, TOPK]
            tv = top2.rearrange("p (h k) -> p h k", h=RH)
            i16 = iota[:, 0:TOPK].unsqueeze(1).broadcast_to([P, RH * TOPK, TOPK])

            def choose(t, h):
                for q in range(2):
                    hp = 2 * h + q
                    top16(sc[t][:, hp * P:(hp + 1) * P], top1[:, hp * TOPK:(hp + 1) * TOPK],
                          idx1.bitcast(U32)[:, hp * TOPK:(hp + 1) * TOPK])
                cand = sc[t][:, h * 256:(h + 1) * 256]
                step(V.tensor_tensor(cand.rearrange("p (a b) -> p a b", a=TOPK),
                                     s3[:, h, 0, :].unsqueeze(2).broadcast_to([P, TOPK, TOPK]),
                                     s3[:, h, 1, :].unsqueeze(1).broadcast_to([P, TOPK, TOPK]), ALU.add))
                top16(cand, top2[:, h * TOPK:(h + 1) * TOPK], pos.bitcast(U32)[:, h * TOPK:(h + 1) * TOPK])

            def look_up(t):
                tmpr = sc[t]
                step(V.tensor_copy(idx1, idx1.bitcast(U32)))
                cv = choice[t][:, 256:384].rearrange("p (h k) -> p h k", h=RH)
                step(V.tensor_scalar(posa.bitcast(U32), pos.bitcast(U32), 4, None, ALU.logical_shift_right))
                step(V.tensor_scalar(pos.bitcast(U32), pos.bitcast(U32), 15, None, ALU.bitwise_and))
                step(V.tensor_copy(posa, posa.bitcast(U32)))
                step(V.tensor_copy(pos, pos.bitcast(U32)))
                for q, pf in ((0, posa), (1, pos)):
                    step(V.tensor_tensor(tmpr.rearrange("p (n a) -> p n a", a=TOPK),
                                         pf.unsqueeze(2).broadcast_to([P, RH * TOPK, TOPK]), i16, ALU.is_equal))
                    step(V.tensor_tensor(big3(tmpr), big3(tmpr), i3[:, :, q, :].unsqueeze(2).broadcast_to(shape), ALU.mult))
                    step(V.tensor_reduce(choice[t][:, q * P:(q + 1) * P], tmpr.rearrange("p (n a) -> p n a", a=TOPK),
                                         X, ALU.add))
                V.tensor_tensor(cv, tv, tv[:, :, 0:1].broadcast_to([P, RH, TOPK]), ALU.subtract).then_inc(top_ready, 1)
                dve.wait_ge(top_ready, t + 1)

            dve.wait_ge(h_hi_ready, 1)
            dve.wait_ge(bank_filled, UNITS_B1 + UNITS_Q)
            V.tensor_tensor(h_lo[:, :], hT[:, :], h_hi[:, :].bitcast(F32), ALU.subtract).then_inc(h_lo_ready, 1)

            for t in range(NT):
                dve.wait_ge(rscores_stored, 4 * (t + 1))
                for h in range(RH):
                    choose(t, h)
                look_up(t)
            for t in range(NT):
                cv = choice[t][:, 256:384].rearrange("p (h k) -> p h k", h=RH)
                dve.wait_ge(texp_ready, t + 1)
                step(V.tensor_reduce(zsum[:, 0:RH], cv, X, ALU.add))
                step(V.reciprocal(zsum[:, 0:RH], zsum[:, 0:RH]))
                V.tensor_tensor(cv, cv, zsum[:, 0:RH].unsqueeze(2).broadcast_to([P, RH, TOPK]),
                                ALU.mult).then_inc(choice_ready, 1)
                dve.wait_ge(choice_ready, t + 1)

            dve.wait_ge(pick_ready, NT)
            groups = T // GROUP
            gview = gate.rearrange("p (e m) -> p m e", m=T)
            for half in range(2):
                if half:
                    with dve.Fori(0, CHUNKS // 16) as i:
                        for j in range(16):
                            low_part(dve, V, 2 * CHUNKS + j, i)

                def one_hots(g, s, half=half):
                    n = g * 2 + (half * groups + s)
                    if not (isinstance(g, int) and half == 0):
                        dve.wait_ge(gate_filled, n - 1)
                    o = g * (2 * GROUP) + s * GROUP
                    V.tensor_tensor(oh1[s].rearrange("p (m e) -> p m e", m=GROUP),
                                    iota[:, half * HALF_E1:(half + 1) * HALF_E1].unsqueeze(1)
                                    .broadcast_to([P, GROUP, HALF_E1]),
                                    pick[:, bass.ds(o, GROUP)].unsqueeze(2).broadcast_to([P, GROUP, HALF_E1]),
                                    ALU.is_equal).then_inc(oh1_ready, 1)
                    V.tensor_tensor(oh2[s].rearrange("p (m e) -> p m e", m=GROUP),
                                    iota.unsqueeze(1).broadcast_to([P, GROUP, P]),
                                    pick[:, bass.ds(o + T, GROUP)].unsqueeze(2).broadcast_to([P, GROUP, P]),
                                    ALU.is_equal).then_inc(oh2_ready, 1)

                def weigh(g, s, half=half):
                    n = g * 2 + (half * groups + s)
                    dve.wait_ge(gate_filled, n + 1)
                    w = gview[:, bass.ds(g * (2 * GROUP) + s * GROUP, GROUP), :]
                    V.tensor_tensor(w, bank(s).rearrange("p (m e) -> p m e", m=GROUP), w, ALU.mult).then_inc(weight_ready, 1)

                for s in range(2):
                    one_hots(0, s)
                dve.wait_ge(gelu_ready, (half + 1) * 2 * HALF_SLABS)
                with dve.Fori(1, groups // 2) as g:
                    for s in range(2):
                        weigh(g - 1, s)
                        one_hots(g, s)
                for s in range(2):
                    weigh(groups // 2 - 1, s)
                with dve.Fori(0, CHUNKS // 16) as i:
                    for j in range(16):
                        q = (2 * half + 1) * CHUNKS + j
                        low_part(dve, V, q, i)
                        dve.wait_ge(ghi_ready, i * 16 + (half * CHUNKS + j + 1))
                        V.tensor_tensor(g_lo[q % 2][:, :], gate[:, bass.ds(i * (16 * T) + j * T, T)],
                                        g_hi[q % 2][:, :].bitcast(F32), ALU.subtract).then_inc(glo_ready, 1)
            dve.wait_ge(peer_half, 2)
            residual(0, 5, 0, src=4)
            dve.wait_ge(x_updated, 2 * KD)

            dve.wait_ge(ctx2_loaded, 16)
            squares(3, hcT)
            squares(4, xT)
            norm(3, hcT, hcT, colv("g1"), modp(1, 1, 1))
            dve.wait_ge(norm_scaled, 4 * KD)
            norm(4, xT, hT, colv("g1"), modp(1, 1, 0))
            dve.wait_ge(small2_loaded, 48)
            b3 = bias2.rearrange("p (n k) -> p n k", k=64)
            step(V.tensor_tensor(b3, b3, const("near").unsqueeze(1).broadcast_to([P, 48, 64]), ALU.add))
            dve.wait_ge(bank_emptied, UNITS_B1 + UNITS_Q + UNITS_B2)
            cv2 = lambda t: t.rearrange("p (j t) -> p j t", j=2)
            step(V.tensor_tensor(ucv, gbc[:, 512:1024], hcv, ALU.mult))
            wc = colv("w_conv")
            for j in range(2):
                u, v = cv2(ucv)[:, j, :], cv2(vcv)[:, j, :]
                step(V.tensor_scalar(v, u, wc[:, 3 * j + 1:3 * j + 2], None, ALU.mult))
                step(V.scalar_tensor_tensor(out=v[:, 1:T], in0=u[:, 0:T - 1], scalar=wc[:, 3 * j:3 * j + 1],
                                            in1=v[:, 1:T], op0=ALU.mult, op1=ALU.add))
                step(V.scalar_tensor_tensor(out=v[:, 0:T - 1], in0=u[:, 1:T], scalar=wc[:, 3 * j + 2:3 * j + 3],
                                            in1=v[:, 0:T - 1], op0=ALU.mult, op1=ALU.add))
            V.tensor_tensor(catT[:, 1536:2048], gbc[:, 0:512], vcv, ALU.mult).then_inc(conv_ready, 1)
            attention(1, aN2)
            residual(1, 2, 2)
            dve.wait_ge(x_updated, 3 * KD)
            squares(5, xT)
            norm(5, xT, hT, colv("g2"), modp(1, 4))

            nr = NG + NE
            V.memset(lgp, BIG_NEG)
            for t in range(NT):
                dve.wait_ge(router_filled, t + 1)
                step(V.tensor_tensor(lg[:, 0:nr], bank(t, nr), rowv("b_router"), ALU.add))
                step(V.tensor_copy(lgp[:, 0:NG], lg[:, 0:NG]))
                step(V.max(m8, lgp))
                step(V.max_index(i8, m8, lgp))
                step(V.tensor_copy(gidx, i8[:, 0:1]))
                step(V.tensor_scalar(goh, iota[:, 0:NG], gidx, None, ALU.is_equal))
                V.tensor_scalar(gex, lg[:, 0:NG], m8[:, 0:1], None, ALU.subtract).then_inc(rexp_in, 1)
                el = lg[:, NG:nr].rearrange("p (g e) -> p g e", g=NG)
                es = esel4.rearrange("p (g e) -> p g e", g=NG)
                step(V.tensor_tensor(es, el, goh.unsqueeze(2).broadcast_to([P, NG, EPG]), ALU.mult))
                step(V.tensor_reduce(esel, esel4.rearrange("p (g e) -> p e g", g=NG), X, ALU.add))
                step(V.max(e8, esel))
                step(V.max_index(j8, e8, esel))
                step(V.tensor_copy(j8f, j8))
                V.tensor_scalar(pw[:, 0:2], e8[:, 0:2], e8[:, 0:1], None, ALU.subtract).then_inc(rexp_in, 1)
                dve.wait_ge(rexp_out, 2 * t + 2)
                step(V.tensor_tensor(pw[:, 2:3], pw[:, 2:3], gz, ALU.mult))
                step(V.reciprocal(pw[:, 2:3], pw[:, 2:3]))
                step(V.tensor_scalar(pw[:, 0:2], pw[:, 0:2], pw[:, 2:3], None, ALU.mult))
                for q in range(2):
                    step(V.tensor_scalar(s8[:, 8 * q:8 * q + 8], iota[:, 0:EPG], j8f[:, q:q + 1], None, ALU.is_equal))
                    step(V.tensor_scalar(c8[:, 8 * q:8 * q + 8], s8[:, 8 * q:8 * q + 8], pw[:, q:q + 1], None, ALU.mult))
                step(V.tensor_tensor(c8[:, 0:8], c8[:, 0:8], c8[:, 8:16], ALU.add))
                step(V.tensor_tensor(s8[:, 0:8], s8[:, 0:8], s8[:, 8:16], ALU.add))
                for dst, src in ((comb32, c8), (sel32, s8)):
                    step(V.tensor_tensor(dst[:, t * NE:(t + 1) * NE].rearrange("p (g e) -> p g e", g=NG),
                                         goh.unsqueeze(2).broadcast_to([P, NG, EPG]),
                                         src[:, 0:8].unsqueeze(1).broadcast_to([P, NG, EPG]), ALU.mult))
            V.engine_nop().then_inc(sel32_ready, 1)
            dve.wait_ge(counts_filled, 1)
            step(V.tensor_tensor(place, bank(6, 2 * NE), sel32, ALU.mult))
            step(V.tensor_scalar(place, place, -1.0, None, ALU.add))
            step(V.tensor_reduce(most, bank(6, NE, 2 * NE), X, ALU.max))
            step(V.tensor_scalar(roundf, iota[:, 0:MAX_ROUNDS], float(ROOM), None, ALU.mult))
            step(V.tensor_scalar(roundf, roundf, most, None, ALU.is_lt))
            step(V.tensor_reduce(most, roundf, X, ALU.add))
            V.tensor_copy(rounds[:, 0:1], most).then_inc(rounds_ready, 1)
            dve.wait_ge(rounds_ready, 1)

            n_rounds = dve.value_load(rounds[0:1, 0:1], min_val=1, max_val=MAX_ROUNDS)
            v4 = lambda a: a.rearrange("p (t e) -> p t e", t=NT)
            o4 = lambda a: a.rearrange("p (t e s) -> p t e s", t=NT, e=QUAD)
            spread = lambda a, q: v4(a)[:, :, bass.ds(q * QUAD, QUAD)].unsqueeze(3).broadcast_to([P, NT, QUAD, ROOM])
            places = iota[:, 0:ROOM].unsqueeze(1).unsqueeze(1).broadcast_to([P, NT, QUAD, ROOM])
            with dve.Fori(0, n_rounds) as r:
                with dve.Fori(0, QUADS) as q:
                    t = r * QUADS + q
                    dve.wait_ge(gathered, t + 1)
                    V.tensor_tensor(o4(sel), spread(place, q), places, ALU.is_equal).then_inc(sel_made, 1)
                    dve.wait_ge(sel_made, t + 1)
                    V.tensor_tensor(o4(selw), o4(sel), spread(comb32, q), ALU.mult).then_inc(sel_ready, 1)
                    dve.wait_ge(gathered, t + 2)
                    V.tensor_copy(xg[:, 0:512], bank(3)).then_inc(xg_low, 1)
                    dve.wait_ge(silu_ready, t + 1)
                    dve.wait_ge(hidden_filled, t * 2 + 2)
                    V.tensor_tensor(he, silg, bank(1), ALU.mult).then_inc(he_ready, 1)
                    dve.wait_ge(heT_filled, t + 1)
                    V.tensor_copy(heT, bank(2)).then_inc(heT_ready, 1)
                    dve.wait_ge(down_filled, t + 1)
                    V.tensor_copy(ye[:, 0:512], bank(3)).then_inc(ye_low, 1)
                V.tensor_scalar(place, place, -float(ROOM), None, ALU.add).then_inc(place_moved, 1)
                dve.wait_ge(place_moved, r + 1)
            dve.wait_ge(experts_done, 1)
            residual(1, 5, 0, src=4)
            dve.wait_ge(x_updated, 4 * KD)
            squares(6, xT)
            norm(6, xT, yfin, colv("g_final"), None)


NORM_SCALED = [KD * i for i in range(6)] + [6 * KD]
NORM_DONE = [KD * i for i in range(7)]


def constants():
    f = np.float32
    c = np.zeros((P, N_CONST), f)

    def put(name, a):
        o, w = CONSTS[name]
        c[:, o:o + w] = np.asarray(a, f).reshape(P, w)

    p = np.arange(P)
    put("ident", np.eye(P))
    put("ones", np.ones((P, P)))
    put("tri0", p[:, None] <= p[None, :])
    put("tri1", p[:, None] >= p[None, :])
    put("seen0", np.where(p[None, :] <= p[:, None], 0.0, NEG))
    put("seen1", np.where(p[None, :] >= p[:, None], 0.0, NEG))
    q = p[:, None] + P * np.arange(NT)[None, :]
    k = np.arange(T)
    put("window", np.where(np.abs(k[None, None, :] - q[:, :, None]) <= P, 0.0, NEG))
    qc, kc = p[:, None] % 64, np.arange(64)[None, :]
    first = np.clip(qc - 8, 0, 48)
    put("near", np.where((kc >= first) & (kc < first + 16), 0.0, NEG))
    tok = q
    inv = (10000.0 ** (-np.arange(16, dtype=f) / f(16))).astype(f)
    r = (tok // 64)[:, :, None].astype(f) * inv
    w = (tok % 64)[:, :, None].astype(f) * inv
    ang = np.concatenate([r, w], axis=-1)
    put("cos", np.cos(ang.astype(np.float64)))
    put("sin", np.sin(ang.astype(np.float64)))
    put("iota", np.broadcast_to(p[None, :], (P, P)))
    th = 2 * np.pi * (tok[:, :, None] * k[None, None, :] % T) / T
    put("dft_c", np.cos(th) / 16.0)
    put("dft_s", np.sin(th) / 16.0)
    j = np.arange(P)
    same = (j[:, None] // 64) == (j[None, :] // 64)
    th = 2 * np.pi * ((j[:, None] % 64) * (j[None, :] % 64) % 64) / 64
    put("dch_c", np.where(same, np.cos(th), 0) / 8.0)
    put("pairs", (p[:, None] % 32) == np.arange(2)[None, :])
    put("dch_s", np.where(same, -np.sin(th), 0) / 8.0)
    return c


def kernel(**inputs):
    import concourse.bacc as bacc
    from concourse.bass_utils import run_bass_kernel_spmd

    a = {k: np.asarray(v) for k, v in inputs.items()}

    def by_rows(w):
        return w.reshape(-1, P, w.shape[-1]).transpose(1, 0, 2)

    slabs = np.zeros((N_SLABS, P, SLAB), np.float32)

    def put(n, w):
        w = by_rows(w).reshape(P, -1)
        slabs[n, :, :w.shape[1]] = w

    for m, name in enumerate(("w_ada", "w_ada_2")):
        for s in range(ADA_SLABS):
            put(ada_slab(m * ADA_SLABS + s), a[name][0][:, s * 512:(s + 1) * 512])
    w = a["w_in"][0]
    put(S_Q, w[:, 0:512])
    put(S_K, w[:, 512:1024])
    put(S_V, w[:, 1024:1536])
    put(S_O, w[:, 1536:2048])
    put(S_GKV, np.concatenate([w[:, 2048:2064], w[:, 2576:2832]], axis=1))
    put(S_AQ, w[:, 2064:2576])
    for s in range(4):
        put(S_MG + s, w[:, 2832 + s * 512:2832 + (s + 1) * 512])
        put(S_QUERY + s, a["peer_w_query"][0][:, s * 512:(s + 1) * 512])
    put(S_BM, a["w_branch_m"][0])
    put(S_BA, a["w_branch_a"][0])
    for s in range(2):
        put(S_OUT + s, a["w_out"][0][:, s * 512:(s + 1) * 512])
        put(S_OUT2 + s, a["w_out_2"][0][:, s * 512:(s + 1) * 512])
    u = a["peer_u"][0].reshape(2 * HALF_SLABS, 512, KD, P).reshape(2 * HALF_SLABS, 4, P, KD, P).transpose(0, 4, 1, 3, 2).reshape(2 * HALF_SLABS, P, SLAB)
    v = a["peer_v"][0].reshape(2 * HALF_SLABS, 4, P, D).transpose(0, 2, 1, 3).reshape(2 * HALF_SLABS, P, SLAB)
    for half in range(2):
        s0 = S_PEER + 2 * half * HALF_SLABS
        slabs[s0:s0 + HALF_SLABS] = u[half * HALF_SLABS:(half + 1) * HALF_SLABS]
        slabs[s0 + HALF_SLABS:s0 + 2 * HALF_SLABS] = v[half * HALF_SLABS:(half + 1) * HALF_SLABS]
    w = a["w_in_2"][0]
    put(S_Q2, w[:, 256:768])
    put(S_K2, w[:, 768:1280])
    put(S_V2, w[:, 1280:1792])
    put(S_FH2, np.concatenate([w[:, 0:256], w[:, 2304:2560]], axis=1))
    put(S_G2, w[:, 1792:2304])
    for q in range(QUADS):
        es = slice(q * QUAD, (q + 1) * QUAD)
        s0 = S_MOE + q * Q_SLABS
        for b, name in enumerate(("w_gate_2", "w_up_2")):
            w = a[name][0, es].reshape(QUAD, 4, 2, P, 512).transpose(1, 3, 0, 2, 4)
            slabs[s0 + 4 * b:s0 + 4 * b + 4] = w.reshape(4, P, SLAB)
        w = a["w_down_2"][0, es].reshape(QUAD, 4, P, D).transpose(1, 2, 0, 3)
        slabs[s0 + 8:s0 + 12] = w.reshape(4, P, SLAB)

    def column(v):
        return v.reshape(-1, P).T

    def tokens(x):
        return x.T.reshape(KD, P, T).transpose(1, 0, 2).reshape(P, KD * T)

    cond = np.zeros((P, KD, 2, ROOM), np.float32)
    for i, n in enumerate(("c", "c_ctx", "c_2", "c_ctx_2")):
        cond[:, :, i // 2, i % 2] = column(a[n].reshape(-1))
    cond = cond.reshape(P, -1)
    cols = np.concatenate(
        [column(a[n].reshape(-1)) for n in ("b_ada", "b_ada_2", "norm_mix_g", "norm_ffn_g", "norm1_2", "norm2_2",
                                            "norm_final_2")]
        + [a["w_conv_2"][0].reshape(3, 2, P).transpose(2, 1, 0).reshape(P, 6)], axis=1)
    rows = np.concatenate([a[n].reshape(-1) for n in ("b_mgates", "mlstm_norm_g", "attn_q_norm_g", "attn_k_norm_g",
                                                      "attn_sink", "b_rg_2", "b_re_2")])
    rows = np.broadcast_to(rows, (P, N_ROW))
    subk = a["peer_sub_keys"][0].transpose(3, 0, 1, 2).reshape(P, -1)
    r2 = a["rpb_2"][0]
    shift = np.clip(np.arange(64)[None, :] - np.arange(64)[:, None] + 15, 0, 30)
    toe = r2[:, :, shift].transpose(2, 0, 1, 3)
    rpb = np.concatenate([toe[:, :, 5:11], toe[:, :, 4:10]], axis=0).reshape(P, -1)
    wr = by_rows(np.concatenate([a["w_rg_2"][0], a["w_re_2"][0]], axis=1)).reshape(P, -1)
    arrays = {
        "w_stream": slabs, "cond": cond, "x_t": tokens(a["x"][0]), "ctx_t": tokens(a["ctx"][0]),
        "ctx2_t": tokens(a["ctx_2"][0]), "consts": constants(), "cols": cols, "rows": rows, "sub_keys": subk,
        "rpb": rpb, "w_four": by_rows(a["w_fourier_2"][0]).reshape(P, -1), "w_router": wr,
    }
    arrays = {k: np.ascontiguousarray(v) for k, v in arrays.items()}
    nc = bacc.Bacc("TRN2", target_bir_lowering=False, num_devices=1)
    args = [nc.dram_tensor(k, v.shape, mybir.dt.from_np(v.dtype), kind="ExternalInput").ap() for k, v in arrays.items()]
    args.append(nc.dram_tensor("out", (P, KD * T), F32, kind="ExternalOutput").ap())
    two_block_kernel(nc, *args)
    r = run_bass_kernel_spmd(nc, [arrays], core_ids=[0])
    y = r.results[0]["out"]
    return np.ascontiguousarray(y.reshape(P, KD, T).transpose(2, 1, 0).reshape(1, T, D))
```

```python
from contextlib import ExitStack

import numpy as np

import concourse.bass as bass
from concourse import mybir

F32 = mybir.dt.float32
F32R = mybir.dt.float32r
U32 = mybir.dt.uint32
ALU = mybir.AluOpType
ACT = mybir.ActivationFunctionType
X = mybir.AxisListType.X

P = 128
D = 1024
KD = D // P
T = 256
NT = T // P
EPS = 1e-6
NEG = -1e30
BIG_NEG = -3.0e38
SLAB = 4096
SLOTS = 4

HEADS = 4
KEY_SCALE = float(P) ** -0.5
AH = 8
DH = 64
ATT_SCALE = float(DH) ** -0.5
UNITS = NT * AH

RH = 8
TOPK = 16
NKEY = 128
HALF_E1 = NKEY // 2
GROUP = 8

NG = 4
EPG = 8
NE = NG * EPG
QUAD = 4
ROOM = 32
QUADS = NE // QUAD
MAX_ROUNDS = T // ROOM
OUT_PARTS = 4
Q_SLABS = 12

ADA_SLABS = 6 * D // 512
ADA_FIRST = 4
S_ADA = 0
S_K, S_V, S_GKV, S_Q, S_AQ, S_O, S_MG = (ADA_FIRST + i for i in range(7))
S_ADA2 = S_MG + 4
S_BM = S_ADA2 + ADA_SLABS - ADA_FIRST
S_BA = S_BM + 1
S_OUT = S_BA + 1
S_QUERY = S_OUT + 2
S_PEER = S_QUERY + 4
HALF_SLABS = HALF_E1 // 4
S_ADA3 = S_PEER + HALF_SLABS
S_K2 = S_PEER + 4 * HALF_SLABS + ADA_SLABS
S_V2, S_Q2, S_FH2, S_G2 = (S_K2 + i for i in range(1, 5))
S_OUT2 = S_G2 + 1
S_MOE = S_OUT2 + 2
N_SLABS = S_MOE + QUADS * Q_SLABS

CONSTS = {}
_n = 0
for _name, _w in (("ident", P), ("ones", P), ("tri0", P), ("tri1", P), ("seen0", P), ("seen1", P),
                  ("window", NT * T), ("near", DH), ("cos", NT * 32), ("sin", NT * 32), ("iota", P),
                  ("dft_c", NT * T), ("dft_s", NT * T), ("dch_c", P), ("dch_s", P), ("pairs", 2)):
    CONSTS[_name] = (_n, _w)
    _n += _w
N_CONST = _n

COLS = {}
_n = 0
for _name, _w in (("b_ada", 2 * 6 * KD), ("g_mix", KD), ("g_ffn", KD), ("g1", KD), ("g2", KD),
                  ("g_final", KD), ("w_conv", 6)):
    COLS[_name] = (_n, _w)
    _n += _w
N_COL = _n
ROWS = {}
_n = 0
for _name, _w in (("b_gates", 16), ("g_mlstm", 512), ("g_q", DH), ("g_k", DH), ("sink", AH),
                  ("b_router", NG + NE)):
    ROWS[_name] = (_n, _w)
    _n += _w
N_ROW = _n


def ada_slab(n):
    if n < ADA_FIRST:
        return S_ADA + n
    return S_ADA2 + n - ADA_FIRST if n < ADA_SLABS else S_ADA3 + n - ADA_SLABS


CHUNKS = 4 * HALF_SLABS


GP_CHUNKS = CHUNKS - 16


def chunk_slab(q):
    return S_PEER + q // 4 + (ADA_SLABS if q >= CHUNKS else 0)


def two_block_kernel(nc, w_stream, cond, x_t, ctx_t, ctx2_t, consts, cols, rows, sub_keys, rpb,
                     w_four, w_router, out):
    with ExitStack() as ctx:
        def sb(name, n, dt=F32):
            return ctx.enter_context(nc.sbuf_tensor(name, [P, n], dt))

        def sem(name):
            return ctx.enter_context(nc.semaphore(name))

        def placed(name, n, dt=F32):
            o = -(-nc.sbuf_base // 32) * 32
            return sb(name, n, dt), o

        def over(name, n, offset):
            return nc.alloc_sbuf_tensor_at(name, [P, n], F32R, offset=offset)

        slab, slab_lo = [], []
        for i in range(SLOTS):
            t, o = placed(f"slab{i}", SLAB)
            slab.append(t)
            slab_lo.append(over(f"slab_lo{i}", SLAB, o))
        big, o_big = placed("big", 20080)
        scratch = sb("scratch", 4096)
        xT = sb("xT", KD * T)
        hT, o_hT = placed("hT", KD * T)
        hcT, o_hcT = placed("hcT", KD * T)
        cst = sb("cst", N_CONST)
        col = sb("col", N_COL)
        row = sb("row", N_ROW)
        conds = sb("conds", KD * 2 * ROOM)
        mod = sb("mod", 2 * 6 * KD * 2)
        gain = sb("gain", KD)
        rstd = sb("rstd", T)
        stat = sb("stat", 4 * 2 * UNITS)
        small = sb("small", 640)
        pick = sb("pick", 3 * T)
        ps = ctx.enter_context(nc.psum_tensor("ps", [P, 8 * 512], F32))

        def bank(b, n=512, at=0):
            return ps[:, b * 512 + at:b * 512 + at + n]

        def const(name):
            o, w = CONSTS[name]
            return cst[:, o:o + w]

        def colv(name):
            o, w = COLS[name]
            return col[:, o:o + w]

        def rowv(name):
            o, w = ROWS[name]
            return row[:, o:o + w]

        def at(t, o, n):
            return t[:, o:o + n]

        ident, ones, iota = const("ident"), const("ones"), const("iota")

        def modc(block, part, j, who=0):
            c = ((block * 6 + part) * KD + j) * 2 + who
            return mod[:, c:c + 1]

        def modp(block, part, who=0):
            c = (block * 6 + part) * KD * 2 + who
            return mod[:, c:c + 2 * KD - 1:2]

        qT = at(big, 0, 1024)
        kN = at(big, 1024, 2048)
        kTl = at(big, 3072, 1024)
        vA = at(big, 4096, 4 * HEADS * 129).rearrange("p (c h v) -> p c h v", c=4, h=HEADS)
        sigO = at(big, 6160, 1024)
        gat = at(big, 7184, 64)
        aqN = at(big, 7248, 1024)
        akN = at(big, 8272, 512)
        avN = at(big, 8784, 512)
        qR = at(big, 9296, 1024)
        kR = at(big, 10320, 512)
        kSw = at(big, 10832, 512)
        qTa = at(big, 11344, 1024)
        kTa = at(big, 12368, 1024)
        hN = at(big, 13392, 1024)
        pair = [at(big, 14416, 512), at(big, 14928, 512)]
        state = [[at(big, 15440 + (2 * v + d) * 516, 516).rearrange("p (h v) -> p h v", h=HEADS)
                  for d in range(2)] for v in range(2)]
        t1 = at(big, 17504, 516).rearrange("p (h v) -> p h v", h=HEADS)
        t2 = at(big, 18020, 516).rearrange("p (h v) -> p h v", h=HEADS)
        probsT = [at(big, 19052, 512), at(big, 19564, 512), at(hcT, 1536, 512)]
        decay = hcT
        logit = [at(hT, 0, 512), at(hT, 512, 512), at(hcT, 512, 512)]
        probs = [at(hT, 1024, 512), at(hT, 1536, 512), at(hcT, 1024, 512)]
        aN = at(big, 0, 1024)
        mT = at(big, 1024, 1024)
        aT = at(big, 2048, 1024)
        merged = at(big, 3072, 2048)
        tmpm = [at(big, 5120, 512), at(big, 5632, 512)]
        sigG = scratch
        qTr = at(big, 0, 4096)
        subk = at(big, 4096, 2048)
        sc = [at(scratch, 0, 2048), at(scratch, 2048, 2048)]
        R0 = HALF_E1 * T + 2048
        top1 = at(big, R0, 256)
        idx1 = at(big, R0 + 256, 256)
        top2 = at(big, R0 + 512, 128)
        pos = at(big, R0 + 640, 128)
        posa = at(big, R0 + 768, 128)
        choice = [at(big, R0 + 1024, 384), at(small, 0, 384)]
        zsum = at(big, R0 + 1408, 16)
        ada_rows2 = at(scratch, 3072, 512)
        gate = at(big, 0, HALF_E1 * T)
        CHUNK = 1024
        h_hi = over("h_hi", KD * T, o_hcT)
        h_lo = over("h_lo", KD * T, o_hT)
        PIECE = CHUNK // 2
        w_hi = [over(f"w_hi{i}", PIECE, o_big + 4 * (HALF_E1 * T + i * PIECE)) for i in range(4)]
        g_hi = [over(f"g_hi{i}", T, o_big + 4 * (18432 + i * T)) for i in range(2)]
        g_lo = [over(f"g_lo{i}", T, o_big + 4 * (18944 + i * T)) for i in range(2)]
        oh2 = [at(scratch, 0, 1024), at(scratch, 1024, 1024)]
        oh1 = [at(scratch, 2048, 512), at(scratch, 2560, 512)]
        kT2 = at(big, 0, 2048)
        vN2 = at(big, 2048, 2048)
        qT2 = at(big, 4096, 1024)
        fN = at(big, 5120, 512)
        hcv = at(big, 5632, 512)
        gbc = at(big, 6144, 1024)
        tCS = at(big, 7168, 1024)
        foT = at(big, 8192, 512)
        catT = at(big, 8704, 2048)
        aN2 = at(big, 10752, 1024)
        ucv = at(big, 11776, 512)
        vcv = at(big, 12288, 512)
        bias2 = at(big, 12800, 3072)
        wf = at(big, 15872, 512)
        wr = at(big, 16384, KD * (NG + NE))
        xN = at(big, 0, NT * D)
        sel = at(big, 2048, 256)
        selw = at(big, 2304, 256)
        selT = at(big, 2560, 256)
        xg = at(big, 2816, 1024)
        silg = at(big, 3840, 512)
        he = at(big, 4352, 512)
        heT = at(big, 4864, 512)
        ye = at(big, 5376, 1024)
        yfin = at(big, 0, 2048)
        M0 = 13312
        lg = at(big, M0, 40)
        lgp = at(big, M0 + 40, 8)
        m8 = at(big, M0 + 48, 8)
        i8 = at(big, M0 + 56, 8).bitcast(U32)
        gidx = at(big, M0 + 64, 1)
        goh = at(big, M0 + 68, 4)
        gex = at(big, M0 + 76, 4)
        gz = at(big, M0 + 80, 1)
        esel = at(big, M0 + 88, 8)
        esel4 = at(big, M0 + 96, 32)
        e8 = at(big, M0 + 128, 8)
        j8 = at(big, M0 + 136, 8).bitcast(U32)
        j8f = at(big, M0 + 144, 8)
        pw = at(big, M0 + 152, 4)
        s8 = at(big, M0 + 160, 16)
        c8 = at(big, M0 + 176, 16)
        comb32 = at(big, M0 + 192, 64)
        sel32 = at(big, M0 + 256, 64)
        place = at(big, M0 + 320, 64)
        most = at(big, M0 + 384, 1)
        roundf = at(big, M0 + 392, 8)
        rounds = at(big, M0 + 400, 2).bitcast(U32)
        slab_loaded = [sem(f"slab_loaded{i}") for i in range(SLOTS)]
        slab_used = sem("slab_used")
        cond_loaded = sem("cond_loaded")
        inputs_loaded = sem("inputs_loaded")
        subk_loaded = sem("subk_loaded")
        ctx2_loaded = sem("ctx2_loaded")
        small2_loaded = sem("small2_loaded")
        out_stored = sem("out_stored")
        cond_ready = sem("cond_ready")
        mod_filled = sem("mod_filled")
        mod_stored = sem("mod_stored")
        norm_sq = sem("norm_sq")
        norm_sum = sem("norm_sum")
        norm_inv = sem("norm_inv")
        norm_rstd = sem("norm_rstd")
        norm_scaled = sem("norm_scaled")
        norm_done = sem("norm_done")
        bank_filled = sem("bank_filled")
        bank_emptied = sem("bank_emptied")
        gates_biased = sem("gates_biased")
        soft_ready = sem("soft_ready")
        lf_ready = sem("lf_ready")
        cums_filled = sem("cums_filled")
        diag_ready = sem("diag_ready")
        rrow_filled = sem("rrow_filled")
        rrow_used = sem("rrow_used")
        exps_in = sem("exps_in")
        exps_out = sem("exps_out")
        kw_ready = sem("kw_ready")
        cloc_filled = sem("cloc_filled")
        cloc_used = sem("cloc_used")
        kT_filled = sem("kT_filled")
        kT_stored = sem("kT_stored")
        qk_filled = sem("qk_filled")
        decay_in = sem("decay_in")
        decay_out = sem("decay_out")
        smat_ready = sem("smat_ready")
        smatT_filled = sem("smatT_filled")
        smatT_stored = sem("smatT_stored")
        num_filled = sem("num_filled")
        num_used = sem("num_used")
        hms_ready = sem("hms_ready")
        hrstd_ready = sem("hrstd_ready")
        m_ready = sem("m_ready")
        turn_filled = sem("turn_filled")
        turn_stored = sem("turn_stored")
        qkms_ready = sem("qkms_ready")
        qkrstd_ready = sem("qkrstd_ready")
        roped = sem("roped")
        scores_filled = sem("scores_filled")
        scaled = sem("scaled")
        logits_ready = sem("logits_ready")
        probs_ready = sem("probs_ready")
        sink_ready = sem("sink_ready")
        probsT_filled = sem("probsT_filled")
        probsT_stored = sem("probsT_stored")
        head_filled = sem("head_filled")
        head_stored = sem("head_stored")
        branch_filled = sem("branch_filled")
        merged_ready = sem("merged_ready")
        y_filled = sem("y_filled")
        x_updated = sem("x_updated")
        rscores_filled = sem("rscores_filled")
        rscores_stored = sem("rscores_stored")
        top_ready = sem("top_ready")
        texp_ready = sem("texp_ready")
        choice_ready = sem("choice_ready")
        choiceT_filled = sem("choiceT_filled")
        pick_ready = sem("pick_ready")
        oh1_ready = sem("oh1_ready")
        oh2_ready = sem("oh2_ready")
        ohw_ready = sem("ohw_ready")
        gate_filled = sem("gate_filled")
        gate_stored = sem("gate_stored")
        h_hi_ready = sem("h_hi_ready")
        h_lo_ready = sem("h_lo_ready")
        hi_ready = sem("hi_ready")
        lo_ready = sem("lo_ready")
        lo_ready_gp = sem("lo_ready_gp")
        ghi_ready = sem("ghi_ready")
        glo_ready = sem("glo_ready")
        piece_used = sem("piece_used")
        gelu_ready = sem("gelu_ready")
        weight_ready = sem("weight_ready")
        peer_half = sem("peer_half")
        conv_ready = sem("conv_ready")
        four_filled = sem("four_filled")
        four_stored = sem("four_stored")
        router_filled = sem("router_filled")
        rexp_in = sem("rexp_in")
        rexp_out = sem("rexp_out")
        adarow_filled = sem("adarow_filled")
        adarow_stored = sem("adarow_stored")
        counts_filled = sem("counts_filled")
        sel32_ready = sem("sel32_ready")
        rounds_ready = sem("rounds_ready")
        sel_ready = sem("sel_ready")
        gathered = sem("gathered")
        xg_low = sem("xg_low")
        xg_high = sem("xg_high")
        hidden_filled = sem("hidden_filled")
        silu_ready = sem("silu_ready")
        he_ready = sem("he_ready")
        heT_filled = sem("heT_filled")
        heT_ready = sem("heT_ready")
        down_filled = sem("down_filled")
        ye_low = sem("ye_low")
        ye_high = sem("ye_high")
        scattered = sem("scattered")
        sel_made = sem("sel_made")
        place_moved = sem("place_moved")
        experts_done = sem("experts_done")
        zeros_ready = sem("zeros_ready")
        dve_step = sem("dve_step")
        act_step = sem("act_step")
        pool_step = sem("pool_step")

        block = ctx.enter_context(nc.Block())

        UNITS_B1 = 4 + 4 + 4 + 2 + 2 + 2 + 8
        UNITS_RING = 4 + 4 + 4 + 2
        UNITS_Q = 8

        def norm_bank(i):
            return (4, 5, 6, 1, 2, 7, 2)[i]

        def unit_bank(u):
            return 6 + u % 2 if UNITS_RING <= u < UNITS_B1 else u % 8
        UNITS_B2 = 14

        @block.sync
        def _(sp):
            def load(n, slot, value):
                if value is not None:
                    sp.wait_ge(slab_used, value)
                sp.dma_start(slab[slot][:, :], w_stream[n]).then_inc(slab_loaded[slot], 16)

            sp.dma_start(conds[:, :], cond).then_inc(cond_loaded, 16)
            load(0, 0, None)
            for dst, src in ((xT, x_t), (hcT, ctx_t), (col, cols), (row, rows), (cst, consts)):
                sp.dma_start(dst[:, :], src).then_inc(inputs_loaded, 16)
            for s in range(1, SLOTS):
                load(s, s, None)
            whole = S_MOE // SLOTS
            with sp.Fori(1, whole) as i:
                for s in range(SLOTS):
                    load(i * SLOTS + s, s, i * SLOTS + (s - SLOTS + 1))
            for n in range(whole * SLOTS, S_MOE):
                load(n, n % SLOTS, n - SLOTS + 1)

            def expert_round(r):
                turns = QUADS * Q_SLABS // SLOTS
                with sp.Fori(0, turns) as i:
                    for s in range(SLOTS):
                        n = i * SLOTS + (S_MOE + s)
                        used_before = n - SLOTS + 1 + r * (turns * SLOTS)
                        load(n, (S_MOE + s) % SLOTS, used_before)

            expert_round(0)
            sp.wait_ge(rounds_ready, 1)
            n_rounds = sp.value_load(rounds[0:1, 0:1], min_val=1, max_val=MAX_ROUNDS)
            with sp.If(n_rounds > 1):
                with sp.Fori(1, n_rounds) as r:
                    expert_round(r)

        def low_part(engine, ops, q, i, signal):
            n = chunk_slab(q)
            for h in range(2):
                o = (q % 4) * CHUNK + h * PIECE
                b = (2 * q + h) % 4
                engine.wait_ge(hi_ready, i * 32 + (2 * q + h + 1))
                ops.tensor_tensor(slab_lo[n % SLOTS][:, o:o + PIECE], slab[n % SLOTS][:, o:o + PIECE],
                                  w_hi[b][:, :].bitcast(F32), ALU.subtract).then_inc(signal, 1)

        @block.gpsimd
        def _(pool):
            with pool.Fori(0, CHUNKS // 16 - 1) as i:
                for j in range(16):
                    low_part(pool, nc.gpsimd, j, i, lo_ready_gp)
            pool.wait_ge(pick_ready, NT)
            groups = T // GROUP
            for half in range(2):
                with pool.Fori(0, groups // 2) as g:
                    for s in range(2):
                        pool.wait_ge(oh1_ready, g * 2 + (half * groups + s + 1))
                        o1 = oh1[s].rearrange("p (m e) -> p m e", m=GROUP)
                        nc.gpsimd.tensor_tensor(
                            o1, o1, pick[:, bass.ds(g * (2 * GROUP) + (s * GROUP + 2 * T), GROUP)].unsqueeze(2)
                            .broadcast_to([P, GROUP, HALF_E1]), ALU.mult).then_inc(ohw_ready, 1)

        @block.scalar
        def _(act):
            steps = [0]

            def step(ins):
                steps[0] += 1
                ins.then_inc(act_step, 1)
                act.wait_ge(act_step, steps[0])

            act.wait_ge(cond_loaded, 16)
            nc.scalar.activation(conds[:, :], conds[:, :], ACT.Silu).then_inc(cond_ready, 1)

            def ada_row(n, buf, b=6):
                act.wait_ge(adarow_filled, n + 1)
                nc.scalar.activation(buf, bank(b), ACT.Copy).then_inc(adarow_stored, 1)

            for n in range(ADA_FIRST):
                ada_row(n, big[:, 0:512])

            def norm(i, dst, shift):
                act.wait_ge(norm_inv, i + 1)
                nc.scalar.activation(rstd[:, :], rstd[:, :], ACT.Sqrt).then_inc(norm_rstd, 1)
                if shift is not None:
                    for k in range(KD):
                        act.wait_ge(norm_scaled, NORM_SCALED[i] + k + 1)
                        nc.scalar.activation(dst[:, k * T:(k + 1) * T], dst[:, k * T:(k + 1) * T],
                                             ACT.Identity, bias=shift(k)).then_inc(norm_done, 1)

            unit = [0]

            def empty(dst, func=ACT.Copy, scale=1.0, src=None):
                u = unit[0]
                unit[0] += 1
                act.wait_ge(bank_filled, u + 1)
                b = unit_bank(u)
                nc.scalar.activation(dst, bank(b) if src is None else src(b), func,
                                     scale=scale).then_inc(bank_emptied, 1)

            norm(0, hT, lambda k: modc(0, 0, k, 0))
            norm(1, hcT, lambda k: modc(0, 0, k, 1))
            for c in (2, 3, 0, 1):
                empty(kN[:, c * 512:(c + 1) * 512], scale=KEY_SCALE)
            for c in (2, 3, 0, 1):
                empty(vA[:, c, :, 0:P], src=lambda b: bank(b).rearrange("p (h v) -> p h v", h=HEADS))
            for c in (2, 3, 0, 1):
                u = unit[0]
                unit[0] += 1
                act.wait_ge(bank_filled, u + 1)
                nc.scalar.activation(gat[:, c * 16:(c + 1) * 16], bank(u % 8, 16), ACT.Copy)
                nc.scalar.activation(akN[:, c * P:(c + 1) * P], bank(u % 8, P, 16), ACT.Copy)
                nc.scalar.activation(avN[:, c * P:(c + 1) * P], bank(u % 8, P, 16 + P),
                                     ACT.Copy).then_inc(bank_emptied, 1)
            for c in range(2):
                empty(qT[:, c * 512:(c + 1) * 512])
            soft = small[:, 64:96]
            act.wait_ge(gates_biased, 1)
            step(nc.scalar.activation(soft, small[:, 32:64], ACT.Abs))
            step(nc.scalar.activation(soft, soft, ACT.Exp, scale=-1.0))
            nc.scalar.activation(soft, soft, ACT.Ln, bias=1.0).then_inc(soft_ready, 1)
            for c in range(2):
                act.wait_ge(kT_filled, c + 1)
                nc.scalar.activation(
                    kTl.rearrange("p (h t) -> p h t", h=HEADS)[:, :, c * P:(c + 1) * P],
                    bank(6 + c).rearrange("p (h t) -> p h t", h=HEADS), ACT.Copy).then_inc(kT_stored, 1)
            for c in range(2):
                empty(aqN[:, c * 512:(c + 1) * 512])
            for c in range(2):
                empty(sigO[:, c * 512:(c + 1) * 512], ACT.Sigmoid)

            def merge_gates(c):
                empty(sigG[:, c * 512:(c + 1) * 512], ACT.Sigmoid)

            merge_gates(0)
            act.wait_ge(exps_in, 1)
            nc.scalar.activation(small[:, 400:504], small[:, 296:400], ACT.Exp).then_inc(exps_out, 1)
            act.wait_ge(decay_in, 4)
            nc.scalar.activation(decay[:, :], decay[:, :], ACT.Exp).then_inc(decay_out, 1)
            for c in range(1, 4):
                merge_gates(c)
            for n in range(4):
                act.wait_ge(smatT_filled, n + 1)
                if n >= 2:
                    act.wait_ge(num_filled, n - 1)
                else:
                    act.wait_ge(cloc_filled, 6)
                nc.scalar.activation(pair[n % 2], bank(1 + n % 2), ACT.Copy).then_inc(smatT_stored, 1)
            act.wait_ge(hms_ready, 1)
            nc.scalar.activation(small[:, 512:520], small[:, 512:520], ACT.Sqrt).then_inc(hrstd_ready, 1)
            act.wait_ge(qkms_ready, 1)
            nc.scalar.activation(small[:, 520:544], small[:, 520:544], ACT.Sqrt).then_inc(qkrstd_ready, 1)

            for c in range(4, 8):
                merge_gates(c)

            def turned(n, dst):
                act.wait_ge(turn_filled, n + 1)
                nc.scalar.activation(dst, bank(n % 8), ACT.Copy).then_inc(turn_stored, 1)

            for n in range(2):
                turned(n, qTa[:, n * 512:(n + 1) * 512])
            for n in range(2):
                turned(2 + n, kTa[:, n * 512:(n + 1) * 512])

            def attention(blk):
                def softmax(u):
                    st = stat[:, 4 * u:4 * u + 4]
                    act.wait_ge(logits_ready, u + 1)
                    if u >= 3:
                        act.wait_ge(probsT_filled, u - 2)
                    nc.scalar.activation(probs[u % 3], logit[u % 3], ACT.Exp, bias=st[:, 0:1],
                                         accum_out=st[:, 1:2]).then_inc(probs_ready, 1)
                    if blk == 0:
                        h = u % AH
                        nc.scalar.activation(st[:, 2:3], rowv("sink")[:, h:h + 1], ACT.Exp,
                                             bias=st[:, 0:1]).then_inc(sink_ready, 1)

                def store_turned(u):
                    act.wait_ge(probsT_filled, u + 1)
                    if u >= 3:
                        act.wait_ge(head_filled, u - 2)
                    nc.scalar.activation(probsT[u % 3], bank(2 + u % 2), ACT.Copy).then_inc(probsT_stored, 1)

                first = blk * UNITS
                softmax(first)
                for u in range(first, first + UNITS):
                    if u + 1 < first + UNITS:
                        softmax(u + 1)
                    store_turned(u)
                    if blk == 0 and u % 2 == 0:
                        ada_row(ADA_FIRST + u // 2, hcT[:, 0:512])

            attention(0)
            for n in range(2):
                turned(4 + n, mT[:, n * 512:(n + 1) * 512])
            for n in range(2):
                turned(6 + n, aT[:, n * 512:(n + 1) * 512])
            act.wait_ge(y_filled, 2)
            act.dma_start(subk, sub_keys).then_inc(subk_loaded, 16)
            norm(2, hT, lambda k: modc(0, 3, k, 0))
            act.wait_ge(norm_done, 3 * KD)
            nc.scalar.activation(h_hi[:, :], hT[:, :], ACT.Copy).then_inc(h_hi_ready, 1)
            for c in range(8):
                empty(qTr[:, c * 512:(c + 1) * 512])
            for t in range(NT):
                for b in range(4):
                    act.wait_ge(rscores_filled, t * 4 + b + 1)
                    nc.scalar.activation(sc[t][:, b * 512:(b + 1) * 512], bank(4 * t + b),
                                         ACT.Copy).then_inc(rscores_stored, 1)
            def high(q, i=0):
                n = chunk_slab(q)
                act.wait_ge(slab_loaded[n % SLOTS], i * 16 + 16 * (n // SLOTS + 1))
                for h in range(2):
                    p = 2 * q + h
                    if not (isinstance(i, int) and p < 4):
                        act.wait_ge(piece_used, i * 32 + (p - 3))
                    o = (q % 4) * CHUNK + h * PIECE
                    nc.scalar.activation(w_hi[p % 4][:, :], slab[n % SLOTS][:, o:o + PIECE],
                                         ACT.Copy).then_inc(hi_ready, 1)

            def activations(half):
                q0 = 2 * half * CHUNKS

                def turn_(i, stop=18):
                    for p in range(8):
                        if 2 * p + 2 < stop:
                            high(q0 + 2 * p + 2, i)
                            high(q0 + 2 * p + 3, i)
                        act.wait_ge(piece_used, i * 32 + 2 * (q0 + 2 * p + 2))
                        if half:
                            act.wait_ge(peer_half, half)
                        nc.scalar.activation(gate[:, bass.ds(i * (16 * T) + p * 512, 512)] if not isinstance(i, int)
                                             else gate[:, i * 16 * T + p * 512:i * 16 * T + (p + 1) * 512],
                                             bank(p % 4), ACT.Gelu_apprx_tanh).then_inc(gelu_ready, 1)

                if half == 0:
                    high(0)
                    high(1)
                with act.Fori(0, CHUNKS // 16 - (half == 0)) as i:
                    turn_(i)
                if half == 0:
                    turn_(CHUNKS // 16 - 1, 16)

            def weights_high(half):
                q0 = (2 * half + 1) * CHUNKS
                act.wait_ge(weight_ready, (half + 1) * (T // GROUP))

                def weight_high(q, i=0):
                    o = (q - q0) * T
                    src = gate[:, bass.ds(i * (16 * T) + o, T)] if not isinstance(i, int) else \
                        gate[:, i * 16 * T + o:i * 16 * T + o + T]
                    act.wait_ge(piece_used, i * 32 + 2 * (q - 1))
                    nc.scalar.activation(g_hi[q % 2][:, :], src, ACT.Copy).then_inc(ghi_ready, 1)

                for j in range(2):
                    if half == 0:
                        high(q0 + j)
                    weight_high(q0 + j)
                last = CHUNKS // 16 - 1
                with act.Fori(0, last) as i:
                    for j in range(2, 18):
                        high(q0 + j, i)
                        weight_high(q0 + j, i)
                for j in range(2, 18):
                    if half == 0 or j < 16:
                        high(q0 + j, last)
                    if j < 16:
                        weight_high(q0 + j, last)

            activations(0)
            act.wait_ge(top_ready, NT)
            for t in range(NT):
                nc.scalar.activation(choice[t][:, 256:384], choice[t][:, 256:384], ACT.Exp).then_inc(texp_ready, 1)
            pview = pick.rearrange("p (i m) -> p i m", i=3)
            for t in range(NT):
                act.wait_ge(choiceT_filled, t + 1)
                nc.scalar.activation(pview[:, :, t * P:(t + 1) * P], bank(t, 384).rearrange("p (i m) -> p i m", i=3),
                                     ACT.Copy).then_inc(pick_ready, 1)
            with act.Fori(0, ADA_SLABS // SLOTS) as i:
                for j in range(SLOTS):
                    ada_row(i * SLOTS + (ADA_SLABS + j), ada_rows2, 2)
            weights_high(0)
            activations(1)
            act.dma_start(hcT[:, :], ctx2_t).then_inc(ctx2_loaded, 16)
            weights_high(1)

            act.wait_ge(peer_half, 2)
            for dst, src in ((bias2, rpb), (wf, w_four), (wr, w_router)):
                act.dma_start(dst, src).then_inc(small2_loaded, 16)
            norm(3, hcT, lambda k: modc(1, 0, k, 1))
            norm(4, hT, lambda k: modc(1, 0, k, 0))
            for c in range(4):
                empty(kT2[:, c * 512:(c + 1) * 512])
            for c in range(4):
                empty(vN2[:, c * 512:(c + 1) * 512])
            for c in range(2):
                empty(qT2[:, c * 512:(c + 1) * 512])
            empty(fN)
            empty(hcv)
            for c in range(2):
                empty(gbc[:, c * 512:(c + 1) * 512])
            for n, dst in enumerate((tCS[:, 0:512], tCS[:, 512:1024], foT, catT[:, 0:512])):
                act.wait_ge(four_filled, n + 1)
                nc.scalar.activation(dst, bank(n % 2), ACT.Copy).then_inc(four_stored, 1)
            attention(1)
            for n in range(2):
                turned(8 + n, catT[:, (1 + n) * 512:(2 + n) * 512])
            norm(5, hT, lambda k: modc(1, 3, k, 0))
            for t in range(NT):
                act.wait_ge(rexp_in, 2 * t + 1)
                nc.scalar.activation(gex, gex, ACT.Exp, accum_out=gz).then_inc(rexp_out, 1)
                act.wait_ge(rexp_in, 2 * t + 2)
                nc.scalar.activation(pw[:, 0:2], pw[:, 0:2], ACT.Exp,
                                     accum_out=pw[:, 2:3]).then_inc(rexp_out, 1)
            for n in range(4):
                turned(10 + n, xN[:, n * 512:(n + 1) * 512])
            act.wait_ge(rounds_ready, 1)
            n_rounds = act.value_load(rounds[0:1, 0:1], min_val=1, max_val=MAX_ROUNDS)
            with act.Fori(0, n_rounds) as r:
                with act.Fori(0, QUADS) as q:
                    t = r * QUADS + q
                    act.wait_ge(gathered, t + 2)
                    act.wait_ge(scattered, t + 1)
                    nc.scalar.activation(selT, bank(2, 256), ACT.Copy)
                    nc.scalar.activation(xg[:, 512:1024], bank(0), ACT.Copy).then_inc(xg_high, 1)
                    act.wait_ge(hidden_filled, t * 2 + 1)
                    nc.scalar.activation(silg, bank(0), ACT.Silu).then_inc(silu_ready, 1)
                    act.wait_ge(down_filled, t + 1)
                    nc.scalar.activation(ye[:, 512:1024], bank(1), ACT.Copy).then_inc(ye_high, 1)
            norm(6, None, None)
            for q in range(OUT_PARTS):
                act.wait_ge(norm_done, NORM_DONE[6] + (q + 1) * KD // OUT_PARTS)
                c = slice(q * KD * T // OUT_PARTS, (q + 1) * KD * T // OUT_PARTS)
                act.dma_start(out[:, c], yfin[:, c]).then_inc(out_stored, 16)
            act.wait_ge(out_stored, 16 * OUT_PARTS)

        @block.tensor
        def _(pe):
            def weights(n, i=None):
                v = 16 * (n // SLOTS + 1)
                pe.wait_ge(slab_loaded[n % SLOTS], v if i is None else i * 16 + v)
                return slab[n % SLOTS]

            spent = [False]

            def release():
                pe.sem_inc(slab_used, 1)

            def mm(*a, signal=None, **kw):
                ins = nc.tensor.matmul(*a, **kw)
                if signal is not None:
                    ins.then_inc(signal, 1)
                elif spent[0]:
                    ins.then_inc(slab_used, 1)
                    spent[0] = False

            def slab_done():
                assert not spent[0]
                spent[0] = True

            def chain(dst, pairs, signal=None):
                for k, (a, b) in enumerate(pairs):
                    last = k == len(pairs) - 1
                    mm(dst, a, b, start=k == 0, stop=last, signal=signal if last else None)

            pe.wait_ge(cond_ready, 1)
            cnd = conds.rearrange("p (k m c) -> p k m c", k=KD, m=2)

            def ada_rows(w, m, b=6):
                w = w.rearrange("p (k n) -> p k n", k=KD)
                for k in range(KD):
                    j = k % 4
                    mm(ps[32 * j:32 * j + 32, b * 512:(b + 1) * 512], cnd[:, k, m, :], w[:, k, :],
                       start=k < 4, stop=k >= 4, signal=adarow_filled if k == KD - 1 else None)
                slab_done()

            def ada_turn(n, buf, o=7 * 512):
                pe.wait_ge(adarow_stored, n + 1)
                if isinstance(n, int) and n:
                    pe.wait_ge(mod_stored, n)
                for j in range(4):
                    mm(ps[:, bass.ds(o + 2 * j, 2)], buf[:, j * P:(j + 1) * P], const("pairs"), start=True, stop=True,
                       signal=mod_filled if j == 3 else None)

            def norm(i):
                b = norm_bank(i)
                sq = scratch[:, (i % 2) * 2048:(i % 2) * 2048 + 2048]
                for k in range(KD):
                    pe.wait_ge(norm_sq, i * KD + k + 1)
                    mm(bank(b, T), ones, sq[:, k * T:(k + 1) * T], start=k == 0, stop=k == KD - 1,
                       signal=norm_sum if k == KD - 1 else None)

            ada_rows(weights(ada_slab(0)), 0)
            pe.wait_ge(inputs_loaded, 16 * 5)
            norm(0)
            norm(1)
            for n in range(ADA_FIRST):
                if n:
                    ada_rows(weights(ada_slab(n)), 0)
                ada_turn(n, big[:, 0:512])
            pe.wait_ge(mod_stored, ADA_FIRST)
            unit = [0]

            def fill(parts, after=None):
                u = unit[0]
                unit[0] += 1
                if u >= 8:
                    pe.wait_ge(bank_emptied, u - 7)
                for i, (o, n, pairs) in enumerate(parts):
                    chain(bank(unit_bank(u), n, o), pairs, bank_filled if i == len(parts) - 1 else None)

            def by_token(h, t, w, n):
                return [(0, n, [(h[:, k * T + t * P:k * T + (t + 1) * P], w[:, k, 0:n]) for k in range(KD)])]

            def by_feature(h, w, j):
                return [(w[:, k, j * P:(j + 1) * P], h[:, k * T:(k + 1) * T]) for k in range(KD)]

            def k_view(n, width=512):
                return weights(n)[:, 0:KD * width].rearrange("p (k n) -> p k n", k=KD)

            tiles = ((hT, 0), (hT, 1), (hcT, 0), (hcT, 1))
            for s, width in ((S_K, 512), (S_V, 512), (S_GKV, 272)):
                w = k_view(s, width)
                for n, (h, t) in enumerate(tiles):
                    if s == S_K and n % 2 == 0:
                        pe.wait_ge(norm_done, (n // 2 + 1) * KD)
                    fill(by_token(h, t, w, width))
                slab_done()
            w = k_view(S_Q)
            for j in range(0, 4, 2):
                fill([(0, T, by_feature(hT, w, j)), (T, T, by_feature(hT, w, j + 1))])
            slab_done()
            pe.wait_ge(bank_emptied, unit[0])

            spare = []
            for s in (S_AQ, S_O):
                for t in range(NT):
                    for o in range(0, 512, T):
                        spare.append((s, o, lambda w, t=t, o=o: [(hT[:, k * T + t * P:k * T + (t + 1) * P],
                                                                  w[:, k, o:o + T]) for k in range(KD)]))
            for s in range(S_MG, S_MG + 4):
                for j in range(4):
                    spare.append((s, (j % 2) * T, lambda w, j=j: by_feature(hT, w, j)))
            spare_at = [0]

            def fill_spare(count):
                for _ in range(count):
                    s, o, pairs = spare[spare_at[0]]
                    last_of_slab = spare_at[0] % 4 == 3
                    spare_at[0] += 1
                    u = unit[0]
                    if o == 0:
                        if u < UNITS_RING + 2:
                            pe.wait_ge(kT_stored, u - UNITS_RING + 1)
                        else:
                            pe.wait_ge(bank_emptied, u - 1)
                    else:
                        unit[0] += 1
                    chain(bank(unit_bank(u), T, o), pairs(k_view(s)), bank_filled if o else None)
                    if last_of_slab:
                        slab_done()

            pe.wait_ge(lf_ready, 1)
            lf = small[:, 96:128]
            for d in range(2):
                nc.tensor.matmul(bank(0, 16, 16 * d), const(f"tri{d}"), lf[:, 16 * d:16 * d + 16],
                                 start=True, stop=True)
            nc.tensor.matmul(bank(0, 32, 32), ones, lf, start=True, stop=True).then_inc(cums_filled, 1)
            for c in range(2):
                for h in range(HEADS):
                    ins = nc.tensor.transpose(bank(6 + c, P, h * P), kN[:, (2 + c) * 512 + h * P:(2 + c) * 512 + (h + 1) * P],
                                              ident)
                ins.then_inc(kT_filled, 1)
            for n in range(8):
                pe.wait_ge(diag_ready, n + 1)
                if n >= 2:
                    pe.wait_ge(rrow_used, n - 1)
                nc.tensor.matmul(bank(1 + n % 2), ones, pair[n % 2], start=True, stop=True).then_inc(rrow_filled, 1)
                fill_spare(1)
            fill_spare(2)
            for c in range(2):
                pe.wait_ge(kT_stored, c + 1)
                for h in range(HEADS):
                    o = h * T + c * P
                    ins = nc.tensor.matmul(bank(3 * c, P, h * P), qT[:, o:o + P], kTl[:, o:o + P],
                                           start=True, stop=True)
                ins.then_inc(qk_filled, 1)
            for n in range(6):
                p, d = n // 2, n % 2
                c = (p, p ^ 1)[d]
                pe.wait_ge(kw_ready, n + 1)
                if n >= 1:
                    pe.wait_ge(cloc_used, n)
                for h in range(HEADS):
                    ins = nc.tensor.matmul(ps[:, 4 * 512 + h * 256:4 * 512 + h * 256 + 129],
                                           pair[n % 2][:, h * P:(h + 1) * P], vA[:, c, h, :], start=True, stop=True)
                ins.then_inc(cloc_filled, 1)
                fill_spare(1)
            pe.wait_ge(bank_emptied, unit[0])
            for n in range(4):
                p, d = n // 2, n % 2
                lc = (p, p ^ 1)[d]
                pe.wait_ge(smat_ready, n + 1)
                for h in range(HEADS):
                    o = (2 * d + p) * 512 + h * P
                    ins = nc.tensor.transpose(bank(1 + n % 2, P, h * P), decay[:, o:o + P], ident)
                ins.then_inc(smatT_filled, 1)
                if n == 0:
                    pe.wait_ge(cloc_used, 6)
                else:
                    pe.wait_ge(num_used, n)
                for h in range(HEADS):
                    nc.tensor.matmul(ps[:, 4 * 512 + h * 256:4 * 512 + h * 256 + 129],
                                     qT[:, h * T + lc * P:h * T + (lc + 1) * P], state[p][d][:, h, :],
                                     start=True, stop=True)
                pe.wait_ge(smatT_stored, n + 1)
                for h in range(HEADS):
                    ins = nc.tensor.matmul(ps[:, 6 * 512 + h * 256:6 * 512 + h * 256 + 129],
                                           pair[n % 2][:, h * P:(h + 1) * P], vA[:, 2 + lc, h, :],
                                           start=True, stop=True)
                ins.then_inc(num_filled, 1)

            pe.wait_ge(num_used, 4)
            fill_spare(8)

            def turn(n, srcs):
                for j, s in enumerate(srcs):
                    ins = nc.tensor.transpose(bank(n % 8, P, j * P), s, ident)
                ins.then_inc(turn_filled, 1)

            pe.wait_ge(roped, 1)
            for n in range(2):
                turn(n, [qR[:, t * 512 + pr * P:t * 512 + (pr + 1) * P]
                         for pr in (2 * n, 2 * n + 1) for t in range(NT)])
            for n, k in enumerate((kR, kSw)):
                turn(2 + n, [k[:, c * P:(c + 1) * P] for c in (2, 3, 0, 1)])

            def attention(blk):
                first = blk * UNITS

                def keys(h):
                    if blk == 0:
                        kv, base = h // 4, h % 2
                        return kTa[DH * base:DH * base + DH, (0 if kv == base else 512):(512 if kv == base else 1024)]
                    return kT2[DH * (h % 2):DH * (h % 2) + DH, (h // 2) * 512:(h // 2 + 1) * 512]

                def queries(b, h):
                    q = qTa if blk == 0 else qT2
                    o = (h // 2) * T + b * P
                    return q[DH * (h % 2):DH * (h % 2) + DH, o:o + P]

                def values(c, h):
                    if blk == 0:
                        o = (2, 3, 0, 1)[c] * P
                        return avN[:, o:o + P]
                    return vN2[:, c * 512 + (h // 2) * P:c * 512 + (h // 2 + 1) * P]

                def scores(u):
                    b, h = (u - first) // AH, u % AH
                    if u >= 2:
                        pe.wait_ge(scaled, u - 1)
                    nc.tensor.matmul(bank(u % 2), queries(b, h), keys(h), start=True,
                                     stop=True).then_inc(scores_filled, 1)

                def turn_probs(u):
                    pe.wait_ge(probs_ready, u + 1)
                    if u >= 2:
                        pe.wait_ge(probsT_stored, u - 1)
                    for c in range(4):
                        ins = nc.tensor.transpose(bank(2 + u % 2, P, c * P), probs[u % 3][:, c * P:(c + 1) * P], ident)
                    ins.then_inc(probsT_filled, 1)

                def apply(u):
                    h = u % AH
                    pe.wait_ge(probsT_stored, u + 1)
                    if u >= 2:
                        pe.wait_ge(head_stored, u - 1)
                    chain(bank(4 + u % 2, P), [(probsT[u % 3][:, c * P:(c + 1) * P], values(c, h))
                                               for c in range(4)], head_filled)

                scores(first)
                scores(first + 1)
                for u in range(first, first + UNITS):
                    if blk == 0 and u % 2 == 0:
                        ada_rows(weights(ada_slab(ADA_FIRST + u // 2)), 0)
                    turn_probs(u)
                    if u + 2 < first + UNITS:
                        scores(u + 2)
                    if u > first:
                        apply(u - 1)
                    if blk == 0 and u % 2:
                        ada_turn(ADA_FIRST + u // 2, hcT[:, 0:512])
                apply(first + UNITS - 1)

            pe.wait_ge(turn_stored, 4)
            attention(0)
            pe.wait_ge(mod_stored, ADA_SLABS)
            pe.wait_ge(m_ready, 1)
            pe.wait_ge(head_stored, UNITS)
            for i, src in enumerate((hN, aN)):
                for n in range(2):
                    turn(4 + 2 * i + n, [src[:, t * 512 + j * P:t * 512 + (j + 1) * P]
                                         for j in (2 * n, 2 * n + 1) for t in range(NT)])
            pe.wait_ge(turn_stored, 8)
            for i, src in enumerate((mT, aT)):
                w = weights(S_BM + i).rearrange("p (k n) -> p k n", k=4)
                for b in range(4):
                    for j in range(2):
                        o = (2 * b + j) * P
                        chain(bank(4 * i + b, T, j * T), [(w[:, k, o:o + P], src[:, k * T:(k + 1) * T]) for k in range(4)],
                              branch_filled if (b, j) == (3, 1) else None)
                slab_done()

            def project_out(s0, src):
                for half in range(2):
                    w = weights(s0 + half).rearrange("p (k n) -> p k n", k=KD)
                    for b in range(2):
                        for j in range(2):
                            chain(bank(2 * half + b, T, j * T), by_feature(src, w, 2 * b + j),
                                  y_filled if b and j else None)
                    slab_done()

            pe.wait_ge(merged_ready, 4)
            project_out(S_OUT, merged)

            norm(2)
            pe.wait_ge(norm_done, 3 * KD)
            for s in range(4):
                w = k_view(S_QUERY + s)
                for j in range(0, 4, 2):
                    fill([(0, T, by_feature(hT, w, j)), (T, T, by_feature(hT, w, j + 1))])
                slab_done()
            pe.wait_ge(bank_emptied, unit[0])
            pe.wait_ge(subk_loaded, 16)
            for t in range(NT):
                for b in range(4):
                    for j in range(4):
                        hp = 4 * b + j
                        ins = nc.tensor.matmul(bank(4 * t + b, P, j * P), qTr[:, hp * T + t * P:hp * T + (t + 1) * P],
                                               subk[:, hp * P:(hp + 1) * P], start=True, stop=True)
                    ins.then_inc(rscores_filled, 1)
            pe.wait_ge(rscores_stored, 8)
            zeros512 = cst[:, CONSTS["window"][0]:CONSTS["window"][0] + 512]
            pe.wait_ge(zeros_ready, 1)

            def open_sums():
                for b in range(4):
                    mm(bank(4 + b), ones, zeros512, start=True, stop=True)

            open_sums()
            groups = T // GROUP
            for half in range(2):
                def piece_split(q, h, i, by_gpsimd=False):
                    if by_gpsimd:
                        pe.wait_ge(lo_ready_gp, i * 32 + (2 * q + h + 1))
                    else:
                        pe.wait_ge(lo_ready, i * 32 + (2 * (q - GP_CHUNKS) + h + 1))

                def split_product(dst, q, o, high, low, start, i=None, **kw):
                    n = chunk_slab(q)
                    wl = slab_lo[n % SLOTS][:, (q % 4) * CHUNK + o:(q % 4) * CHUNK + o + P]
                    wh = w_hi[(2 * q + o // PIECE) % 4][:, o % PIECE:o % PIECE + P]
                    mm(dst, wh, high, start=start, stop=False, **kw)
                    mm(dst, wh, low, start=False, stop=False, **kw)
                    return wl, high

                def activations(i, by_gpsimd=False, q0=2 * half * CHUNKS, half=half):
                    for j in range(16):
                        q = q0 + j
                        if j % 2 == 0 and not (isinstance(i, int) and half == 0 and j < 8):
                            pe.wait_ge(gelu_ready, i * 8 + (half * CHUNKS // 2 + j // 2 - 3))
                        dst = bank((j // 2) % 4, T, (j % 2) * T)
                        for k in range(KD):
                            if k % 4 == 0:
                                piece_split(q, k // 4, i, by_gpsimd)
                            hk = slice(k * T, (k + 1) * T)
                            wl, hh = split_product(dst, q, k * P, h_hi[:, hk], h_lo[:, hk], k == 0)
                            mm(dst, wl, hh, start=False, stop=k == KD - 1, signal=piece_used if k % 4 == 3 else None)
                        if j % 4 == 3:
                            slab_done()

                pe.wait_ge(h_lo_ready, 1)
                activations(0, half == 0)
                with pe.Fori(1, HALF_SLABS // 4 - (half == 0)) as i:
                    activations(i, half == 0)
                if half == 0:
                    activations(HALF_SLABS // 4 - 1)
                pe.wait_ge(gelu_ready, (half + 1) * 2 * HALF_SLABS)
                if half == 0:
                    for t in range(NT):
                        pe.wait_ge(choice_ready, t + 1)
                        for i in range(3):
                            ins = nc.tensor.transpose(bank(t, P, i * P), choice[t][:, i * P:(i + 1) * P], ident)
                        ins.then_inc(choiceT_filled, 1)
                    pe.wait_ge(pick_ready, NT)

                def gates(g, s, half=half):
                    n = g * 2 + (half * groups + s)
                    pe.wait_ge(ohw_ready, n + 1)
                    pe.wait_ge(oh2_ready, n + 1)
                    if not (isinstance(g, int) and half == 0):
                        pe.wait_ge(weight_ready, n - 1)
                    for m in range(GROUP):
                        n2 = min(2, GROUP - m) * HALF_E1
                        mm(bank(s, n2, m * HALF_E1), oh2[s][:, m * P:(m + 1) * P],
                           oh1[s][:, m * HALF_E1:m * HALF_E1 + n2], start=True, stop=True,
                           signal=gate_filled if m == GROUP - 1 else None)

                for s in range(2):
                    gates(0, s)
                if half:
                    with pe.Fori(1, groups // 2) as g:
                        for s in range(2):
                            gates(g, s)
                else:
                    with pe.Fori(0, ADA_SLABS // SLOTS) as i:
                        for j in range(SLOTS + 1):
                            for s in range(2):
                                gates(i * (SLOTS + 1) + (j + 1), s)
                            if j:
                                ada_turn(i * SLOTS + (ADA_SLABS + j - 1), ada_rows2, i * (8 * SLOTS) + (3 * 512 + 8 * (j - 1)))
                            if j < SLOTS:
                                ada_rows(weights(S_ADA3 + j, i), 1, 2)
                    pe.wait_ge(mod_stored, ADA_SLABS + 1)
                pe.wait_ge(weight_ready, (half + 1) * groups)

                def combine(i, q0=(2 * half + 1) * CHUNKS):
                    for j in range(16):
                        q = q0 + j
                        pe.wait_ge(glo_ready, i * 16 + (half * CHUNKS + j + 1))
                        for c in range(KD):
                            if c % 4 == 0:
                                piece_split(q, c // 4, i)
                            dst = bank(4 + c // 2, T, (c % 2) * T)
                            wl, gh = split_product(dst, q, c * P, g_hi[q % 2][:, :], g_lo[q % 2][:, :], False,
                                                   skip_group_check=True)
                            mm(dst, wl, gh, start=False, stop=True, skip_group_check=True,
                               signal=piece_used if c % 4 == 3 else None)
                        if j % 4 == 3:
                            slab_done()

                combine(0)
                with pe.Fori(1, HALF_SLABS // 4) as i:
                    combine(i)
                mm(bank(0, P), ones, ident, start=True, stop=True, signal=peer_half)

            norm(3)
            norm(4)
            pe.wait_ge(norm_done, 5 * KD)
            w = k_view(S_K2)
            for j in range(4):
                fill([(0, T, by_feature(hT, w, j)), (T, T, by_feature(hcT, w, j))])
            slab_done()
            w = k_view(S_V2)
            for h, t in ((hT, 0), (hT, 1), (hcT, 0), (hcT, 1)):
                fill(by_token(h, t, w, 512))
            slab_done()
            w = k_view(S_Q2)
            for j in range(0, 4, 2):
                fill([(0, T, by_feature(hT, w, j)), (T, T, by_feature(hT, w, j + 1))])
            slab_done()
            w = k_view(S_FH2)
            fill([(t * T, T, [(hT[:, k * T + t * P:k * T + (t + 1) * P], w[:, k, 0:T]) for k in range(KD)])
                  for t in range(NT)])
            fill([(0, T, by_feature(hT, w, 2)), (T, T, by_feature(hT, w, 3))])
            slab_done()
            w = k_view(S_G2)
            for j in range(0, 4, 2):
                fill([(0, T, by_feature(hT, w, j)), (T, T, by_feature(hT, w, j + 1))])
            slab_done()
            pe.wait_ge(bank_emptied, unit[0])
            pe.wait_ge(small2_loaded, 48)
            for n, name in enumerate(("dft_c", "dft_s")):
                tab = const(name)
                for j in range(2):
                    chain(bank(n, T, j * T), [(fN[:, t * T + j * P:t * T + (j + 1) * P], tab[:, t * T:(t + 1) * T])
                                              for t in range(NT)], four_filled if j else None)
            pe.wait_ge(four_stored, 2)
            for j in range(2):
                chain(bank(0, T, j * T), [(const("dch_c"), tCS[:, j * T:(j + 1) * T]),
                                          (const("dch_s"), tCS[:, 512 + j * T:512 + (j + 1) * T])],
                      four_filled if j else None)
            pe.wait_ge(four_stored, 3)
            for j in range(2):
                chain(bank(1, T, j * T), [(wf[:, k * T + j * P:k * T + (j + 1) * P], foT[:, k * T:(k + 1) * T])
                                          for k in range(2)], four_filled if j else None)
            pe.wait_ge(four_stored, 4)
            attention(1)
            pe.wait_ge(head_stored, 2 * UNITS)
            for n in range(2):
                turn(8 + n, [aN2[:, t * 512 + j * P:t * 512 + (j + 1) * P] for j in (2 * n, 2 * n + 1) for t in range(NT)])
            pe.wait_ge(turn_stored, 10)
            pe.wait_ge(conv_ready, 1)
            project_out(S_OUT2, catT)
            norm(5)
            pe.wait_ge(norm_done, 6 * KD)
            nr = NG + NE
            for t in range(NT):
                chain(bank(t, nr), [(hT[:, k * T + t * P:k * T + (t + 1) * P], wr[:, k * nr:(k + 1) * nr])
                                    for k in range(KD)], router_filled)
            for n in range(4):
                turn(10 + n, [hT[:, (4 * (n % 2) + k) * T + (n // 2) * P:(4 * (n % 2) + k) * T + (n // 2 + 1) * P]
                              for k in range(4)])
            pe.wait_ge(sel32_ready, 1)
            mm(bank(6, NE), const("tri0"), sel32[:, 0:NE], start=True, stop=True)
            chain(bank(6, NE, NE), [(ones, sel32[:, 0:NE]), (const("tri0"), sel32[:, NE:2 * NE])])
            chain(bank(6, NE, 2 * NE), [(ones, sel32[:, 0:NE]), (ones, sel32[:, NE:2 * NE])], counts_filled)
            pe.wait_ge(rounds_ready, 1)
            pe.wait_ge(turn_stored, 14)
            open_sums()
            mm(bank(0, P), ones, ident, start=True, stop=True, signal=gathered)
            mm(bank(0, P), ones, ident, start=True, stop=True, signal=scattered)
            n_rounds = pe.value_load(rounds[0:1, 0:1], min_val=1, max_val=MAX_ROUNDS)
            with pe.Fori(0, n_rounds) as r:
                with pe.Fori(0, QUADS) as q:
                    t = r * QUADS + q
                    ring = r * (QUADS * Q_SLABS // SLOTS) + q * (Q_SLABS // SLOTS)
                    pe.wait_ge(sel_ready, t + 1)
                    for b in range(NT):
                        nc.tensor.transpose(bank(2, P, b * P), selw[:, b * P:(b + 1) * P], ident)
                    for k in range(KD):
                        chain(bank((3, 0)[k // 4], P, (k % 4) * P),
                              [(xN[:, b * D + k * P:b * D + (k + 1) * P], sel[:, b * P:(b + 1) * P]) for b in range(NT)],
                              gathered if k == KD - 1 else None)
                    pe.wait_ge(xg_low, t + 1)
                    pe.wait_ge(xg_high, t + 1)
                    for b in range(2):
                        for s in range(4):
                            w = weights(S_MOE + 4 * b + s, ring).rearrange("p (e k n) -> p e k n", e=QUAD, k=2)
                            for k2 in range(2):
                                for e in range(QUAD):
                                    k = 2 * s + k2
                                    mm(ps[32 * e:32 * e + 32, b * 512:(b + 1) * 512],
                                       xg[:, k * P + e * ROOM:k * P + (e + 1) * ROOM], w[:, e, k2, :],
                                       start=k == 0, stop=k == KD - 1,
                                       signal=hidden_filled if (k, e) == (KD - 1, QUAD - 1) else None)
                            slab_done()
                    pe.wait_ge(he_ready, t + 1)
                    for f in range(4):
                        ins = nc.tensor.transpose(bank(2, P, f * P), he[:, f * P:(f + 1) * P], ident)
                    ins.then_inc(heT_filled, 1)
                    pe.wait_ge(heT_ready, t + 1)
                    for f in range(4):
                        w = weights(S_MOE + 8 + f, ring).rearrange("p (e n) -> p e n", e=QUAD)
                        for b in range(2):
                            for e in range(QUAD):
                                o = (3, 1)[b] * 512
                                mm(ps[32 * e:32 * e + 32, o:o + 512],
                                   heT[:, f * P + e * ROOM:f * P + (e + 1) * ROOM], w[:, e, b * 512:(b + 1) * 512],
                                   start=f == 0, stop=f == 3,
                                   signal=down_filled if (f, b, e) == (3, 1, QUAD - 1) else None)
                        if f < 3:
                            slab_done()
                    pe.wait_ge(down_filled, t + 1)
                    release()
                    pe.wait_ge(ye_low, t + 1)
                    pe.wait_ge(ye_high, t + 1)
                    for c in range(KD):
                        mm(bank(4 + c // 2, T, (c % 2) * T), ye[:, c * P:(c + 1) * P], selT, start=False, stop=True,
                           skip_group_check=True, signal=scattered if c == KD - 1 else None)
            mm(bank(0, P), ones, ident, start=True, stop=True, signal=experts_done)
            norm(6)

        @block.vector
        def _(dve):
            V = nc.vector
            steps = [0]

            def step(ins):
                steps[0] += 1
                ins.then_inc(dve_step, 1)
                dve.wait_ge(dve_step, steps[0])

            dve.wait_ge(inputs_loaded, 16 * 5)

            def square(i, src, k):
                c = slice(k * T, (k + 1) * T)
                V.tensor_tensor(scratch[:, (i % 2) * 2048 + k * T:(i % 2) * 2048 + (k + 1) * T], src[:, c], src[:, c],
                                ALU.mult).then_inc(norm_sq, 1)

            def squares(i, src):
                for k in range(KD):
                    square(i, src, k)

            def norm(i, src, dst, g, scale):
                b = norm_bank(i)
                dve.wait_ge(norm_sum, i + 1)
                step(V.tensor_scalar(rstd[:, :], bank(b, T), 1.0 / D, EPS, ALU.mult, ALU.add))
                V.reciprocal(rstd[:, :], rstd[:, :]).then_inc(norm_inv, 1)
                if scale is None:
                    step(V.tensor_copy(gain[:, :], g))
                else:
                    step(V.tensor_scalar(gain[:, :], scale, 1.0, None, ALU.add))
                    step(V.tensor_tensor(gain[:, :], gain[:, :], g, ALU.mult))
                dve.wait_ge(norm_rstd, i + 1)
                for k in range(KD):
                    V.scalar_tensor_tensor(out=dst[:, k * T:(k + 1) * T], in0=src[:, k * T:(k + 1) * T],
                                           scalar=gain[:, k:k + 1], in1=rstd[:, :], op0=ALU.mult,
                                           op1=ALU.mult).then_inc(norm_scaled if scale is not None else norm_done, 1)

            squares(0, xT)
            squares(1, hcT)
            md = mod.rearrange("p (n c) -> p n c", c=2)
            def ada(n, count=1, b=7):
                dve.wait_ge(mod_filled, n + count)
                V.tensor_tensor(md[:, 4 * n:4 * (n + count), :], bank(b, 8 * count).rearrange("p (j c) -> p j c", c=2),
                                colv("b_ada")[:, 4 * n:4 * (n + count)].unsqueeze(2).broadcast_to([P, 4 * count, 2]),
                                ALU.add).then_inc(mod_stored, 1)

            for n in range(ADA_FIRST):
                ada(n)
            dve.wait_ge(mod_stored, ADA_FIRST)
            norm(0, xT, hT, colv("g_mix"), modp(0, 1, 0))
            dve.wait_ge(norm_scaled, KD)
            norm(1, hcT, hcT, colv("g_mix"), modp(0, 1, 1))

            L2 = small
            li, fg, soft, lf = L2[:, 0:32], L2[:, 32:64], L2[:, 64:96], L2[:, 96:128]
            cum, tot, rr = L2[:, 128:160], L2[:, 160:192], L2[:, 192:224]
            rmax = L2[:, 224:256]
            lmax = L2[:, 256:272]
            mst = L2[:, 272:296]
            exin, exout = L2[:, 296:400], L2[:, 400:504]
            v3 = lambda t: t.rearrange("p (d c h) -> p d c h", d=2, c=4)
            g4 = gat.rearrange("p (c d g h) -> p c d g h", c=4, d=2, g=2)
            bg = rowv("b_gates").rearrange("p (d g h) -> p d g h", d=2, g=2)
            dve.wait_ge(bank_emptied, 12)
            dve.wait_ge(norm_done, 2 * KD)
            for gi, dst in ((0, li), (1, fg)):
                for d in range(2):
                    for p in range(4):
                        c = (p, p ^ 1)[d]
                        ins = V.tensor_tensor(v3(dst)[:, d, p, :], g4[:, c, d, gi, :], bg[:, d, gi, :], ALU.add)
            ins.then_inc(gates_biased, 1)
            dve.wait_ge(gates_biased, 1)
            V.memset(vA[:, :, :, P:P + 1], 1.0)
            step(V.tensor_scalar(lf, fg, 0.0, None, ALU.min))
            dve.wait_ge(soft_ready, 1)
            V.tensor_tensor(lf, lf, soft, ALU.subtract).then_inc(lf_ready, 1)
            dve.wait_ge(cums_filled, 1)
            V.tensor_copy(cum, bank(0, 32))
            step(V.tensor_copy(tot, bank(0, 32, 32)))
            step(V.tensor_tensor(rr, li, cum, ALU.subtract))
            idb = ident.unsqueeze(1).broadcast_to([P, HEADS, P])
            h3 = lambda t: t.rearrange("p (h s) -> p h s", h=HEADS)

            def place_diag(n):
                if n >= 2:
                    dve.wait_ge(rrow_filled, n - 1)
                V.tensor_tensor(h3(pair[n % 2]), idb, rr[:, 4 * n:4 * n + 4].unsqueeze(2).broadcast_to([P, HEADS, P]),
                                ALU.mult).then_inc(diag_ready, 1)

            place_diag(0)
            dve.wait_ge(bank_filled, 12)
            for n in range(8):
                d, p = n // 4, n % 4
                if n + 1 < 8:
                    place_diag(n + 1)
                dve.wait_ge(rrow_filled, n + 1)
                rowb = bank(1 + n % 2).rearrange("p (h s) -> p h s", h=HEADS)
                ins = V.tensor_reduce(rmax[:, 4 * n:4 * n + 4], rowb, X, ALU.max)
                if p >= 2:
                    dst = h3(decay[:, (2 * d + p - 2) * 512:(2 * d + p - 1) * 512])
                    ins = V.tensor_tensor(dst, rowb, const(f"seen{d}").unsqueeze(1).broadcast_to([P, HEADS, P]), ALU.add)
                ins.then_inc(rrow_used, 1)
            dve.wait_ge(rrow_used, 8)
            for n in range(4):
                ins = V.tensor_reduce(lmax[:, 4 * n:4 * n + 4], h3(decay[:, n * 512:(n + 1) * 512]), X, ALU.max)
            ex = lambda q: exin[:, 8 * q:8 * q + 8].rearrange("p (d h) -> p d h", d=2)
            eo = lambda q: exout[:, 8 * q:8 * q + 8].rearrange("p (d h) -> p d h", d=2)
            ms = lambda q: mst[:, 8 * q:8 * q + 8].rearrange("p (d h) -> p d h", d=2)
            lm = lmax.rearrange("p (d c h) -> p d c h", d=2, c=2)
            step(ins)
            for p in range(3):
                if p == 0:
                    step(V.tensor_copy(ex(0), v3(tot)[:, :, 0, :]))
                else:
                    step(V.tensor_tensor(ex(3 * p), v3(tot)[:, :, p, :], ms(p - 1), ALU.add))
                step(V.tensor_tensor(ex(3 * p + 1), v3(tot)[:, :, p, :], v3(rmax)[:, :, p, :], ALU.add))
                step(V.tensor_tensor(ms(p), ex(3 * p), ex(3 * p + 1), ALU.max))
                step(V.tensor_tensor(ex(3 * p), ex(3 * p), ms(p), ALU.subtract))
                step(V.tensor_tensor(ex(3 * p + 1), ex(3 * p + 1), ms(p), ALU.subtract))
                step(V.tensor_tensor(ex(3 * p + 2), v3(rr)[:, :, p, :], v3(rmax)[:, :, p, :], ALU.subtract))
            for q in range(2):
                step(V.tensor_tensor(lm[:, :, q, :], lm[:, :, q, :], ms(q + 1), ALU.max))
                step(V.tensor_tensor(ex(9 + q), ms(q + 1), lm[:, :, q, :], ALU.subtract))
                step(V.tensor_tensor(ex(11 + q), v3(cum)[:, :, 2 + q, :], lm[:, :, q, :], ALU.add))
                step(V.tensor_scalar(ex(11 + q), ex(11 + q), -1.0, None, ALU.mult))
            V.engine_nop().then_inc(exps_in, 1)
            for n in range(4):
                dd = h3(decay[:, n * 512:(n + 1) * 512])
                V.tensor_tensor(dd, dd, lmax[:, 4 * n:4 * n + 4].unsqueeze(2).broadcast_to([P, HEADS, P]),
                                ALU.subtract).then_inc(decay_in, 1)
            dve.wait_ge(exps_out, 1)
            bc = lambda a: a.unsqueeze(2).broadcast_to([P, HEADS, 129])
            ps4 = lambda b: ps[:, b * 512:(b + 2) * 512].rearrange("p (h v) -> p h v", h=HEADS)[:, :, 0:129]

            def weight_keys(n):
                p, d = n // 2, n % 2
                c = (p, p ^ 1)[d]
                if n >= 2:
                    dve.wait_ge(cloc_filled, n - 1)
                else:
                    dve.wait_ge(rrow_filled, 8)
                V.tensor_tensor(h3(pair[n % 2]), h3(kN[:, c * 512:(c + 1) * 512]),
                                eo(3 * p + 2)[:, d, :].unsqueeze(2).broadcast_to([P, HEADS, P]),
                                ALU.mult).then_inc(kw_ready, 1)

            weight_keys(0)
            for n in range(6):
                p, d = n // 2, n % 2
                if n + 1 < 6:
                    weight_keys(n + 1)
                dve.wait_ge(cloc_filled, n + 1)
                old, new = eo(3 * p)[:, d, :], eo(3 * p + 1)[:, d, :]
                src, dst = (state[0][d], state[0][d]) if p < 2 else (state[0][d], state[1][d])
                if p == 0:
                    V.tensor_tensor(dst, ps4(4), bc(new), ALU.mult).then_inc(cloc_used, 1)
                    dve.wait_ge(cloc_used, n + 1)
                else:
                    V.tensor_tensor(t1, ps4(4), bc(new), ALU.mult).then_inc(cloc_used, 1)
                    step(V.tensor_tensor(dst, src, bc(old), ALU.mult))
                    dve.wait_ge(cloc_used, n + 1)
                    step(V.tensor_tensor(dst, dst, t1, ALU.add))
            dve.wait_ge(decay_out, 1)
            dve.wait_ge(qk_filled, 2)
            for n in range(4):
                p, d = n // 2, n % 2
                lc = (p, p ^ 1)[d]
                o = (2 * d + p) * 512
                V.tensor_tensor(decay[:, o:o + 512], bank(3 * lc), decay[:, o:o + 512], ALU.mult).then_inc(smat_ready, 1)
            for n in range(4):
                p, d = n // 2, n % 2
                lc = (p, p ^ 1)[d]
                dve.wait_ge(num_filled, n + 1)
                step(V.tensor_tensor(t1, ps4(4), bc(eo(9 + p)[:, d, :]), ALU.mult))
                V.tensor_tensor(t1, t1, ps4(6), ALU.add).then_inc(num_used, 1)
                dve.wait_ge(num_used, n + 1)
                den, den2 = small[:, 608:612], small[:, 612:616]
                step(V.tensor_scalar(den2, t1[:, :, P], -1.0, None, ALU.mult))
                step(V.tensor_tensor(den, t1[:, :, P], den2, ALU.max))
                step(V.tensor_tensor(den, den, eo(11 + p)[:, d, :], ALU.max))
                step(V.reciprocal(den, den))
                hb = den.unsqueeze(2).broadcast_to([P, HEADS, P])
                dst = h3(hN[:, lc * 512:(lc + 1) * 512])
                if p == 0:
                    step(V.tensor_tensor(dst, t1[:, :, 0:P], hb, ALU.mult))
                else:
                    step(V.tensor_tensor(t1[:, :, 0:P], t1[:, :, 0:P], hb, ALU.mult))
                    step(V.tensor_tensor(dst, dst, t1[:, :, 0:P], ALU.add))
            sqh = at(big, 14416, 1024)
            h8 = lambda t: t.rearrange("p (h s) -> p h s", s=P)
            rs8 = small[:, 512:520]
            step(V.tensor_tensor(sqh, hN, hN, ALU.mult))
            step(V.tensor_reduce(rs8, h8(sqh), X, ALU.add))
            step(V.tensor_scalar(rs8, rs8, 1.0 / P, EPS, ALU.mult, ALU.add))
            V.reciprocal(rs8, rs8).then_inc(hms_ready, 1)
            sqk = at(big, 16464, 1536)
            rq = small[:, 520:544]
            dve.wait_ge(bank_emptied, 16)
            step(V.tensor_tensor(sqk[:, 0:1024], aqN, aqN, ALU.mult))
            step(V.tensor_tensor(sqk[:, 1024:1536], akN, akN, ALU.mult))
            step(V.tensor_reduce(rq, sqk.rearrange("p (h s) -> p h s", s=DH), X, ALU.add))
            step(V.tensor_scalar(rq, rq, 1.0 / DH, EPS, ALU.mult, ALU.add))
            V.reciprocal(rq, rq).then_inc(qkms_ready, 1)
            dve.wait_ge(hrstd_ready, 1)
            step(V.tensor_tensor(h8(hN), h8(hN), rs8.unsqueeze(2).broadcast_to([P, 8, P]), ALU.mult))
            h2 = lambda t: t.rearrange("p (t f) -> p t f", t=NT)
            step(V.tensor_tensor(h2(hN), h2(hN), rowv("g_mlstm").unsqueeze(1).broadcast_to([P, NT, 512]), ALU.mult))
            dve.wait_ge(bank_emptied, 18)
            V.tensor_tensor(hN, hN, sigO, ALU.mult).then_inc(m_ready, 1)
            dve.wait_ge(qkrstd_ready, 1)
            d64 = lambda t: t.rearrange("p (h s) -> p h s", s=DH)
            for t, nh, r, g in ((aqN, 16, rq[:, 0:16], "g_q"), (akN, 8, rq[:, 16:24], "g_k")):
                step(V.tensor_tensor(d64(t), d64(t), r.unsqueeze(2).broadcast_to([P, nh, DH]), ALU.mult))
                step(V.tensor_tensor(d64(t), d64(t), rowv(g).unsqueeze(1).broadcast_to([P, nh, DH]), ALU.mult))
            step(V.tensor_copy(kR[:, 0:256], akN[:, 0:256]))
            for src, dst, nh in ((aqN, qR, AH), (akN[:, 256:512], kR[:, 256:512], 2)):
                s4 = src.rearrange("p (t h s) -> p t h s", t=NT, s=DH)
                o4 = dst.rearrange("p (t h s) -> p t h s", t=NT, s=DH)
                u4 = sqk[:, 0:NT * nh * 32].rearrange("p (t h s) -> p t h s", t=NT, s=32)
                cs, sn = (const(x).rearrange("p (t s) -> p t s", t=NT).unsqueeze(2).broadcast_to([P, NT, nh, 32])
                          for x in ("cos", "sin"))
                lo, hi = slice(0, 32), slice(32, 64)
                for a, b, op in ((lo, hi, ALU.subtract), (hi, lo, ALU.add)):
                    V.tensor_tensor(o4[:, :, :, a], s4[:, :, :, a], cs, ALU.mult)
                    step(V.tensor_tensor(u4, s4[:, :, :, b], sn, ALU.mult))
                    step(V.tensor_tensor(o4[:, :, :, a], o4[:, :, :, a], u4, op))
            k4 = kR.rearrange("p (c h s) -> p c h s", c=4, h=2)
            w4 = kSw.rearrange("p (c h s) -> p c h s", c=4, h=2)
            V.tensor_copy(w4[:, :, 0, :], k4[:, :, 1, :])
            V.tensor_copy(w4[:, :, 1, :], k4[:, :, 0, :]).then_inc(roped, 1)

            def attention(blk, dst):
                first = blk * UNITS

                def logits(u):
                    b, h = (u - first) // AH, u % AH
                    st = stat[:, 4 * u:4 * u + 4]
                    if blk == 0:
                        bias = const("window")[:, b * T:(b + 1) * T]
                    else:
                        bias = bias2[:, h * 384 + (2 - 2 * b) * 64:h * 384 + (2 - 2 * b) * 64 + T]
                    dve.wait_ge(scores_filled, u + 1)
                    if u >= 3:
                        dve.wait_ge(probs_ready, u - 2)
                    l = logit[u % 3]
                    V.scalar_tensor_tensor(out=l[:, 0:T], in0=bank(u % 2, T), scalar=ATT_SCALE, in1=bias,
                                           op0=ALU.mult, op1=ALU.add)
                    V.tensor_scalar(l[:, T:2 * T], bank(u % 2, T, T), ATT_SCALE, None, ALU.mult).then_inc(scaled, 1)
                    dve.wait_ge(scaled, u + 1)
                    step(V.tensor_reduce(st[:, 3:4], l, X, ALU.max))
                    if blk == 0:
                        V.tensor_scalar(st[:, 0:1], st[:, 3:4], rowv("sink")[:, h:h + 1], -1.0, ALU.max,
                                        ALU.mult).then_inc(logits_ready, 1)
                    else:
                        V.tensor_scalar(st[:, 0:1], st[:, 3:4], -1.0, None, ALU.mult).then_inc(logits_ready, 1)

                def finish(u):
                    b, h = (u - first) // AH, u % AH
                    st = stat[:, 4 * u:4 * u + 4]
                    if blk == 0:
                        dve.wait_ge(sink_ready, u + 1)
                        step(V.tensor_tensor(st[:, 1:2], st[:, 1:2], st[:, 2:3], ALU.add))
                    step(V.reciprocal(st[:, 1:2], st[:, 1:2]))
                    dve.wait_ge(head_filled, u + 1)
                    half = (h // 4 if blk == 0 else h % 2) * DH
                    V.tensor_scalar(dst[:, b * 512 + h * DH:b * 512 + (h + 1) * DH], bank(4 + u % 2, DH, half),
                                    st[:, 1:2], None, ALU.mult).then_inc(head_stored, 1)

                logits(first)
                logits(first + 1)
                for u in range(first, first + UNITS):
                    if u >= first + 2:
                        finish(u - 2)
                    if u + 2 < first + UNITS:
                        logits(u + 2)
                    if blk == 0 and u >= 2 and u % 2 == 0:
                        ada(ADA_FIRST + u // 2 - 1)
                finish(first + UNITS - 2)
                finish(first + UNITS - 1)
                if blk == 0:
                    ada(ADA_SLABS - 1)

            attention(0, aN)
            dve.wait_ge(branch_filled, 2)
            dve.wait_ge(bank_emptied, UNITS_B1)
            for b in range(4):
                o = b * 512
                V.tensor_tensor(tmpm[0], bank(b), sigG[:, o:o + 512], ALU.mult)
                step(V.tensor_tensor(tmpm[1], bank(4 + b), sigG[:, 2048 + o:2048 + o + 512], ALU.mult))
                V.tensor_tensor(merged[:, o:o + 512], tmpm[0], tmpm[1], ALU.add).then_inc(merged_ready, 1)
                dve.wait_ge(merged_ready, b + 1)

            def residual(n, block_, part, i, src=0, ybase=0):
                for j in range(KD + 1):
                    if j < KD:
                        if src == 0:
                            dve.wait_ge(y_filled, ybase + 1 + j // 4)
                        x = xT[:, j * T:(j + 1) * T]
                        V.scalar_tensor_tensor(out=x, in0=bank(src + j // 2, T, (j % 2) * T),
                                               scalar=modc(block_, part, j), in1=x, op0=ALU.mult,
                                               op1=ALU.add).then_inc(x_updated, 1)
                    if j:
                        dve.wait_ge(x_updated, n * KD + j)
                        square(i, xT, j - 1)

            residual(0, 0, 2, 2)
            norm(2, xT, hT, colv("g_ffn"), modp(0, 4))

            V.memset(cst[:, CONSTS["window"][0]:CONSTS["window"][0] + 512], 0.0).then_inc(zeros_ready, 1)

            def top16(src, val, idx):
                step(V.max(val[:, 0:8], src))
                step(V.max_index(idx[:, 0:8], val[:, 0:8], src))
                step(V.match_replace(src, val[:, 0:8], src, BIG_NEG))
                step(V.max(val[:, 8:16], src))
                step(V.max_index(idx[:, 8:16], val[:, 8:16], src))

            s3 = top1.rearrange("p (h q a) -> p h q a", h=RH, q=2)
            i3 = idx1.rearrange("p (h q a) -> p h q a", h=RH, q=2)
            big3 = lambda t: t.rearrange("p (h a b) -> p h a b", h=RH, a=TOPK)
            shape = [P, RH, TOPK, TOPK]
            tv = top2.rearrange("p (h k) -> p h k", h=RH)
            i16 = iota[:, 0:TOPK].unsqueeze(1).broadcast_to([P, RH * TOPK, TOPK])

            def choose(t, h):
                for q in range(2):
                    hp = 2 * h + q
                    top16(sc[t][:, hp * P:(hp + 1) * P], top1[:, hp * TOPK:(hp + 1) * TOPK],
                          idx1.bitcast(U32)[:, hp * TOPK:(hp + 1) * TOPK])
                cand = sc[t][:, h * 256:(h + 1) * 256]
                step(V.tensor_tensor(cand.rearrange("p (a b) -> p a b", a=TOPK),
                                     s3[:, h, 0, :].unsqueeze(2).broadcast_to([P, TOPK, TOPK]),
                                     s3[:, h, 1, :].unsqueeze(1).broadcast_to([P, TOPK, TOPK]), ALU.add))
                top16(cand, top2[:, h * TOPK:(h + 1) * TOPK], pos.bitcast(U32)[:, h * TOPK:(h + 1) * TOPK])

            def look_up(t):
                tmpr = sc[t]
                step(V.tensor_copy(idx1, idx1.bitcast(U32)))
                cv = choice[t][:, 256:384].rearrange("p (h k) -> p h k", h=RH)
                step(V.tensor_scalar(posa.bitcast(U32), pos.bitcast(U32), 4, None, ALU.logical_shift_right))
                step(V.tensor_scalar(pos.bitcast(U32), pos.bitcast(U32), 15, None, ALU.bitwise_and))
                step(V.tensor_copy(posa, posa.bitcast(U32)))
                step(V.tensor_copy(pos, pos.bitcast(U32)))
                for q, pf in ((0, posa), (1, pos)):
                    step(V.tensor_tensor(tmpr.rearrange("p (n a) -> p n a", a=TOPK),
                                         pf.unsqueeze(2).broadcast_to([P, RH * TOPK, TOPK]), i16, ALU.is_equal))
                    step(V.tensor_tensor(big3(tmpr), big3(tmpr), i3[:, :, q, :].unsqueeze(2).broadcast_to(shape), ALU.mult))
                    step(V.tensor_reduce(choice[t][:, q * P:(q + 1) * P], tmpr.rearrange("p (n a) -> p n a", a=TOPK),
                                         X, ALU.add))
                V.tensor_tensor(cv, tv, tv[:, :, 0:1].broadcast_to([P, RH, TOPK]), ALU.subtract).then_inc(top_ready, 1)
                dve.wait_ge(top_ready, t + 1)

            dve.wait_ge(h_hi_ready, 1)
            dve.wait_ge(bank_filled, UNITS_B1 + UNITS_Q)
            V.tensor_tensor(h_lo[:, :], hT[:, :], h_hi[:, :].bitcast(F32), ALU.subtract).then_inc(h_lo_ready, 1)

            for t in range(NT):
                dve.wait_ge(rscores_stored, 4 * (t + 1))
                for h in range(RH):
                    choose(t, h)
                look_up(t)
            for j in range(CHUNKS - 16, CHUNKS):
                low_part(dve, V, j, 0, lo_ready)
            for t in range(NT):
                cv = choice[t][:, 256:384].rearrange("p (h k) -> p h k", h=RH)
                dve.wait_ge(texp_ready, t + 1)
                step(V.tensor_reduce(zsum[:, 0:RH], cv, X, ALU.add))
                step(V.reciprocal(zsum[:, 0:RH], zsum[:, 0:RH]))
                V.tensor_tensor(cv, cv, zsum[:, 0:RH].unsqueeze(2).broadcast_to([P, RH, TOPK]),
                                ALU.mult).then_inc(choice_ready, 1)
                dve.wait_ge(choice_ready, t + 1)

            dve.wait_ge(pick_ready, NT)
            groups = T // GROUP
            gview = gate.rearrange("p (e m) -> p m e", m=T)
            for half in range(2):
                if half:
                    with dve.Fori(0, CHUNKS // 16) as i:
                        for j in range(16):
                            low_part(dve, V, 2 * CHUNKS + j, i, lo_ready)

                def one_hots(g, s, half=half):
                    n = g * 2 + (half * groups + s)
                    if not (isinstance(g, int) and half == 0):
                        dve.wait_ge(gate_filled, n - 1)
                    o = g * (2 * GROUP) + s * GROUP
                    V.tensor_tensor(oh1[s].rearrange("p (m e) -> p m e", m=GROUP),
                                    iota[:, half * HALF_E1:(half + 1) * HALF_E1].unsqueeze(1)
                                    .broadcast_to([P, GROUP, HALF_E1]),
                                    pick[:, bass.ds(o, GROUP)].unsqueeze(2).broadcast_to([P, GROUP, HALF_E1]),
                                    ALU.is_equal).then_inc(oh1_ready, 1)
                    V.tensor_tensor(oh2[s].rearrange("p (m e) -> p m e", m=GROUP),
                                    iota.unsqueeze(1).broadcast_to([P, GROUP, P]),
                                    pick[:, bass.ds(o + T, GROUP)].unsqueeze(2).broadcast_to([P, GROUP, P]),
                                    ALU.is_equal).then_inc(oh2_ready, 1)

                def weigh(g, s, half=half):
                    n = g * 2 + (half * groups + s)
                    dve.wait_ge(gate_filled, n + 1)
                    w = gview[:, bass.ds(g * (2 * GROUP) + s * GROUP, GROUP), :]
                    V.tensor_tensor(w, bank(s).rearrange("p (m e) -> p m e", m=GROUP), w, ALU.mult).then_inc(weight_ready, 1)

                for s in range(2):
                    one_hots(0, s)
                dve.wait_ge(gelu_ready, (half + 1) * 2 * HALF_SLABS)
                if half:
                    with dve.Fori(1, groups // 2) as g:
                        for s in range(2):
                            weigh(g - 1, s)
                            one_hots(g, s)
                else:
                    with dve.Fori(0, ADA_SLABS // SLOTS) as i:
                        for j in range(SLOTS + 1):
                            for s in range(2):
                                weigh(i * (SLOTS + 1) + j, s)
                                one_hots(i * (SLOTS + 1) + (j + 1), s)
                    ada(ADA_SLABS, ADA_SLABS, 3)
                for s in range(2):
                    weigh(groups // 2 - 1, s)
                with dve.Fori(0, CHUNKS // 16) as i:
                    for j in range(16):
                        q = (2 * half + 1) * CHUNKS + j
                        low_part(dve, V, q, i, lo_ready)
                        dve.wait_ge(ghi_ready, i * 16 + (half * CHUNKS + j + 1))
                        V.tensor_tensor(g_lo[q % 2][:, :], gate[:, bass.ds(i * (16 * T) + j * T, T)],
                                        g_hi[q % 2][:, :].bitcast(F32), ALU.subtract).then_inc(glo_ready, 1)
            dve.wait_ge(ctx2_loaded, 16)
            squares(3, hcT)
            dve.wait_ge(peer_half, 2)
            residual(1, 0, 5, 4, src=4)

            norm(3, hcT, hcT, colv("g1"), modp(1, 1, 1))
            dve.wait_ge(norm_scaled, 4 * KD)
            norm(4, xT, hT, colv("g1"), modp(1, 1, 0))
            dve.wait_ge(small2_loaded, 48)
            b3 = bias2.rearrange("p (n k) -> p n k", k=64)
            step(V.tensor_tensor(b3, b3, const("near").unsqueeze(1).broadcast_to([P, 48, 64]), ALU.add))
            dve.wait_ge(bank_emptied, UNITS_B1 + UNITS_Q + UNITS_B2)
            cv2 = lambda t: t.rearrange("p (j t) -> p j t", j=2)
            step(V.tensor_tensor(ucv, gbc[:, 512:1024], hcv, ALU.mult))
            wc = colv("w_conv")
            for j in range(2):
                u, v = cv2(ucv)[:, j, :], cv2(vcv)[:, j, :]
                step(V.tensor_scalar(v, u, wc[:, 3 * j + 1:3 * j + 2], None, ALU.mult))
                step(V.scalar_tensor_tensor(out=v[:, 1:T], in0=u[:, 0:T - 1], scalar=wc[:, 3 * j:3 * j + 1],
                                            in1=v[:, 1:T], op0=ALU.mult, op1=ALU.add))
                step(V.scalar_tensor_tensor(out=v[:, 0:T - 1], in0=u[:, 1:T], scalar=wc[:, 3 * j + 2:3 * j + 3],
                                            in1=v[:, 0:T - 1], op0=ALU.mult, op1=ALU.add))
            V.tensor_tensor(catT[:, 1536:2048], gbc[:, 0:512], vcv, ALU.mult).then_inc(conv_ready, 1)
            attention(1, aN2)
            residual(2, 1, 2, 5, ybase=2)
            norm(5, xT, hT, colv("g2"), modp(1, 4))

            nr = NG + NE
            V.memset(lgp, BIG_NEG)
            for t in range(NT):
                dve.wait_ge(router_filled, t + 1)
                step(V.tensor_tensor(lg[:, 0:nr], bank(t, nr), rowv("b_router"), ALU.add))
                step(V.tensor_copy(lgp[:, 0:NG], lg[:, 0:NG]))
                step(V.max(m8, lgp))
                step(V.max_index(i8, m8, lgp))
                step(V.tensor_copy(gidx, i8[:, 0:1]))
                step(V.tensor_scalar(goh, iota[:, 0:NG], gidx, None, ALU.is_equal))
                V.tensor_scalar(gex, lg[:, 0:NG], m8[:, 0:1], None, ALU.subtract).then_inc(rexp_in, 1)
                el = lg[:, NG:nr].rearrange("p (g e) -> p g e", g=NG)
                es = esel4.rearrange("p (g e) -> p g e", g=NG)
                step(V.tensor_tensor(es, el, goh.unsqueeze(2).broadcast_to([P, NG, EPG]), ALU.mult))
                step(V.tensor_reduce(esel, esel4.rearrange("p (g e) -> p e g", g=NG), X, ALU.add))
                step(V.max(e8, esel))
                step(V.max_index(j8, e8, esel))
                step(V.tensor_copy(j8f, j8))
                V.tensor_scalar(pw[:, 0:2], e8[:, 0:2], e8[:, 0:1], None, ALU.subtract).then_inc(rexp_in, 1)
                dve.wait_ge(rexp_out, 2 * t + 2)
                step(V.tensor_tensor(pw[:, 2:3], pw[:, 2:3], gz, ALU.mult))
                step(V.reciprocal(pw[:, 2:3], pw[:, 2:3]))
                step(V.tensor_scalar(pw[:, 0:2], pw[:, 0:2], pw[:, 2:3], None, ALU.mult))
                for q in range(2):
                    step(V.tensor_scalar(s8[:, 8 * q:8 * q + 8], iota[:, 0:EPG], j8f[:, q:q + 1], None, ALU.is_equal))
                    step(V.tensor_scalar(c8[:, 8 * q:8 * q + 8], s8[:, 8 * q:8 * q + 8], pw[:, q:q + 1], None, ALU.mult))
                step(V.tensor_tensor(c8[:, 0:8], c8[:, 0:8], c8[:, 8:16], ALU.add))
                step(V.tensor_tensor(s8[:, 0:8], s8[:, 0:8], s8[:, 8:16], ALU.add))
                for dst, src in ((comb32, c8), (sel32, s8)):
                    step(V.tensor_tensor(dst[:, t * NE:(t + 1) * NE].rearrange("p (g e) -> p g e", g=NG),
                                         goh.unsqueeze(2).broadcast_to([P, NG, EPG]),
                                         src[:, 0:8].unsqueeze(1).broadcast_to([P, NG, EPG]), ALU.mult))
            V.engine_nop().then_inc(sel32_ready, 1)
            dve.wait_ge(counts_filled, 1)
            step(V.tensor_tensor(place, bank(6, 2 * NE), sel32, ALU.mult))
            step(V.tensor_scalar(place, place, -1.0, None, ALU.add))
            step(V.tensor_reduce(most, bank(6, NE, 2 * NE), X, ALU.max))
            step(V.tensor_scalar(roundf, iota[:, 0:MAX_ROUNDS], float(ROOM), None, ALU.mult))
            step(V.tensor_scalar(roundf, roundf, most, None, ALU.is_lt))
            step(V.tensor_reduce(most, roundf, X, ALU.add))
            V.tensor_copy(rounds[:, 0:1], most).then_inc(rounds_ready, 1)
            dve.wait_ge(rounds_ready, 1)

            n_rounds = dve.value_load(rounds[0:1, 0:1], min_val=1, max_val=MAX_ROUNDS)
            v4 = lambda a: a.rearrange("p (t e) -> p t e", t=NT)
            o4 = lambda a: a.rearrange("p (t e s) -> p t e s", t=NT, e=QUAD)
            spread = lambda a, q: v4(a)[:, :, bass.ds(q * QUAD, QUAD)].unsqueeze(3).broadcast_to([P, NT, QUAD, ROOM])
            places = iota[:, 0:ROOM].unsqueeze(1).unsqueeze(1).broadcast_to([P, NT, QUAD, ROOM])
            with dve.Fori(0, n_rounds) as r:
                with dve.Fori(0, QUADS) as q:
                    t = r * QUADS + q
                    dve.wait_ge(gathered, t + 1)
                    V.tensor_tensor(o4(sel), spread(place, q), places, ALU.is_equal).then_inc(sel_made, 1)
                    dve.wait_ge(sel_made, t + 1)
                    V.tensor_tensor(o4(selw), o4(sel), spread(comb32, q), ALU.mult).then_inc(sel_ready, 1)
                    dve.wait_ge(gathered, t + 2)
                    V.tensor_copy(xg[:, 0:512], bank(3)).then_inc(xg_low, 1)
                    dve.wait_ge(silu_ready, t + 1)
                    dve.wait_ge(hidden_filled, t * 2 + 2)
                    V.tensor_tensor(he, silg, bank(1), ALU.mult).then_inc(he_ready, 1)
                    dve.wait_ge(heT_filled, t + 1)
                    V.tensor_copy(heT, bank(2)).then_inc(heT_ready, 1)
                    dve.wait_ge(down_filled, t + 1)
                    V.tensor_copy(ye[:, 0:512], bank(3)).then_inc(ye_low, 1)
                V.tensor_scalar(place, place, -float(ROOM), None, ALU.add).then_inc(place_moved, 1)
                dve.wait_ge(place_moved, r + 1)
            dve.wait_ge(experts_done, 1)
            residual(3, 1, 5, 6, src=4)
            norm(6, xT, yfin, colv("g_final"), None)


NORM_SCALED = [KD * i for i in range(6)] + [6 * KD]
NORM_DONE = [KD * i for i in range(7)]


def constants():
    f = np.float32
    c = np.zeros((P, N_CONST), f)

    def put(name, a):
        o, w = CONSTS[name]
        c[:, o:o + w] = np.asarray(a, f).reshape(P, w)

    p = np.arange(P)
    put("ident", np.eye(P))
    put("ones", np.ones((P, P)))
    put("tri0", p[:, None] <= p[None, :])
    put("tri1", p[:, None] >= p[None, :])
    put("seen0", np.where(p[None, :] <= p[:, None], 0.0, NEG))
    put("seen1", np.where(p[None, :] >= p[:, None], 0.0, NEG))
    q = p[:, None] + P * np.arange(NT)[None, :]
    k = np.arange(T)
    put("window", np.where(np.abs(k[None, None, :] - q[:, :, None]) <= P, 0.0, NEG))
    qc, kc = p[:, None] % 64, np.arange(64)[None, :]
    first = np.clip(qc - 8, 0, 48)
    put("near", np.where((kc >= first) & (kc < first + 16), 0.0, NEG))
    tok = q
    inv = (10000.0 ** (-np.arange(16, dtype=f) / f(16))).astype(f)
    r = (tok // 64)[:, :, None].astype(f) * inv
    w = (tok % 64)[:, :, None].astype(f) * inv
    ang = np.concatenate([r, w], axis=-1)
    put("cos", np.cos(ang.astype(np.float64)))
    put("sin", np.sin(ang.astype(np.float64)))
    put("iota", np.broadcast_to(p[None, :], (P, P)))
    th = 2 * np.pi * (tok[:, :, None] * k[None, None, :] % T) / T
    put("dft_c", np.cos(th) / 16.0)
    put("dft_s", np.sin(th) / 16.0)
    j = np.arange(P)
    same = (j[:, None] // 64) == (j[None, :] // 64)
    th = 2 * np.pi * ((j[:, None] % 64) * (j[None, :] % 64) % 64) / 64
    put("dch_c", np.where(same, np.cos(th), 0) / 8.0)
    put("pairs", (p[:, None] % 32) == np.arange(2)[None, :])
    put("dch_s", np.where(same, -np.sin(th), 0) / 8.0)
    return c


def kernel(**inputs):
    import concourse.bacc as bacc
    from concourse.bass_utils import run_bass_kernel_spmd

    a = {k: np.asarray(v) for k, v in inputs.items()}

    def by_rows(w):
        return w.reshape(-1, P, w.shape[-1]).transpose(1, 0, 2)

    slabs = np.zeros((N_SLABS, P, SLAB), np.float32)

    def put(n, w):
        w = by_rows(w).reshape(P, -1)
        slabs[n, :, :w.shape[1]] = w

    for m, name in enumerate(("w_ada", "w_ada_2")):
        for s in range(ADA_SLABS):
            put(ada_slab(m * ADA_SLABS + s), a[name][0][:, s * 512:(s + 1) * 512])
    w = a["w_in"][0]
    put(S_Q, w[:, 0:512])
    put(S_K, w[:, 512:1024])
    put(S_V, w[:, 1024:1536])
    put(S_O, w[:, 1536:2048])
    put(S_GKV, np.concatenate([w[:, 2048:2064], w[:, 2576:2832]], axis=1))
    put(S_AQ, w[:, 2064:2576])
    for s in range(4):
        put(S_MG + s, w[:, 2832 + s * 512:2832 + (s + 1) * 512])
        put(S_QUERY + s, a["peer_w_query"][0][:, s * 512:(s + 1) * 512])
    put(S_BM, a["w_branch_m"][0])
    put(S_BA, a["w_branch_a"][0])
    for s in range(2):
        put(S_OUT + s, a["w_out"][0][:, s * 512:(s + 1) * 512])
        put(S_OUT2 + s, a["w_out_2"][0][:, s * 512:(s + 1) * 512])
    u = a["peer_u"][0].reshape(2 * HALF_SLABS, 512, KD, P).reshape(2 * HALF_SLABS, 4, P, KD, P).transpose(0, 4, 1, 3, 2).reshape(2 * HALF_SLABS, P, SLAB)
    v = a["peer_v"][0].reshape(2 * HALF_SLABS, 4, P, D).transpose(0, 2, 1, 3).reshape(2 * HALF_SLABS, P, SLAB)
    for half in range(2):
        for phase, w in enumerate((u, v)):
            s0 = chunk_slab((2 * half + phase) * CHUNKS)
            slabs[s0:s0 + HALF_SLABS] = w[half * HALF_SLABS:(half + 1) * HALF_SLABS]
    w = a["w_in_2"][0]
    put(S_Q2, w[:, 256:768])
    put(S_K2, w[:, 768:1280])
    put(S_V2, w[:, 1280:1792])
    put(S_FH2, np.concatenate([w[:, 0:256], w[:, 2304:2560]], axis=1))
    put(S_G2, w[:, 1792:2304])
    for q in range(QUADS):
        es = slice(q * QUAD, (q + 1) * QUAD)
        s0 = S_MOE + q * Q_SLABS
        for b, name in enumerate(("w_gate_2", "w_up_2")):
            w = a[name][0, es].reshape(QUAD, 4, 2, P, 512).transpose(1, 3, 0, 2, 4)
            slabs[s0 + 4 * b:s0 + 4 * b + 4] = w.reshape(4, P, SLAB)
        w = a["w_down_2"][0, es].reshape(QUAD, 4, P, D).transpose(1, 2, 0, 3)
        slabs[s0 + 8:s0 + 12] = w.reshape(4, P, SLAB)

    def column(v):
        return v.reshape(-1, P).T

    def tokens(x):
        return x.T.reshape(KD, P, T).transpose(1, 0, 2).reshape(P, KD * T)

    cond = np.zeros((P, KD, 2, ROOM), np.float32)
    for i, n in enumerate(("c", "c_ctx", "c_2", "c_ctx_2")):
        cond[:, :, i // 2, i % 2] = column(a[n].reshape(-1))
    cond = cond.reshape(P, -1)
    cols = np.concatenate(
        [column(a[n].reshape(-1)) for n in ("b_ada", "b_ada_2", "norm_mix_g", "norm_ffn_g", "norm1_2", "norm2_2",
                                            "norm_final_2")]
        + [a["w_conv_2"][0].reshape(3, 2, P).transpose(2, 1, 0).reshape(P, 6)], axis=1)
    rows = np.concatenate([a[n].reshape(-1) for n in ("b_mgates", "mlstm_norm_g", "attn_q_norm_g", "attn_k_norm_g",
                                                      "attn_sink", "b_rg_2", "b_re_2")])
    rows = np.broadcast_to(rows, (P, N_ROW))
    subk = a["peer_sub_keys"][0].transpose(3, 0, 1, 2).reshape(P, -1)
    r2 = a["rpb_2"][0]
    shift = np.clip(np.arange(64)[None, :] - np.arange(64)[:, None] + 15, 0, 30)
    toe = r2[:, :, shift].transpose(2, 0, 1, 3)
    rpb = np.concatenate([toe[:, :, 5:11], toe[:, :, 4:10]], axis=0).reshape(P, -1)
    wr = by_rows(np.concatenate([a["w_rg_2"][0], a["w_re_2"][0]], axis=1)).reshape(P, -1)
    arrays = {
        "w_stream": slabs, "cond": cond, "x_t": tokens(a["x"][0]), "ctx_t": tokens(a["ctx"][0]),
        "ctx2_t": tokens(a["ctx_2"][0]), "consts": constants(), "cols": cols, "rows": rows, "sub_keys": subk,
        "rpb": rpb, "w_four": by_rows(a["w_fourier_2"][0]).reshape(P, -1), "w_router": wr,
    }
    arrays = {k: np.ascontiguousarray(v) for k, v in arrays.items()}
    nc = bacc.Bacc("TRN2", target_bir_lowering=False, num_devices=1)
    args = [nc.dram_tensor(k, v.shape, mybir.dt.from_np(v.dtype), kind="ExternalInput").ap() for k, v in arrays.items()]
    args.append(nc.dram_tensor("out", (P, KD * T), F32, kind="ExternalOutput").ap())
    two_block_kernel(nc, *args)
    r = run_bass_kernel_spmd(nc, [arrays], core_ids=[0])
    y = r.results[0]["out"]
    return np.ascontiguousarray(y.reshape(P, KD, T).transpose(2, 1, 0).reshape(1, T, D))
```
